# Optimizing a Trainium2 kernel written in Bass

```python
import math
import jax
import jax.numpy as jnp
from jax import lax
import numpy as np

D_MODEL = 1024
BATCH = 1
SEQ = 1024
DEPTH = 2
DEC_BATCH = 8
DEC_SEQ = 1
PAST_LEN = 1024
PAGE_SIZE = 128

HEAD_DIM = 64
N_HEADS_EVEN = D_MODEL // HEAD_DIM
HEADS_A = N_HEADS_EVEN // 2
HEADS_B = N_HEADS_EVEN - HEADS_A
D_A = HEADS_A * HEAD_DIM
D_B = HEADS_B * HEAD_DIM
D_MIX_EVEN = D_A + D_B
P_EVEN = 3 * D_A + HEADS_A + 3 * D_B
SCALE = HEAD_DIM ** -0.5
ROPE_DIM = HEAD_DIM // 4
ROPE_THETA = 500000.0
Q_BLOCK = 128
DILATIONS = (1, 4, 16)
DIL_BAND = 128
WIN_MAX = DIL_BAND * max(DILATIONS)
CHUNK = 128
D_C = D_MODEL
C_GROUPS = 8
C_GROUP_DIM = D_C // C_GROUPS
D_FF = -(-8 * D_MODEL // (3 * 256)) * 256
N_EVEN = (DEPTH + 1) // 2
N_ODD = DEPTH // 2
NORM_EPS = 1e-6

kernel_name = 'fox_dilated_gmlp_hybrid_step'

def rms_norm(x, g):
    xf = x.astype(jnp.float32)
    y = xf * lax.rsqrt(jnp.mean(xf * xf, axis=-1, keepdims=True) + NORM_EPS)
    return (y * g.astype(jnp.float32)).astype(x.dtype)

def layer_norm(x, g, b):
    xf = x.astype(jnp.float32)
    xc = xf - jnp.mean(xf, axis=-1, keepdims=True)
    y = xc * lax.rsqrt(jnp.mean(xc * xc, axis=-1, keepdims=True) + NORM_EPS)
    return (y * g.astype(jnp.float32) + b.astype(jnp.float32)).astype(x.dtype)

def partial_rope(x, pos):
    half = ROPE_DIM // 2
    inv_freq = ROPE_THETA ** (-jnp.arange(0, ROPE_DIM, 2, dtype=jnp.float32) / ROPE_DIM)
    ang = pos.astype(jnp.float32)[:, None] * inv_freq[None, :]
    cos = jnp.cos(ang)[:, None, :]
    sin = jnp.sin(ang)[:, None, :]
    xr = x[..., :ROPE_DIM].astype(jnp.float32)
    x1, x2 = xr[..., :half], xr[..., half:]
    rot = jnp.concatenate([x1 * cos - x2 * sin, x2 * cos + x1 * sin], axis=-1).astype(x.dtype)
    return jnp.concatenate([rot, x[..., ROPE_DIM:]], axis=-1)

def even_project(h, pos, w_in, b_f, g_qa, g_ka, g_qb, g_kb):
    n, t, _ = h.shape
    z = h @ w_in
    ob = 3 * D_A + HEADS_A
    heads = lambda u, nh: u.reshape(n, t, nh, HEAD_DIM)
    qa = rms_norm(heads(z[..., 0:D_A], HEADS_A), g_qa)
    ka = rms_norm(heads(z[..., D_A:2 * D_A], HEADS_A), g_ka)
    va = heads(z[..., 2 * D_A:3 * D_A], HEADS_A)
    logf = jax.nn.log_sigmoid(z[..., 3 * D_A:ob].astype(jnp.float32) + b_f.astype(jnp.float32))
    qb = partial_rope(rms_norm(heads(z[..., ob:ob + D_B], HEADS_B), g_qb), pos)
    kb = partial_rope(rms_norm(heads(z[..., ob + D_B:ob + 2 * D_B], HEADS_B), g_kb), pos)
    vb = heads(z[..., ob + 2 * D_B:ob + 3 * D_B], HEADS_B)
    return qa, ka, va, logf, qb, kb, vb

def fox_block(q, c_q, pos_q, k, v, c_k, pos_k):
    s = jnp.einsum('nqhe,nkhe->nhqk', q, k, preferred_element_type=jnp.float32) * SCALE
    s = s + (jnp.swapaxes(c_q, 1, 2)[..., :, None] - jnp.swapaxes(c_k, 1, 2)[..., None, :])
    s = jnp.where(pos_k[None, :] <= pos_q[:, None], s, -jnp.inf)
    p = jax.nn.softmax(s, axis=-1)
    return jnp.einsum('nhqk,nkhe->nqhe', p, v.astype(jnp.float32))

def fox_attention(q, k, v, c_q, c_k, pos_q, pos_k):
    n, t, h, e = q.shape
    if t <= Q_BLOCK or t % Q_BLOCK != 0:
        return fox_block(q, c_q, pos_q, k, v, c_k, pos_k)
    nb = t // Q_BLOCK
    qb = q.reshape(n, nb, Q_BLOCK, h, e).swapaxes(0, 1)
    cb = c_q.reshape(n, nb, Q_BLOCK, h).swapaxes(0, 1)
    pb = pos_q.reshape(nb, Q_BLOCK)
    out = lax.map(lambda blk: fox_block(blk[0], blk[1], blk[2], k, v, c_k, pos_k), (qb, cb, pb))
    return out.swapaxes(0, 1).reshape(n, t, h, e)

def dilated_band_prompt(q, k, v, dil):
    n, s_len, h, e = q.shape
    band = DIL_BAND
    L = s_len // dil
    nb = -(-L // band)
    Lp = nb * band

    def sub(t):
        t = t.reshape(n, L, dil, h, e).transpose(0, 2, 1, 3, 4)
        return jnp.pad(t, ((0, 0), (0, 0), (0, Lp - L), (0, 0), (0, 0)))

    def band_keys(t):
        tp = jnp.pad(t, ((0, 0), (0, 0), (band, 0), (0, 0), (0, 0)))
        prev = tp[:, :, :Lp].reshape(n, dil, nb, band, h, e)
        cur = t.reshape(n, dil, nb, band, h, e)
        return jnp.concatenate([prev, cur], axis=3)

    qs = sub(q).reshape(n, dil, nb, band, h, e)
    kb = band_keys(sub(k))
    vb = band_keys(sub(v))
    s = jnp.einsum('ngbqhe,ngbkhe->ngbhqk', qs, kb, preferred_element_type=jnp.float32) * SCALE
    qi = jnp.arange(band)[:, None]
    ki = jnp.arange(2 * band)[None, :]
    dist = qi + band - ki
    key_ok = (jnp.arange(nb)[:, None] * band - band + jnp.arange(2 * band)[None, :]) >= 0
    valid = ((dist >= 0) & (dist <= band))[None, :, :] & key_ok[:, None, :]
    s = jnp.where(valid[:, None, :, :], s, -jnp.inf)
    m = jnp.max(s, axis=-1, keepdims=True)
    ex = jnp.exp(s - m)
    l = jnp.sum(ex, axis=-1, keepdims=True)
    out = jnp.einsum('ngbhqk,ngbkhe->ngbqhe', ex / l, vb.astype(jnp.float32))
    lse = (m + jnp.log(l))[..., 0]
    out = out.reshape(n, dil, Lp, h, e)[:, :, :L].transpose(0, 2, 1, 3, 4).reshape(n, s_len, h, e)
    lse = lse.transpose(0, 1, 2, 4, 3).reshape(n, dil, Lp, h)[:, :, :L].transpose(0, 2, 1, 3).reshape(n, s_len, h)
    return out, lse

def dilated_mixture_prompt(q, k, v):
    outs, lses = [], []
    for dil in DILATIONS:
        o, l = dilated_band_prompt(q, k, v, dil)
        outs.append(o)
        lses.append(l)
    w = jax.nn.softmax(jnp.stack(lses, axis=0), axis=0)
    return jnp.sum(w[..., None] * jnp.stack(outs, axis=0), axis=0)

def dilated_mixture_decode(q, kc, vc, pos_q, first_pos):
    j = jnp.arange(DIL_BAND + 1, dtype=jnp.int32)
    dil = jnp.array(DILATIONS, dtype=jnp.int32)
    idx = (pos_q - first_pos)[:, None, None] - dil[None, :, None] * j[None, None, :]
    valid = idx >= 0
    idxc = jnp.maximum(idx, 0)
    kg = jnp.take(kc, idxc, axis=1)
    vg = jnp.take(vc, idxc, axis=1)
    s = jnp.einsum('nthe,ntpjhe->ntphj', q, kg, preferred_element_type=jnp.float32) * SCALE
    s = jnp.where(valid[None, :, :, None, :], s, -jnp.inf)
    m = jnp.max(s, axis=-1, keepdims=True)
    ex = jnp.exp(s - m)
    l = jnp.sum(ex, axis=-1, keepdims=True)
    o = jnp.einsum('ntphj,ntpjhe->ntphe', ex / l, vg.astype(jnp.float32))
    lse = (m + jnp.log(l))[..., 0]
    w = jax.nn.softmax(lse, axis=2)
    return jnp.sum(w[..., None] * o, axis=2)

def merge_heads(oa, ob, w_out, dtype):
    n, t = oa.shape[:2]
    o = jnp.concatenate([oa.reshape(n, t, D_A), ob.reshape(n, t, D_B)], axis=-1).astype(dtype)
    return o @ w_out

def even_prompt(h, pos, proj, w_out):
    qa, ka, va, logf, qb, kb, vb = even_project(h, pos, *proj)
    c = jnp.cumsum(logf, axis=1)
    oa = fox_attention(qa, ka, va, c, c, pos, pos)
    ob = dilated_mixture_prompt(qb, kb, vb)
    return merge_heads(oa, ob, w_out, h.dtype), ka, va, logf, kb, vb

def even_sample(h, pos, proj, w_out, cache_a_k, cache_a_v, cache_a_logf, state_b_k, state_b_v, page_table, li):
    n, t, _ = h.shape
    qa, ka, va, logf, qb, kb, vb = even_project(h, pos, *proj)
    ka_past = cache_a_k[li, page_table].reshape(n, PAST_LEN, HEADS_A, HEAD_DIM)
    va_past = cache_a_v[li, page_table].reshape(n, PAST_LEN, HEADS_A, HEAD_DIM)
    lf_past = cache_a_logf[li, page_table].reshape(n, PAST_LEN, HEADS_A)
    kc = jnp.concatenate([ka_past, ka], axis=1)
    vc = jnp.concatenate([va_past, va], axis=1)
    c = jnp.cumsum(jnp.concatenate([lf_past.astype(jnp.float32), logf], axis=1), axis=1)
    pos_k = jnp.arange(PAST_LEN + t, dtype=jnp.int32)
    oa = fox_attention(qa, kc, vc, c[:, PAST_LEN:], c, pos, pos_k)
    buf_len = state_b_k.shape[2]
    kbc = jnp.concatenate([state_b_k[li], kb], axis=1)
    vbc = jnp.concatenate([state_b_v[li], vb], axis=1)
    ob = dilated_mixture_decode(qb, kbc, vbc, pos, PAST_LEN - buf_len)
    return merge_heads(oa, ob, w_out, h.dtype), ka, va, logf, kb, vb

def chunk_mix(v, w_s, b_s):
    n, t, _ = v.shape
    tp = -(-t // CHUNK) * CHUNK
    vp = jnp.pad(v, ((0, 0), (0, tp - t), (0, 0))).reshape(n, tp // CHUNK, CHUNK, C_GROUPS, C_GROUP_DIM)
    mask = jnp.tril(jnp.ones((CHUNK, CHUNK), dtype=bool))
    w = jnp.where(mask[None], w_s, 0.0)
    o = jnp.einsum('gts,ncsgd->nctgd', w, vp) + jnp.swapaxes(b_s, 0, 1)[None, None, :, :, None]
    return o.reshape(n, tp, D_C)[:, :t]

def chunk_gmlp(h, w_in, g_v, b_v, w_s, b_s, w_out):
    z = jax.nn.gelu(h @ w_in, approximate=False)
    u, v = z[..., :D_C], z[..., D_C:]
    v = layer_norm(v, g_v, b_v)
    return (u * chunk_mix(v, w_s, b_s).astype(u.dtype)) @ w_out, v

def swiglu(h, w_gate_up, w_down):
    gu = h @ w_gate_up
    return (jax.nn.silu(gu[..., :D_FF]) * gu[..., D_FF:]) @ w_down

def setup_inputs(seed: int = 0) -> dict:
    key = jax.random.key(seed)
    ks = jax.random.split(key, 32)
    n_pages = PAST_LEN // PAGE_SIZE
    n_used = DEC_BATCH * n_pages
    n_phys = (5 * n_used + 3) // 4
    buf_len = min(WIN_MAX, PAST_LEN)
    nrm = lambda k, shape, scale: jax.random.normal(k, shape, jnp.float32) * scale
    gain = lambda k, shape: 1.0 + 0.02 * jax.random.normal(k, shape, jnp.float32)
    page_table = jax.random.permutation(ks[7], n_phys)[:n_used].reshape(DEC_BATCH, n_pages).astype(jnp.int32)
    return {
        'x_prompt': nrm(ks[0], (BATCH, SEQ, D_MODEL), 1.0),
        'x_sample': nrm(ks[1], (DEC_BATCH, DEC_SEQ, D_MODEL), 1.0),
        'cache_a_k': nrm(ks[2], (N_EVEN, n_phys, PAGE_SIZE, HEADS_A, HEAD_DIM), 1.0),
        'cache_a_v': nrm(ks[3], (N_EVEN, n_phys, PAGE_SIZE, HEADS_A, HEAD_DIM), 1.0),
        'cache_a_logf': jax.nn.log_sigmoid(nrm(ks[4], (N_EVEN, n_phys, PAGE_SIZE, HEADS_A), 1.0)),
        'state_b_k': nrm(ks[5], (N_EVEN, DEC_BATCH, buf_len, HEADS_B, HEAD_DIM), 1.0),
        'state_b_v': nrm(ks[6], (N_EVEN, DEC_BATCH, buf_len, HEADS_B, HEAD_DIM), 1.0),
        'page_table': page_table,
        'norm_mix': gain(ks[8], (DEPTH, D_MODEL)),
        'norm_ffn': gain(ks[9], (DEPTH, D_MODEL)),
        'w_in_even': nrm(ks[10], (N_EVEN, D_MODEL, P_EVEN), D_MODEL ** -0.5),
        'b_forget': nrm(ks[11], (N_EVEN, HEADS_A), 0.1),
        'g_q_a': gain(ks[12], (N_EVEN, HEAD_DIM)),
        'g_k_a': gain(ks[13], (N_EVEN, HEAD_DIM)),
        'g_q_b': gain(ks[14], (N_EVEN, HEAD_DIM)),
        'g_k_b': gain(ks[15], (N_EVEN, HEAD_DIM)),
        'w_out_even': nrm(ks[16], (N_EVEN, D_MIX_EVEN, D_MODEL), D_MIX_EVEN ** -0.5),
        'w_in_c': nrm(ks[17], (N_ODD, D_MODEL, 2 * D_C), D_MODEL ** -0.5),
        'g_v_c': gain(ks[18], (N_ODD, D_C)),
        'b_v_c': nrm(ks[19], (N_ODD, D_C), 0.02),
        'w_spatial': nrm(ks[20], (N_ODD, C_GROUPS, CHUNK, CHUNK), CHUNK ** -0.5),
        'b_spatial': nrm(ks[21], (N_ODD, C_GROUPS, CHUNK), 0.02),
        'w_out_c': nrm(ks[22], (N_ODD, D_C, D_MODEL), D_C ** -0.5),
        'w_gate_up': nrm(ks[23], (DEPTH, D_MODEL, 2 * D_FF), D_MODEL ** -0.5),
        'w_down': nrm(ks[24], (DEPTH, D_FF, D_MODEL), D_FF ** -0.5),
    }

def reference(x_prompt, x_sample, cache_a_k, cache_a_v, cache_a_logf, state_b_k, state_b_v, page_table,
              norm_mix, norm_ffn, w_in_even, b_forget, g_q_a, g_k_a, g_q_b, g_k_b, w_out_even,
              w_in_c, g_v_c, b_v_c, w_spatial, b_spatial, w_out_c, w_gate_up, w_down):
    pos_p = jnp.arange(SEQ, dtype=jnp.int32)
    pos_s = PAST_LEN + jnp.arange(DEC_SEQ, dtype=jnp.int32)
    keep = min(WIN_MAX, SEQ)
    ak_p, av_p, alf_p, bk_p, bv_p = [], [], [], [], []
    ak_s, av_s, alf_s, bk_s, bv_s = [], [], [], [], []
    cv_s = []
    xp, xs = x_prompt, x_sample
    for layer in range(DEPTH):
        hp = rms_norm(xp, norm_mix[layer])
        hs = rms_norm(xs, norm_mix[layer])
        li = layer // 2
        if layer % 2 == 0:
            proj = (w_in_even[li], b_forget[li], g_q_a[li], g_k_a[li], g_q_b[li], g_k_b[li])
            yp, ka, va, lf, kb, vb = even_prompt(hp, pos_p, proj, w_out_even[li])
            ak_p.append(ka)
            av_p.append(va)
            alf_p.append(lf)
            bk_p.append(kb[:, SEQ - keep:])
            bv_p.append(vb[:, SEQ - keep:])
            ys, ka, va, lf, kb, vb = even_sample(hs, pos_s, proj, w_out_even[li], cache_a_k, cache_a_v,
                                                 cache_a_logf, state_b_k, state_b_v, page_table, li)
            ak_s.append(ka)
            av_s.append(va)
            alf_s.append(lf)
            bk_s.append(kb)
            bv_s.append(vb)
        else:
            cpar = (w_in_c[li], g_v_c[li], b_v_c[li], w_spatial[li], b_spatial[li], w_out_c[li])
            yp, _ = chunk_gmlp(hp, *cpar)
            ys, v_rows = chunk_gmlp(hs, *cpar)
            cv_s.append(v_rows)
        xp = xp + yp
        xs = xs + ys
        xp = xp + swiglu(rms_norm(xp, norm_ffn[layer]), w_gate_up[layer], w_down[layer])
        xs = xs + swiglu(rms_norm(xs, norm_ffn[layer]), w_gate_up[layer], w_down[layer])
    return (xp, xs, jnp.stack(ak_p), jnp.stack(av_p), jnp.stack(alf_p), jnp.stack(bk_p), jnp.stack(bv_p),
            jnp.stack(ak_s), jnp.stack(av_s), jnp.stack(alf_s), jnp.stack(bk_s), jnp.stack(bv_s), jnp.stack(cv_s))


_drawn_inputs = setup_inputs


def setup_inputs(seed=0):
    import zlib

    import numpy as np

    out = dict(_drawn_inputs(seed))
    spreads = {}
    factors = {'norm_ffn': 2.827,
     'g_q_a': 8.0,
     'g_k_a': 2.805,
     'g_q_b': 8.0,
     'g_k_b': 2.977,
     'g_v_c': 8.677,
     'b_v_c': 8.387,
     'b_spatial': 19.863}
    for name, (base, spread) in spreads.items():
        noise = np.random.default_rng([zlib.crc32(name.encode()), seed]).standard_normal(out[name].shape)
        drawn = base * np.exp(spread * noise) if base else spread * noise
        out[name] = jnp.asarray(drawn.astype(out[name].dtype))
    for name, factor in factors.items():
        out[name] = (out[name] * factor).astype(out[name].dtype)
    return out
```

```python
from contextlib import ExitStack

import concourse.bass as bass
from concourse import mybir

ALU = mybir.AluOpType
ACT = mybir.ActivationFunctionType
AX = mybir.AxisListType.X
F32 = mybir.dt.float32
F32R = mybir.dt.float32r
I32 = mybir.dt.int32
RMAX = bass.bass_isa.ReduceOp.max

P = 128
D = 1024
KT = D // P
SEQ = 1024
NS = 8
T = NS + SEQ
TT = 1 + SEQ // P
HEADS = 8
HD = 64
DH = HEADS * HD
FF = 2816
FT = FF // P
GF = 2
STEPS = FT // GF
PAGES = 8
N_PHYS = 80
EPS = 1e-6
SCALE = HD ** -0.5
NEG = -1e30
BLOCKS = [(0, NS + 3 * P), (NS + 3 * P, 3 * P), (NS + 6 * P, 2 * P)]
NB = len(BLOCKS)
RAW = 2
SPL = 6
IN_UNITS = 4
SLOTS = PAGES + 3
LOG = SLOTS + 2


def token_columns(tt):
    return 0 if tt == 0 else NS + (tt - 1) * P


def token_rows(tt):
    return NS if tt == 0 else P


def positive_wait(eng, sem, value):
    if not isinstance(value, int) or value > 0:
        eng.wait_ge(sem, value)


class Counted:

    def __init__(self, sem, start):
        self.sem, self.start = sem, start

    def wait(self, eng, value):
        if not isinstance(value, int) or value > 0:
            eng.wait_ge(self.sem, value + self.start)


def peeled_loop(eng, count, body):
    body(0)
    with eng.Fori(1, count) as i:
        body(i)


def build(nc, a):
    with ExitStack() as ctx:
        used = [nc.sbuf_base]
        ctx.enter_context(nc.sbuf_tensor("arena", [P, (nc.sbuf_usable_end - nc.sbuf_base) // 4 - 16], F32))

        def place(name, shape, dt=F32):
            n = 1
            for s in shape[1:]:
                n *= s
            off = (used[0] + 31) // 32 * 32
            used[0] = off + 4 * n
            assert used[0] <= nc.sbuf_usable_end, (name, used[0], nc.sbuf_usable_end)
            return nc.alloc_sbuf_tensor_at(name, shape, dt, offset=off)

        def sem(name):
            return ctx.enter_context(nc.semaphore(name))

        def sems(name, n):
            return [sem(f"{name}{j}") for j in range(n)]

        ident = place("ident", [P, P])
        ones = place("ones", [P, P])
        tri = place("tri", [P, P])
        gains = place("gains", [P, 4, KT])
        gv = place("gv", [P, KT])
        bv = place("bv", [P, KT])
        eps = place("eps", [P, 1])
        zeros = place("zeros", [P, 1])
        xT = place("xT", [P, KT, T])
        Xh = place("Xh", [P, KT, T], F32R)
        Xl = place("Xl", [P, KT, T], F32R)
        overlay = used[0]
        raw = [place(f"raw{j}", [P, 1024]) for j in range(RAW)]
        Wh = [place(f"Wh{j}", [P, 1024], F32R) for j in range(SPL)]
        Wl = [place(f"Wl{j}", [P, 1024], F32R) for j in range(SPL)]
        stage_memory = used[0]

        sq = place("sq", [P, KT, BLOCKS[0][1]])
        sq_sum = place("sq_sum", [P, BLOCKS[0][1]])
        rstd = place("rstd", [P, BLOCKS[0][1]])
        norm_end = used[0]

        NX = 4
        xs = [place(f"xs{j}", [P, D]) for j in range(NX)]
        NZ = 3
        zt = [place(f"zt{j}", [P, DH]) for j in range(NZ)]
        zsq = [place(f"zsq{j}", [P, DH]) for j in range(2)]
        ss = place("ss", [P, HEADS])
        zstd = place("zstd", [P, HEADS])
        zrs = place("zrs", [P, HEADS])
        rope_u = place("rope_u", [P, HEADS, 16])
        rope_w = place("rope_w", [P, HEADS, 16])
        gqk = place("gqk", [P, 4, HD])
        cs = place("cs", [P, 2, TT, 32])
        wf = place("wf", [P, KT, HEADS])
        wfh = place("wfh", [P, KT, HEADS], F32R)
        wfl = place("wfl", [P, KT, HEADS], F32R)
        bf = place("bf", [P, HEADS])

        used[0] = norm_end
        Hh = place("Hh", [P, GF, T], F32R)
        Hl = place("Hl", [P, GF, T], F32R)
        sg = place("sg", [P, NB, BLOCKS[0][1]])
        hf = place("hf", [P, NB, BLOCKS[0][1]])

        used[0] = stage_memory
        VM = place("VM", [P, SEQ // P, D])
        vs = place("vs", [NS, D])
        ug = [place(f"ug{j}", [P, BLOCKS[0][1]]) for j in range(2)]
        wT = place("wT", [P, KT, P])
        RT = place("RT", [P, KT, P])
        vsum = place("vsum", [P, TT, 2])
        vst = place("vst", [P, 4, TT])
        w00 = place("w00", [P, KT])
        b00 = place("b00", [P, KT])
        vsT = place("vsT", [P, KT, NS])
        msT = place("msT", [P, KT, NS])
        vs2 = vs

        used[0] = overlay
        lft = place("lft", [P, TT, HEADS])
        qp = place("qp", [P, 8, P])
        kp = place("kp", [P, 8, P])
        vp = place("vp", [P, 8, P])
        QT = place("QT", [P, SEQ])
        KTr = place("KTr", [P, SEQ])
        bias = [place(f"bias{j}", [P, SEQ]) for j in range(2)]
        dist = place("dist", [P, SEQ])
        causal = place("causal", [P, P])
        score_memory = used[0]
        S2 = [place(f"S2{j}", [P, SEQ]) for j in range(2)]
        Pr = [place(f"Pr{j}", [P, SEQ]) for j in range(2)]
        PT = [place(f"PT{j}", [P, 8, P]) for j in range(2)]
        mx = place("mx", [P, 16])
        nm = place("nm", [P, 16])
        lsum = place("lsum", [P, 16])
        rl = place("rl", [P, 16])
        O = place("O", [P, 8, P])
        ring = place("ring", [P, SLOTS, DH])
        own = place("own", [NS, 4, DH])
        qrep = place("qrep", [P, 2, DH])
        prod = [place(f"prod{j}", [P, DH]) for j in range(2)]
        dbias = place("dbias", [P, NS, LOG, HEADS])
        L = place("L", [P, LOG, HEADS])
        Lb = place("Lb", [P, LOG, HEADS])
        Lm = place("Lm", [P, 2, HEADS])
        LM = place("LM", [P, 2, HEADS])
        Lp = place("Lp", [P, LOG, HEADS])
        dl = place("dl", [P, 2, HEADS])
        drl = place("drl", [P, 2, HEADS])
        hsel = place("hsel", [P, 4, HEADS])
        do1 = place("do1", [P, 2, 4, HEADS])
        do2 = place("do2", [P, 2, 4, HEADS])
        oS = place("oS", [P, KT, NS])
        pt = place("pt", [1, NS * PAGES], I32)
        used[0] = score_memory
        UO = place("UO", [P, SEQ])
        cneg = place("cneg", [HEADS, SEQ])
        ustr = place("ustr", [P, P])
        lf_t = [place(f"lf_t{j}", [P, TT, HEADS]) for j in range(4)]
        lfp = place("lfp", [P, NS * PAGES, HEADS])
        lnd = place("lnd", [NS, NS, HEADS])
        acc = [place(f"acc{j}", [P, NS, HEADS]) for j in range(2)]

        ps = ctx.enter_context(nc.psum_tensor("ps", [P, 8, 512], F32))

        q_prompt = nc.dram_tensor("q_prompt", (2, SEQ, DH), F32).ap()
        q_sample = nc.dram_tensor("q_sample", (2, NS, DH), F32).ap()
        c_dram = nc.dram_tensor("c_dram", (HEADS, SEQ), F32).ap()
        qkv_prompt = [q_prompt, a["k_prompt"], a["v_prompt"]]
        qkv_sample = [q_sample, a["k_sample"], a["v_sample"]]

        const_in = sem("const_in")
        eps_set = sem("eps_set")
        x_in = sems("x_in", NX)
        xt_lo, xt_hi = sem("xt_lo"), sem("xt_hi")
        xt_act, xt_dve = sem("xt_act"), sem("xt_dve")
        raw_in = sems("raw_in", RAW)
        split_high, split_done, w_used = sem("split_high"), sem("split_done"), sem("w_used")
        zero_set = sem("zero_set")

        BASE_IN, BASE_OUT = 0, 24
        BASE_F0 = BASE_OUT + 8
        BASE_V = BASE_F0 + 6 * STEPS
        BASE_U = BASE_V + 8
        BASE_OC = BASE_U + 8
        BASE_F1 = BASE_OC + 8
        UNITS = BASE_F1 + 6 * STEPS

        def load_unit(sp, n, slot, src, shape):
            positive_wait(sp, split_done, n - RAW + 1)
            dst = raw[slot % RAW][:, :]
            if shape:
                dst = dst.rearrange("p (a b) -> p a b", a=shape)
            with nc.allow_non_contiguous_dma("512-byte and longer runs"):
                return sp.dma_start(dst, src).then_inc(raw_in[slot % RAW], 16)

        def rows(w, k0, nk, c0, nc_):
            return w[k0 * P:(k0 + nk) * P, c0:c0 + nc_].rearrange("(k p) n -> p k n", p=P)

        def load_wide(sp, base, w, col):
            for j in range(IN_UNITS):
                load_unit(sp, base + j, j + (base % SPL if isinstance(base, int) else 0), rows(w, 2 * j, 2, col, DH), 2)

        def load_narrow(sp, base, w, count):
            for m in range(count):
                load_unit(sp, base + m, base + m, rows(w, 0, KT, m * P, P), KT)

        def load_ffn(sp, base, layer):
            gu, down = a["w_gate_up"][layer], a["w_down"][layer]

            def step(i):
                for t in range(GF):
                    f = i * GF + t
                    for half in range(2):
                        n = 2 * t + half
                        src = gu[:, bass.ds(f * P + half * FF, P)].rearrange("(k p) n -> p k n", p=P)
                        load_unit(sp, base + i * 6 + n, base + n, src, KT)
                for t in range(GF):
                    n = 4 + t
                    load_unit(sp, base + i * 6 + n, base + n, down[bass.ds((i * GF + t) * P, P), :], 0)
            peeled_loop(sp, STEPS, step)

        def split_unit(pool, n, slot, first_wait=None):
            h, l, r = Wh[slot % SPL], Wl[slot % SPL], raw[slot % RAW]
            positive_wait(pool, w_used, n - SPL + 1)
            pool.wait_ge(raw_in[slot % RAW], (n + (RAW - slot % RAW)) * 8 if False else raw_value(n, slot))
            pool.tensor_tensor(h[:, :], r[:, :], zeros[:, :].to_broadcast([P, 1024]), ALU.add).then_inc(split_high, 1)
            pool.wait_ge(split_high, n + 1)
            pool.tensor_tensor(l[:, :], r[:, :], h[:, :].bitcast(F32), ALU.subtract).then_inc(split_done, 1)

        def raw_value(n, slot):
            return (n - slot % RAW) * (16 // RAW) + 16

        def wh(n):
            return Wh[n % SPL]

        def wl(n):
            return Wl[n % SPL]

        norm_sem = {k: (sem(f"norm_{k}"), n) for k, n in (
            ("squared", NB), ("summed", NB), ("total", NB), ("root", NB), ("rstd", NB),
            ("scaled", NB * KT), ("high", NB * KT), ("low", NB * KT))}
        NORMS = [{k: Counted(x, n * j) for k, (x, n) in norm_sem.items()} for j in range(4)]

        def norm_act(act, s, ready):
            for b, (c0, n) in enumerate(BLOCKS):
                ready(act, b)
                s["low"].wait(act, KT * b)
                act.activation(sq[:, :, 0:n], xT[:, :, c0:c0 + n], ACT.Square).then_inc(s["squared"].sem, 1)
                s["total"].wait(act, b + 1)
                s["rstd"].wait(act, b)
                act.activation(rstd[:, 0:n], ps[:, 6 + b % 2, 0:n], ACT.Sqrt, bias=eps[:, 0:1],
                               scale=1.0 / D).then_inc(s["root"].sem, 1)
                for m in range(KT):
                    s["scaled"].wait(act, KT * b + m + 1)
                    act.activation(Xh[:, m, c0:c0 + n], sq[:, m, 0:n], ACT.Copy).then_inc(s["high"].sem, 1)

        def norm_dve(dve, s, g, ready):
            for b, (c0, n) in enumerate(BLOCKS):
                ready(dve, b)
                s["squared"].wait(dve, b + 1)
                s["total"].wait(dve, b)
                dve.tensor_reduce(sq_sum[:, 0:n], sq[:, :, 0:n].rearrange("p m t -> p t m"), AX,
                                  ALU.add).then_inc(s["summed"].sem, 1)
                s["root"].wait(dve, b + 1)
                dve.reciprocal(sq_sum[:, 0:n], rstd[:, 0:n]).then_inc(s["rstd"].sem, 1)
                s["rstd"].wait(dve, b + 1)
                for m in range(KT):
                    dve.scalar_tensor_tensor(sq[:, m, 0:n], xT[:, m, c0:c0 + n], gains[:, g, m:m + 1], sq_sum[:, 0:n],
                                             ALU.mult, ALU.mult).then_inc(s["scaled"].sem, 1)
                for m in range(KT):
                    s["high"].wait(dve, KT * b + m + 1)
                    dve.tensor_tensor(Xl[:, m, c0:c0 + n], sq[:, m, 0:n], Xh[:, m, c0:c0 + n].bitcast(F32),
                                      ALU.subtract).then_inc(s["low"].sem, 1)

        def norm_pe(pe, s):
            for b, (c0, n) in enumerate(BLOCKS):
                s["summed"].wait(pe, b + 1)
                s["root"].wait(pe, b - 1)
                nc.tensor.matmul(ps[:, 6 + b % 2, 0:n], ones[:, :], sq_sum[:, 0:n], start=True,
                                 stop=True).then_inc(s["total"].sem, 1)

        def chain(out, pairs, last=None):
            for j, (w, x) in enumerate(pairs):
                ins = nc.tensor.matmul(out, w, x, start=(j == 0), stop=(j == len(pairs) - 1))
            return ins

        def split_products(w_high, w_low, x_high, x_low):
            return [(w_high, x_high), (w_high, x_low), (w_low, x_high)]

        z_ps, z_free, z_squared, z_sum, z_root, z_rs, z_scaled, z_gain, z_rope1, z_done = (
            sem(n) for n in ("z_ps", "z_free", "z_squared", "z_sum", "z_root", "z_rs", "z_scaled", "z_gain", "z_rope1", "z_done"))
        z_out = sems("z_out", NZ)
        wf_in, wf_high, wf_low, f_ps = sem("wf_in"), sem("wf_high"), sem("wf_low"), sem("f_ps")
        ZB = 3
        NZT = 3 * TT

        def wide_products(pe, n0, s0, w_base, c, tt, q, x_ready):
            t0 = token_columns(tt)
            out = ps[:, q % ZB, :]
            for k in range(KT):
                if tt == 0 and k % 2 == 0:
                    pe.wait_ge(split_done, n0 + k // 2 + 1)
                h = Wh[(s0 + k // 2) % SPL][:, (k % 2) * DH:(k % 2 + 1) * DH]
                l = Wl[(s0 + k // 2) % SPL][:, (k % 2) * DH:(k % 2 + 1) * DH]
                xh, xl = Xh[:, k, t0:t0 + P], Xl[:, k, t0:t0 + P]
                nc.tensor.matmul(out, xh, h, start=(k == 0), stop=False)
                nc.tensor.matmul(out, xh, l, start=False, stop=False)
                last = nc.tensor.matmul(out, xl, h, start=False, stop=(k == KT - 1))
                if tt == TT - 1 and k % 2 == 1 and k < KT - 1:
                    last.then_inc(w_used, 1)
            return last

        wd_ps = {}

        def in_pe(pe):
            def step(i):
                for c in range(3):
                    for tt in range(TT):
                        q = c * TT + tt
                        if isinstance(i, int) and c == 0 and tt in (0, 4, 7):
                            NORMS[0]["low"].wait(pe, KT * (1 + (tt >= 4) + (tt >= 7)))
                        positive_wait(pe, z_free, i * NZT + q - ZB + 1)
                        last = wide_products(pe, i * 12 + 4 * c, 4 * c, None, c, tt, q, None)
                        last.then_inc(z_ps, 1)
                    pe.wait_ge(z_ps, i * NZT + (c + 1) * TT)
                    pe.sem_inc(w_used, 1)
            peeled_loop(pe, 2, step)
            pe.wait_ge(wf_low, 1)
            pe.wait_ge(wf_high, 1)
            for tt in range(TT):
                t0 = token_columns(tt)
                last = chain(ps[:, 6, tt * HEADS:(tt + 1) * HEADS],
                             [pr for k in range(KT) for pr in ((Xh[:, k, t0:t0 + P], wfh[:, k, :]),
                                                               (Xh[:, k, t0:t0 + P], wfl[:, k, :]),
                                                               (Xl[:, k, t0:t0 + P], wfh[:, k, :]))])
            last.then_inc(f_ps, 1)

        def in_store(act, i, c, tt, q):
            r = token_rows(tt)
            dst = qkv_sample[c][i] if tt == 0 else qkv_prompt[c][i, (tt - 1) * P:tt * P, :]
            act.wait_ge(z_done, i * NZT + q + 1)
            act.dma_start(dst, zt[q % NZ][0:r, :]).then_inc(z_out[q % NZ], 16)

        def in_act(act):
            def step(i):
                for c in range(3):
                    for tt in range(TT):
                        q, r = c * TT + tt, token_rows(tt)
                        if c < 2:
                            n = i * 2 * TT + q
                            act.wait_ge(z_ps, i * NZT + q + 1)
                            positive_wait(act, z_sum, n - 1)
                            act.activation(zsq[q % 2][0:r, :], ps[0:r, q % ZB, :], ACT.Square).then_inc(z_squared, 1)
                        if q > 0:
                            in_store(act, i, (q - 1) // TT, (q - 1) % TT, q - 1)
                        if c < 2:
                            act.wait_ge(z_sum, n + 1)
                            positive_wait(act, z_rs, n)
                            act.activation(zstd[0:r, :], ss[0:r, :], ACT.Sqrt, bias=eps[0:r, 0:1],
                                           scale=1.0 / HD).then_inc(z_root, 1)
                in_store(act, i, 2, TT - 1, NZT - 1)
            peeled_loop(act, 2, step)

        def in_dve(dve):
            def step(i):
                for c in range(3):
                    for tt in range(TT):
                        q, r = c * TT + tt, token_rows(tt)
                        z, n = zt[q % NZ], i * 2 * TT + q
                        z3 = z[0:r, :].rearrange("p (h e) -> p h e", h=HEADS)
                        p3 = ps[0:r, q % ZB, :].rearrange("p (h e) -> p h e", h=HEADS)
                        if c == 2:
                            positive_wait(dve, z_out[q % NZ], (i * (NZT // NZ) + q // NZ) * 16)
                            dve.wait_ge(z_ps, i * NZT + q + 1)
                            dve.tensor_scalar(z[0:r, :], ps[0:r, q % ZB, :], 1.0, None, ALU.mult).then_inc(z_free, 1)
                            dve.wait_ge(z_free, i * NZT + q + 1)
                            dve.tensor_scalar(ss[0:1, 0:1], z[0:1, 0:1], 1.0, None, ALU.mult).then_inc(z_done, 1)
                            continue
                        dve.wait_ge(z_squared, n + 1)
                        positive_wait(dve, z_root, n)
                        dve.tensor_reduce(ss[0:r, :], zsq[q % 2][0:r, :].rearrange("p (h e) -> p h e", h=HEADS), AX,
                                          ALU.add).then_inc(z_sum, 1)
                        dve.wait_ge(z_root, n + 1)
                        dve.reciprocal(zrs[0:r, :], zstd[0:r, :]).then_inc(z_rs, 1)
                        positive_wait(dve, z_out[q % NZ], (i * (NZT // NZ) + q // NZ) * 16)
                        dve.wait_ge(z_rs, n + 1)
                        dve.tensor_tensor(z3, p3, zrs[0:r, :].unsqueeze(2).to_broadcast([r, HEADS, HD]),
                                          ALU.mult).then_inc(z_free, 1)
                        dve.wait_ge(z_free, i * NZT + q + 1)
                        dve.tensor_tensor(z3, z3, gqk[0:r, bass.ds(2 * i + c, 1), :].to_broadcast([r, HEADS, HD]),
                                          ALU.mult).then_inc(z_gain, 1)
                        dve.wait_ge(z_gain, n + 1)
                        C = cs[0:r, bass.ds(i, 1), tt, 0:16].to_broadcast([r, HEADS, 16])
                        S1 = cs[0:r, bass.ds(i, 1), tt, 16:24].to_broadcast([r, HEADS, 8])
                        S2_ = cs[0:r, bass.ds(i, 1), tt, 24:32].to_broadcast([r, HEADS, 8])
                        dve.tensor_tensor(rope_u[0:r], z3[:, :, 0:16], C, ALU.mult)
                        dve.tensor_tensor(rope_w[0:r, :, 0:8], z3[:, :, 8:16], S1, ALU.mult)
                        dve.tensor_tensor(rope_w[0:r, :, 8:16], z3[:, :, 0:8], S2_, ALU.mult).then_inc(z_rope1, 1)
                        dve.wait_ge(z_rope1, n + 1)
                        dve.tensor_tensor(z3[:, :, 0:16], rope_u[0:r], rope_w[0:r], ALU.add).then_inc(z_done, 1)
            peeled_loop(dve, 2, step)

        lg, lg_a = sem("lg"), sem("lg_a")
        lf_out, c_ps, c_out, c_in = sem("lf_out"), sem("c_ps"), sem("c_out"), sem("c_in")
        att_const_in, page_in, lfp_in, db_ps, db = sem("att_const_in"), sem("page_in"), sem("lfp_in"), sem("db_ps"), sem("db")
        q_in, k_in, v_in, own_in, qrep_in = sem("q_in"), sem("k_in"), sem("v_in"), sem("own_in"), sem("qrep_in")
        bias_in = sems("bias_in", 2)
        ring_in = sems("ring_in", SLOTS)

        def forget_dve(dve):
            count = [0]

            def done(ins):
                count[0] += 1
                ins.then_inc(lg, 1)
                return count[0]
            dve.wait_ge(f_ps, 1)
            z = ps[:, 6, 0:TT * HEADS].rearrange("p (t h) -> p t h", t=TT)
            n = done(dve.tensor_tensor(lf_t[0][:, :, :], z, bf[:, :].unsqueeze(1).to_broadcast([P, TT, HEADS]), ALU.add))
            dve.wait_ge(lg, n)
            n = done(dve.scalar_tensor_tensor(lf_t[1][:, :, :], lf_t[0][:, :, :], -1.0, lf_t[0][:, :, :], ALU.mult, ALU.max))
            dve.wait_ge(lg_a, 2)
            n = done(dve.scalar_tensor_tensor(lft[:, :, :], lf_t[0][:, :, :], 0.0, lf_t[3][:, :, :], ALU.min, ALU.subtract))
            dve.wait_ge(c_ps, 1)
            n = done(dve.tensor_scalar(cneg[:, :], ps[0:HEADS, 0:2, :].rearrange("p a b -> p (a b)"), -1.0 / SCALE, None, ALU.mult))
            dve.wait_ge(att_const_in, ATT_CONSTS * 16)
            n = done(dve.tensor_tensor(lnd[:, :, :], lft[0:NS, 0, :].unsqueeze(1).to_broadcast([NS, NS, HEADS]),
                                       ident[0:NS, 0:NS].unsqueeze(2).to_broadcast([NS, NS, HEADS]), ALU.mult))
            dve.memset(L[:, :, :], 0.0)
            dve.wait_ge(db_ps, 1)
            inner = ps[:, 2, :].rearrange("p (s g h) -> p s g h", s=NS, g=PAGES)
            total = ps[:, 3, :].rearrange("p (s g h) -> p s g h", s=NS, g=PAGES)
            n = done(dve.tensor_scalar(acc[0][:, :, :], ps[:, 4, 0:NS * HEADS].rearrange("p (s h) -> p s h", s=NS),
                                       1.0, None, ALU.mult))
            for j, g in enumerate(reversed(range(PAGES))):
                dve.wait_ge(lg, n)
                dve.tensor_tensor(dbias[:, :, g, :], inner[:, :, g, :], acc[j % 2][:, :, :], ALU.add)
                n = done(dve.tensor_tensor(acc[(j + 1) % 2][:, :, :], total[:, :, g, :], acc[j % 2][:, :, :], ALU.add))
            dve.wait_ge(lg, n)

        def forget_act(act):
            act.wait_ge(lg, 2)
            act.activation(lf_t[2][:, :, :], lf_t[1][:, :, :], ACT.Exp, scale=-1.0).then_inc(lg_a, 1)
            act.wait_ge(lg_a, 1)
            act.activation(lf_t[3][:, :, :], lf_t[2][:, :, :], ACT.Ln, bias=1.0).then_inc(lg_a, 1)

        def forget_pe(pe):
            pe.wait_ge(lg, 3)
            pe.wait_ge(att_const_in, ATT_CONSTS * 16)
            for half in range(2):
                lo, hi = half * 512, (half + 1) * 512
                tiles = [t for t in range(8) if t * P < hi]
                for t in tiles:
                    c0 = max(lo, t * P)
                    last = nc.tensor.matmul(ps[0:HEADS, half, c0 - lo:512], lft[:, t + 1, :],
                                            UO[:, c0 - t * P:hi - t * P], start=(t == 0), stop=(t == tiles[-1]))
            last.then_inc(c_ps, 1)
            pe.wait_ge(lfp_in, 16 * NS * PAGES)
            flat = lfp[:, :, :].rearrange("p g h -> p (g h)")
            nc.tensor.matmul(ps[:, 2, :], ustr[:, :], flat, start=True, stop=True)
            nc.tensor.matmul(ps[:, 3, :], ones[:, :], flat, start=True, stop=True)
            pe.wait_ge(lg, 5)
            nc.tensor.matmul(ps[:, 4, 0:NS * HEADS], ones[0:NS, :], lnd[:, :, :].rearrange("p s h -> p (s h)"),
                             start=True, stop=True).then_inc(db_ps, 1)

        ATT_CONSTS = 7

        def forget_sp(sp):
            sp.wait_ge(f_ps, 1)
            for j in range(NZ):
                sp.wait_ge(z_out[j], 16 * 2 * NZT // NZ)
            for dst, src in ((UO, "c_uo"), (ustr, "c_ustrict"), (dist, "c_dist"), (causal, "c_causal"), (hsel, "c_hsel")):
                sp.dma_start(dst[...] if False else dst[:], a[src]).then_inc(att_const_in, 16)
            sp.dma_start(dbias[:, :, SLOTS - 3:LOG, :], a["c_dbias"]).then_inc(att_const_in, 16)
            sp.dma_start(pt[:, :], a["page_table"].rearrange("s g -> (s g)").rearrange("(o n) -> o n", o=1)).then_inc(att_const_in, 16)
            with nc.allow_non_contiguous_dma("rows of a head group"):
                for j, src in enumerate((a["k_sample"][0], a["v_sample"][0], a["k_sample"][1], a["v_sample"][1])):
                    sp.dma_start(own[:, j, :], src).then_inc(own_in, 16)
            sp.wait_ge(att_const_in, ATT_CONSTS * 16)
            with nc.allow_non_contiguous_dma("eight values a token"):
                with sp.Fori(0, NS * PAGES) as g:
                    page = sp.value_load(pt[0:1, bass.ds(g, 1)], min_val=0, max_val=N_PHYS - 1)
                    sp.dma_start(lfp[:, bass.ds(g, 1), :], a["cache_a_logf"][0, bass.ds(page, 1)].rearrange("o t h -> t o h")).then_inc(lfp_in, 16)
            sp.wait_ge(lg, 3)
            with nc.allow_non_contiguous_dma("eight values a token"):
                sp.dma_start(a["logf_prompt"].rearrange("(t p) h -> p t h", p=P), lft[:, 1:TT, :]).then_inc(lf_out, 16)
                sp.dma_start(a["logf_sample"], lft[0:NS, 0, :]).then_inc(lf_out, 16)
            sp.wait_ge(lg, 4)
            sp.dma_start(c_dram, cneg[:, :]).then_inc(c_out, 16)
            sp.wait_ge(c_out, 16)

        s_ps, s_biased, s_nm, p_done, pt_ps0, pt_ps1, pt_out0, pt_out1, pv_ps, o_done, rl_done = (
            sem(n) for n in ("s_ps", "s_biased", "s_nm", "p_done", "pt_ps0", "pt_ps1", "pt_out0", "pt_out1", "pv_ps", "o_done", "rl_done"))
        qk_ps, qk_act, qk_dve, masked, ot_ps, ot_high, ot_low = (
            sem(n) for n in ("qk_ps", "qk_act", "qk_dve", "masked", "ot_ps", "ot_high", "ot_low"))
        prod_done, log_done, dch, ar_done, dp_done, dsum_ps, dpv_ps, osamp = (
            sem(n) for n in ("prod_done", "log_done", "dch", "ar_done", "dp_done", "dsum_ps", "dpv_ps", "osamp"))
        PAIRS = 8
        QTILES = list(reversed(range(8)))
        STEP = [(hh, qt) for hh in range(2) for qt in QTILES]
        DCH = 10

        def att_sp(sp):
            for it in range(PAIRS):
                grp, j = it // 4, it % 4
                cols = slice(j * P, (j + 1) * P)
                with nc.allow_non_contiguous_dma("512-byte runs"):
                    positive_wait(sp, qk_ps, 4 * it)
                    sp.dma_start(qp[:, :, :], q_prompt[grp, :, cols].rearrange("(t p) e -> p t e", p=P)).then_inc(q_in, 16)
                    sp.dma_start(kp[:, :, :], a["k_prompt"][grp, :, cols].rearrange("(t p) e -> p t e", p=P)).then_inc(k_in, 16)
                    positive_wait(sp, pv_ps, 16 * it)
                    sp.dma_start(vp[:, :, :], a["v_prompt"][grp, :, cols].rearrange("(t p) e -> p t e", p=P)).then_inc(v_in, 16)
                    if grp == 0:
                        for hh in range(2):
                            positive_wait(sp, s_biased, 16 * (it - 1) + 8 * (hh + 1))
                            sp.dma_start(bias[hh][:, :], c_dram[2 * j + hh:2 * j + hh + 1, :].partition_broadcast(P)
                                         if False else c_dram[2 * j + hh, :].partition_broadcast(P)).then_inc(bias_in[hh], 16)
                    positive_wait(sp, prod_done, LOG * it)
                    for g in range(2):
                        sp.dma_start(qrep[:, g, :], q_sample[g, it, :].partition_broadcast(P)).then_inc(qrep_in, 16)
                    for kind in range(2):
                        cache = a["cache_a_k"] if kind == 0 else a["cache_a_v"]
                        state = a["state_b_k"] if kind == 0 else a["state_b_v"]
                        for slot in range(SLOTS):
                            if kind == 0:
                                positive_wait(sp, dpv_ps, it)
                            else:
                                sp.wait_ge(prod_done, LOG * it + slot + 1 + (slot >= PAGES))
                            if slot < PAGES:
                                page = sp.value_load(pt[0:1, it * PAGES + slot:it * PAGES + slot + 1], min_val=0, max_val=N_PHYS - 1)
                                src = cache[0, bass.ds(page, 1)].rearrange("o t h e -> t (o h e)")
                                sp.dma_start(ring[:, slot, :], src).then_inc(ring_in[slot], 16)
                            else:
                                dil = 4 ** (slot - PAGES)
                                r = min(P, PAGES * P // dil)
                                t0 = PAGES * P - r * dil
                                src = state[0, it, t0:PAGES * P, :, :].rearrange("(r d) h e -> r d (h e)", d=dil)[:, 0, :]
                                sp.dma_start(ring[0:r, slot, :], src).then_inc(ring_in[slot], 16)

        def log_slot(j):
            if j < PAGES:
                return P, 0, ring[:, j, :], j
            if j == PAGES:
                return NS, 0, own[0:NS, 0, :], None
            if j < LOG - 1:
                r = min(P, PAGES * P // 4 ** (j - PAGES - 1))
                return r, 1, ring[0:r, j - 1, :], j - 1
            return NS, 1, own[0:NS, 2, :], None

        def value_tile(j, c):
            r, g, _, slot = log_slot(j)
            if slot is None:
                return own[0:NS, 2 * g + 1, c * P:(c + 1) * P]
            return ring[0:r, slot, c * P:(c + 1) * P]

        def att_pool(pool):
            for it in range(PAIRS):
                pool.wait_ge(qrep_in, 32 * (it + 1))
                if it == 0:
                    pool.wait_ge(own_in, 64)
                for j in range(LOG):
                    r, g, keys, slot = log_slot(j)
                    n = LOG * it + j
                    if slot is not None:
                        pool.wait_ge(ring_in[slot], 32 * it + 16)
                    positive_wait(pool, log_done, n - 1)
                    pool.tensor_tensor(prod[n % 2][0:r, :], keys, qrep[0:r, g, :], ALU.mult).then_inc(prod_done, 1)
                pool.wait_ge(dch, DCH * it + 3)
                pool.partition_all_reduce(LM[:, :, :].rearrange("p g h -> p (g h)"), Lm[:, :, :].rearrange("p g h -> p (g h)"),
                                          P, RMAX).then_inc(ar_done, 1)

        def s_banks(s):
            return ps[:, 2 * (s % 2):2 * (s % 2) + 2, :].rearrange("p a b -> p (a b)")

        def att_pe(pe):
            def scores(it, k):
                s = 16 * it + k
                hh, qt = STEP[k]
                n = P * (qt + 1)
                positive_wait(pe, s_biased, s - 1)
                out = s_banks(s)
                hp = slice(hh * HD, (hh + 1) * HD)
                for c0 in range(0, n, 512):
                    c1 = min(n, c0 + 512)
                    last = nc.tensor.matmul(out[:, c0:c1], QT[hp, qt * P:(qt + 1) * P], KTr[hp, c0:c1], start=True, stop=True)
                last.then_inc(s_ps, 1)

            def weigh(it, k):
                s = 16 * it + k
                hh, qt = STEP[k]
                pe.wait_ge(p_done, s + 1)
                for g in range(qt // 4 + 1):
                    free, done = (pt_out0, pt_ps0) if g == 0 else (pt_out1, pt_ps1)
                    positive_wait(pe, free, upto[g][s])
                    for b in range(4 * g, min(qt + 1, 4 * g + 4)):
                        last = nc.tensor.transpose(ps[:, 4 + g, (b % 4) * P:(b % 4 + 1) * P], Pr[s % 2][:, b * P:(b + 1) * P], ident[:, :])
                    last.then_inc(done, 1)
                positive_wait(pe, o_done, s)
                for g in range(qt // 4 + 1):
                    pe.wait_ge((pt_out0, pt_out1)[g], upto[g][s] + 1)
                    for b in range(4 * g, min(qt + 1, 4 * g + 4)):
                        last = nc.tensor.matmul(ps[:, 6, 0:HD], PT[s % 2][:, b, :], vp[:, b, hh * HD:(hh + 1) * HD],
                                                start=(b == 0), stop=(b == qt))
                last.then_inc(pv_ps, 1)

            for it in range(PAIRS):
                for src, landed in ((qp, q_in), (kp, k_in)):
                    pe.wait_ge(landed, 16 * (it + 1))
                    for g in range(2):
                        bank = 2 * (src is kp) + g
                        if src is qp and g == 0:
                            positive_wait(pe, s_biased, 16 * it)
                        for b in range(4):
                            last = nc.tensor.transpose(ps[:, bank, b * P:(b + 1) * P], src[:, 4 * g + b, :], ident[:, :])
                        last.then_inc(qk_ps, 1)
                pe.wait_ge(qk_act, 2 * (it + 1))
                pe.wait_ge(qk_dve, 2 * (it + 1))
                pe.wait_ge(v_in, 16 * (it + 1))
                scores(it, 0)
                for k in range(16):
                    if k < 15:
                        scores(it, k + 1)
                    weigh(it, k)
                for g in range(2):
                    pe.wait_ge(o_done, 16 * (it + 1))
                    positive_wait(pe, ot_low, 2 * it + g)
                    positive_wait(pe, dch, DCH * it)
                    for b in range(4):
                        last = nc.tensor.transpose(ps[:, 7, b * P:(b + 1) * P], O[:, 4 * g + b, :], ident[:, :])
                    last.then_inc(ot_ps, 1)
                pe.wait_ge(dp_done, it + 1)
                pe.wait_ge(ot_low, 2 * (it + 1))
                flat = Lp[:, :, :].rearrange("p j h -> p (j h)")
                nc.tensor.matmul(ps[:, 7, 0:LOG * HEADS], ones[:, :], flat, start=True, stop=True).then_inc(dsum_ps, 1)
                for slot in range(SLOTS):
                    pe.wait_ge(ring_in[slot], 32 * (it + 1))
                for g, tiles in ((0, range(PAGES + 1)), (1, range(PAGES + 1, LOG))):
                    for c in range(4):
                        o0 = 256 + (4 * g + c) * HEADS
                        last = chain(ps[:, 7, o0:o0 + HEADS], [(value_tile(j, c), Lp[0:log_slot(j)[0], j, :]) for j in tiles])
                last.then_inc(dpv_ps, 1)

        upto = [[0], [0]]
        for it in range(PAIRS):
            for hh, qt in STEP:
                for g in range(2):
                    upto[g].append(upto[g][-1] + (qt // 4 >= g))

        def att_act(act):
            for it in range(PAIRS):
                for g in range(2):
                    act.wait_ge(qk_ps, 4 * it + g + 1)
                    act.activation(QT[:, 512 * g:512 * (g + 1)], ps[:, g, :], ACT.Copy).then_inc(qk_act, 1)

                def copy_low(k):
                    s = 16 * it + k
                    act.wait_ge(pt_ps0, upto[0][s] + 1)
                    positive_wait(act, pv_ps, s - 1)
                    n = min(4, STEP[k][1] + 1)
                    act.activation(PT[s % 2][:, 0:n, :].rearrange("p b q -> p (b q)"), ps[:, 4, 0:n * P], ACT.Copy).then_inc(pt_out0, 1)
                for k in range(16):
                    s = 16 * it + k
                    hh, qt = STEP[k]
                    n = P * (qt + 1)
                    act.wait_ge(s_nm, s + 1)
                    if s >= 2:
                        act.wait_ge(pt_ps0, upto[0][s - 2] + 1)
                        if STEP[(k - 2) % 16][1] >= 4:
                            act.wait_ge(pt_ps1, upto[1][s - 2] + 1)
                    if it and k == 0:
                        act.wait_ge(rl_done, 16 * it)
                    act.activation(Pr[s % 2][:, 0:n], S2[s % 2][:, 0:n], ACT.Exp, bias=nm[:, k:k + 1], scale=SCALE,
                                   accum_out=lsum[:, k:k + 1]).then_inc(p_done, 1)
                    if k > 0:
                        copy_low(k - 1)
                copy_low(15)
                act.wait_ge(dch, DCH * it + 5)
                positive_wait(act, dpv_ps, it)
                act.activation(Lp[:, :, :], Lb[:, :, :], ACT.Exp).then_inc(dp_done, 1)

        def att_dve(dve):
            for it in range(PAIRS):
                grp, j4 = it // 4, it % 4

                def log_sum(j):
                    n = LOG * it + j
                    r = log_slot(j)[0]
                    dve.wait_ge(prod_done, n + 1)
                    dve.tensor_reduce(L[0:r, j, :], prod[n % 2][0:r, :].rearrange("p (h e) -> p h e", h=HEADS), AX,
                                      ALU.add).then_inc(log_done, 1)

                def finish(k):
                    s = 16 * it + k
                    hh, qt = STEP[k]
                    if qt >= 4:
                        dve.wait_ge(pt_ps1, upto[1][s] + 1)
                        positive_wait(dve, pv_ps, s - 1)
                        dve.tensor_copy(PT[s % 2][:, 4:qt + 1, :].rearrange("p b q -> p (b q)"), ps[:, 5, 0:(qt - 3) * P]).then_inc(pt_out1, 1)
                    dve.wait_ge(p_done, s + 1)
                    dve.reciprocal(rl[:, k:k + 1], lsum[:, k:k + 1]).then_inc(rl_done, 1)
                    dve.wait_ge(rl_done, s + 1)
                    dve.wait_ge(pv_ps, s + 1)
                    if k == 0 and it:
                        dve.wait_ge(ot_ps, 2 * it)
                    dve.tensor_scalar(O[:, qt, hh * HD:(hh + 1) * HD], ps[:, 6, 0:HD], rl[:, k:k + 1], None, ALU.mult).then_inc(o_done, 1)

                for g in range(2):
                    dve.wait_ge(qk_ps, 4 * it + 2 + g + 1)
                    dve.tensor_copy(KTr[:, 512 * g:512 * (g + 1)], ps[:, 2 + g, :]).then_inc(qk_dve, 1)
                for k in range(16):
                    s = 16 * it + k
                    hh, qt = STEP[k]
                    n = P * (qt + 1)
                    if grp == 0:
                        b = bias[hh]
                        if k % 8 == 0:
                            dve.wait_ge(bias_in[hh], 16 * (it + 1))
                        d = b[:, qt * P:(qt + 1) * P]
                        dve.tensor_tensor(d, d, causal[:, :], ALU.add).then_inc(masked, 1)
                        dve.wait_ge(masked, s + 1)
                        row = b[:, 0:n]
                    else:
                        row = dist[:, SEQ - n:SEQ]
                    dve.wait_ge(s_ps, s + 1)
                    positive_wait(dve, p_done, s - 1)
                    dve.tensor_tensor_reduce(S2[s % 2][:, 0:n], s_banks(s)[:, 0:n], row, 1.0, NEG, ALU.add, ALU.max,
                                             accum_out=mx[:, k:k + 1]).then_inc(s_biased, 1)
                    dve.wait_ge(s_biased, s + 1)
                    dve.tensor_scalar(nm[:, k:k + 1], mx[:, k:k + 1], -SCALE, None, ALU.mult).then_inc(s_nm, 1)
                    if k > 0:
                        finish(k - 1)
                    if k >= 3:
                        log_sum(k - 3)
                finish(15)
                n = DCH * it

                def step(ins):
                    ins.then_inc(dch, 1)
                dve.wait_ge(log_done, LOG * (it + 1))
                step(dve.scalar_tensor_tensor(Lb[:, :, :], L[:, :, :], SCALE, dbias[:, it, :, :], ALU.mult, ALU.add))
                dve.wait_ge(dch, n + 1)
                step(dve.tensor_reduce(Lm[:, 0, :], Lb[:, 0:PAGES + 1, :].rearrange("p j h -> p h j"), AX, ALU.max))
                step(dve.tensor_reduce(Lm[:, 1, :], Lb[:, PAGES + 1:LOG, :].rearrange("p j h -> p h j"), AX, ALU.max))
                dve.wait_ge(ar_done, it + 1)
                step(dve.tensor_tensor(Lb[:, 0:PAGES + 1, :], Lb[:, 0:PAGES + 1, :],
                                       LM[:, 0:1, :].to_broadcast([P, PAGES + 1, HEADS]), ALU.subtract))
                step(dve.tensor_tensor(Lb[:, PAGES + 1:LOG, :], Lb[:, PAGES + 1:LOG, :],
                                       LM[:, 1:2, :].to_broadcast([P, 4, HEADS]), ALU.subtract))
                for g in range(2):
                    c0 = NS + 512 * g
                    dve.wait_ge(ot_ps, 2 * it + g + 1)
                    dve.tensor_copy(Xh[:, it, c0:c0 + 512], ps[:, 7, :]).then_inc(ot_high, 1)
                    dve.wait_ge(ot_high, 2 * it + g + 1)
                    dve.tensor_tensor(Xl[:, it, c0:c0 + 512], ps[:, 7, :], Xh[:, it, c0:c0 + 512].bitcast(F32),
                                      ALU.subtract).then_inc(ot_low, 1)
                dve.wait_ge(dpv_ps, it + 1)
                sums = ps[:, 7, 0:LOG * HEADS].rearrange("p (j h) -> p h j", j=LOG)
                step(dve.tensor_reduce(dl[:, 0, :], sums[:, :, 0:PAGES + 1], AX, ALU.add))
                step(dve.tensor_reduce(dl[:, 1, :], sums[:, :, PAGES + 1:LOG], AX, ALU.add))
                dve.wait_ge(dch, n + 7)
                step(dve.reciprocal(drl[:, :, :], dl[:, :, :]))
                dve.wait_ge(dch, n + 8)
                mine = ps[:, 7, 256:256 + 8 * HEADS].rearrange("p (g c h) -> p g c h", g=2, c=4)
                step(dve.tensor_tensor(do1[:, :, :, :], mine, drl[:, :, :].unsqueeze(2).to_broadcast([P, 2, 4, HEADS]), ALU.mult))
                dve.wait_ge(dch, n + 9)
                step(dve.tensor_tensor(do2[:, :, :, :], do1[:, :, :, :], hsel[:, :, :].unsqueeze(1).to_broadcast([P, 2, 4, HEADS]), ALU.mult))
                dve.wait_ge(dch, n + 10)
                dve.tensor_reduce(oS[:, :, it], do2[:, :, :, :].rearrange("p g c h -> p (g c) h"), AX, ALU.add).then_inc(osamp, 1)
            dve.wait_ge(osamp, PAIRS)
            dve.tensor_copy(Xh[:, :, 0:NS], oS[:, :, :]).then_inc(osamp, 1)
            dve.wait_ge(osamp, PAIRS + 1)
            dve.tensor_tensor(Xl[:, :, 0:NS], oS[:, :, :], Xh[:, :, 0:NS].bitcast(F32), ALU.subtract).then_inc(osamp, 1)
        ATT_DONE = (osamp, PAIRS + 2)

        def narrow_pe(pe, base, ps_done, ps_free, free_offset=0):
            for m in range(KT):
                n = base + m
                pe.wait_ge(split_done, n + 1)
                for b, (c0, w) in enumerate(BLOCKS):
                    j = NB * m + b
                    positive_wait(pe, ps_free, j - 5)
                    last = chain(ps[:, j % 6, 0:w],
                                 [pr for k in range(KT)
                                  for pr in split_products(wh(n)[:, k * P:(k + 1) * P], wl(n)[:, k * P:(k + 1) * P],
                                                           Xh[:, k, c0:c0 + w], Xl[:, k, c0:c0 + w])])
                    last.then_inc(ps_done, 1)
                pe.wait_ge(ps_done, NB * (m + 1))
                pe.sem_inc(w_used, 1)

        def residual_dve(dve, ps_done, ps_free):
            for m in range(KT):
                for b, (c0, w) in enumerate(BLOCKS):
                    j = NB * m + b
                    dve.wait_ge(ps_done, j + 1)
                    x = xT[:, m, c0:c0 + w]
                    dve.tensor_tensor(x, ps[:, j % 6, 0:w], x, ALU.add).then_inc(ps_free, 1)

        op_ps, op_free, oc_ps, oc_free = (sem(n) for n in ("op_ps", "op_free", "oc_ps", "oc_free"))

        GU = 2 * NB * GF
        HB = NB * GF
        DN = NB * KT
        ffn_sem = {k: (sem(f"ffn_{k}"), n * STEPS) for k, n in (
            ("gu_ps", GU), ("silu", HB), ("hid", HB), ("high", HB), ("low", HB), ("dn_ps", DN), ("dn_add", DN))}
        FFN = [{k: Counted(x, n * j) for k, (x, n) in ffn_sem.items()} for j in range(2)]

        def ffn_pe(pe, f, base, norm, layer):
            def step(i):
                for q in range(GU):
                    t, half, b = q // (2 * NB), q // NB % 2, q % NB
                    c0, w = BLOCKS[b]
                    n = 2 * t + half
                    if isinstance(i, int) and q < NB:
                        norm["low"].wait(pe, KT * (b + 1))
                    if b == 0:
                        pe.wait_ge(split_done, base + i * 6 + n + 1)
                    if q < 6:
                        f["dn_add"].wait(pe, i * DN - 5 + q)
                    elif q < 6 + NB:
                        f["silu"].wait(pe, i * HB + q - 5)
                    else:
                        f["hid"].wait(pe, i * HB + q - 5 - NB)
                    last = chain(ps[:, q % 6, 0:w],
                                 [pr for k in range(KT)
                                  for pr in split_products(wh(base + n)[:, k * P:(k + 1) * P], wl(base + n)[:, k * P:(k + 1) * P],
                                                           Xh[:, k, c0:c0 + w], Xl[:, k, c0:c0 + w])])
                    last.then_inc(f["gu_ps"].sem, 1)
                    if b == NB - 1:
                        f["gu_ps"].wait(pe, i * GU + q + 1)
                        pe.sem_inc(w_used, 1)
                for b, (c0, w) in enumerate(BLOCKS):
                    f["low"].wait(pe, i * HB + NB + b + 1)
                    for m in range(KT):
                        q = b * KT + m
                        if q == 0:
                            pe.wait_ge(split_done, base + i * 6 + 6)
                        if q < 3:
                            f["silu"].wait(pe, i * HB + NB + q + 1)
                        elif q < 6:
                            f["hid"].wait(pe, i * HB + NB + q - 3 + 1)
                        else:
                            f["dn_add"].wait(pe, i * DN + q - 5)
                        last = chain(ps[:, q % 6, 0:w],
                                     [pr for t in range(GF)
                                      for pr in split_products(wh(base + 4 + t)[:, m * P:(m + 1) * P], wl(base + 4 + t)[:, m * P:(m + 1) * P],
                                                               Hh[:, t, c0:c0 + w], Hl[:, t, c0:c0 + w])])
                        last.then_inc(f["dn_ps"].sem, 1)
                f["dn_ps"].wait(pe, i * DN + DN)
                pe.sem_inc(w_used, 2)
            peeled_loop(pe, STEPS, step)

        def ffn_act(act, f):
            def step(i):
                for t in range(GF):
                    for b, (c0, w) in enumerate(BLOCKS):
                        f["gu_ps"].wait(act, i * GU + t * 2 * NB + b + 1)
                        f["hid"].wait(act, i * HB + (t - 1) * NB + b + 1)
                        act.activation(sg[:, b, 0:w], ps[:, b, 0:w], ACT.Silu).then_inc(f["silu"].sem, 1)
                    for b, (c0, w) in enumerate(BLOCKS):
                        f["dn_ps"].wait(act, i * DN)
                        f["hid"].wait(act, i * HB + t * NB + b + 1)
                        act.activation(Hh[:, t, c0:c0 + w], hf[:, b, 0:w], ACT.Copy).then_inc(f["high"].sem, 1)
            peeled_loop(act, STEPS, step)

        def ffn_dve(dve, f):
            def step(i):
                for t in range(GF):
                    for b, (c0, w) in enumerate(BLOCKS):
                        f["gu_ps"].wait(dve, i * GU + t * 2 * NB + NB + b + 1)
                        f["silu"].wait(dve, i * HB + t * NB + b + 1)
                        dve.tensor_tensor(hf[:, b, 0:w], ps[:, 3 + b, 0:w], sg[:, b, 0:w], ALU.mult).then_inc(f["hid"].sem, 1)
                        f["high"].wait(dve, i * HB + t * NB + b + 1)
                        dve.tensor_tensor(Hl[:, t, c0:c0 + w], hf[:, b, 0:w], Hh[:, t, c0:c0 + w].bitcast(F32),
                                          ALU.subtract).then_inc(f["low"].sem, 1)
                for b, (c0, w) in enumerate(BLOCKS):
                    for m in range(KT):
                        q = b * KT + m
                        f["dn_ps"].wait(dve, i * DN + q + 1)
                        x = xT[:, m, c0:c0 + w]
                        dve.tensor_tensor(x, ps[:, q % 6, 0:w], x, ALU.add).then_inc(f["dn_add"].sem, 1)
            peeled_loop(dve, STEPS, step)

        names = ("g_in g_in2 g_in3 wt_ps wt_done rt_ps rt_done v_ps v_gelu v_sqsum v_stat v_norm mix_ps mix_done vst_ps vst_done "
                 "vs_ps vs_done u_ps u_gelu y_done yh yl cv_out")
        G = {n: sem(n) for n in names.split()}
        bvrep, bsrow, wsp = VM[:, 7, :], VM[0:1, 6, :], VM[:, 5, :]

        def gmlp_sp(sp, norm):
            norm["low"].wait(sp, NB * KT)
            sp.dma_start(wsp.rearrange("p (g s) -> p g s", g=KT), a["w_spatial"][0].rearrange("g t s -> t g s")).then_inc(G["g_in"], 16)
            sp.dma_start(bvrep, a["b_v_c"][0, :].partition_broadcast(P)).then_inc(G["g_in2"], 16)
            sp.dma_start(bsrow, a["b_spatial"].rearrange("o g t -> o (g t)")).then_inc(G["g_in2"], 16)
            with nc.allow_non_contiguous_dma("one number a head group"):
                sp.dma_start(w00[:, :], a["w_spatial"][0, :, 0, 0].partition_broadcast(P)).then_inc(G["g_in3"], 16)
                sp.dma_start(b00[:, :], a["b_spatial"][0, :, 0].partition_broadcast(P)).then_inc(G["g_in3"], 16)

        def gmlp_pe(pe, norm):
            pe.wait_ge(G["g_in"], 16)
            for g in range(KT):
                last = nc.tensor.transpose(ps[:, 4 + g // 4, (g % 4) * P:(g % 4 + 1) * P], wsp[:, g * P:(g + 1) * P], ident[:, :])
                if g % 4 == 3:
                    last.then_inc(G["wt_ps"], 1)
            pe.wait_ge(G["wt_done"], 2)
            pe.wait_ge(G["g_in2"], 32)
            for g in range(KT):
                last = chain(ps[:, 4 + g // 4, (g % 4) * P:(g % 4 + 1) * P],
                             [(bvrep[:, g * P:(g + 1) * P], wT[:, g, :]), (ones[0:1, :], bsrow[:, g * P:(g + 1) * P])])
                if g % 4 == 3:
                    last.then_inc(G["rt_ps"], 1)
            for c in range(2):
                for tt in range(TT):
                    q = c * TT + tt
                    if c == 0 and tt in (0, 4, 7):
                        norm["low"].wait(pe, KT * (1 + (tt >= 4) + (tt >= 7)))
                    positive_wait(pe, G["v_gelu"], q - ZB + 1)
                    wide_products(pe, BASE_V + 4 * c, BASE_V + 4 * c, None, c, tt, q, None).then_inc(G["v_ps"], 1)
                pe.wait_ge(G["v_ps"], (c + 1) * TT)
                pe.sem_inc(w_used, 1)

            def u_unit(m):
                n = BASE_U + m
                pe.wait_ge(split_done, n + 1)
                for b, (c0, w) in enumerate(BLOCKS):
                    j = NB * m + b
                    if j < 6:
                        pe.wait_ge(G["v_gelu"], 2 * TT)
                        pe.wait_ge(G["rt_done"], 2)
                    positive_wait(pe, G["u_gelu"], j - 5)
                    last = chain(ps[:, j % 6, 0:w],
                                 [pr for k in range(KT)
                                  for pr in split_products(wh(n)[:, k * P:(k + 1) * P], wl(n)[:, k * P:(k + 1) * P],
                                                           Xh[:, k, c0:c0 + w], Xl[:, k, c0:c0 + w])])
                    last.then_inc(G["u_ps"], 1)
                pe.wait_ge(G["u_ps"], NB * (m + 1))
                pe.sem_inc(w_used, 1)
            u_unit(0)
            u_unit(1)
            pe.wait_ge(G["v_norm"], TT)
            for g in range(KT):
                last = nc.tensor.transpose(ps[:, 6, g * NS:(g + 1) * NS], vs[:, g * P:(g + 1) * P], ident[0:NS, 0:NS])
            last.then_inc(G["vst_ps"], 1)
            pe.wait_ge(G["vst_done"], 1)
            for g in range(KT):
                last = nc.tensor.matmul(ps[0:NS, 6 + g // 4, (g % 4) * P:(g % 4 + 1) * P], vsT[:, g, :], ident[:, :], start=True, stop=True)
            last.then_inc(G["vs_ps"], 1)
            pe.wait_ge(G["vs_done"], 2)
            for tile in range(SEQ // P):
                for half in range(2):
                    j = 2 * tile + half
                    positive_wait(pe, G["mix_done"], (j - 1) * 4)
                    for g in range(4 * half, 4 * half + 4):
                        last = nc.tensor.matmul(ps[:, 6 + half, (g % 4) * P:(g % 4 + 1) * P], VM[:, tile, g * P:(g + 1) * P],
                                                wT[:, g, :], start=True, stop=True)
                    last.then_inc(G["mix_ps"], 1)
            for m in range(2, KT):
                u_unit(m)

        def gmlp_act(act, norm):
            for half in range(2):
                act.wait_ge(G["rt_ps"], half + 1)
                act.activation(RT[:, 4 * half:4 * half + 4, :].rearrange("p g t -> p (g t)"), ps[:, 4 + half, :], ACT.Copy).then_inc(G["rt_done"], 1)
            norm["low"].wait(act, NB * KT)
            act.wait_ge(G["rt_ps"], 2)
            act.wait_ge(G["v_stat"], 1)
            for c in range(2):
                for tt in range(TT):
                    q, r = c * TT + tt, token_rows(tt)
                    dst = vs[:, c * DH:(c + 1) * DH] if tt == 0 else VM[:, tt - 1, c * DH:(c + 1) * DH]
                    act.wait_ge(G["v_ps"], q + 1)
                    act.activation(dst, ps[0:r, q % ZB, :], ACT.Gelu, accum_out=vsum[0:r, tt, c:c + 1]).then_inc(G["v_gelu"], 1)
            act.wait_ge(G["v_stat"], 3)
            for tt in range(TT):
                r = token_rows(tt)
                src = vs[:, :] if tt == 0 else VM[:, tt - 1, :]
                for c in range(2):
                    positive_wait(act, G["v_sqsum"], 2 * tt + c)
                    act.activation(junk[0:r, 0:DH], src[:, c * DH:(c + 1) * DH], ACT.Square, bias=vst[0:r, 1, tt:tt + 1],
                                   accum_out=vsum[0:r, tt, c:c + 1]).then_inc(G["v_sqsum"], 1)
            act.wait_ge(G["v_stat"], 4)
            act.activation(vst[:, 3, :], vst[:, 2, :], ACT.Sqrt, bias=eps[:, 0:1], scale=1.0 / D).then_inc(G["v_sqsum"], 1)
            for m in range(KT):
                for b, (c0, w) in enumerate(BLOCKS):
                    j = NB * m + b
                    act.wait_ge(G["u_ps"], j + 1)
                    positive_wait(act, G["y_done"], j - 1)
                    act.wait_ge(G["v_norm"], TT)
                    act.activation(ug[j % 2][:, 0:w], ps[:, j % 6, 0:w], ACT.Gelu).then_inc(G["u_gelu"], 1)
            act.wait_ge(G["u_ps"], NB * KT)
            for b, (c0, w) in enumerate(BLOCKS):
                for m in range(KT):
                    if b == 0:
                        act.wait_ge(G["y_done"], NB * m + 3)
                        act.activation(Xh[:, m, 0:NS], msT[:, m, :], ACT.Copy)
                    t0, t1 = (0, 3, 6, 8)[b:b + 2]
                    lo = NS + t0 * P
                    act.activation(Xh[:, m, lo:lo + (t1 - t0) * P].rearrange("p (t q) -> p t q", q=P),
                                   VM[:, t0:t1, m * P:(m + 1) * P], ACT.Copy).then_inc(G["yh"], 1)

        junk = wT_src = None

        def gmlp_dve(dve, norm):
            for half in range(2):
                dve.wait_ge(G["wt_ps"], half + 1)
                dve.tensor_tensor(wT[:, 4 * half:4 * half + 4, :], ps[:, 4 + half, :].rearrange("p (g t) -> p g t", g=4),
                                  tri[:, :].unsqueeze(1).to_broadcast([P, 4, P]), ALU.mult).then_inc(G["wt_done"], 1)
            dve.memset(vsum[:, :, :], 0.0).then_inc(G["v_stat"], 1)
            dve.wait_ge(G["v_gelu"], 2 * TT)
            dve.tensor_tensor(vst[:, 0, :], vsum[:, :, 0], vsum[:, :, 1], ALU.add).then_inc(G["v_stat"], 1)
            dve.wait_ge(G["v_stat"], 2)
            dve.tensor_scalar(vst[:, 1, :], vst[:, 0, :], -1.0 / D, None, ALU.mult).then_inc(G["v_stat"], 1)
            dve.wait_ge(G["v_sqsum"], 2 * TT)
            dve.tensor_tensor(vst[:, 2, :], vsum[:, :, 0], vsum[:, :, 1], ALU.add).then_inc(G["v_stat"], 1)
            dve.wait_ge(G["v_sqsum"], 2 * TT + 1)
            dve.reciprocal(vst[:, 0, :], vst[:, 3, :]).then_inc(G["v_stat"], 1)
            dve.wait_ge(G["v_stat"], 5)
            for tt in range(TT):
                r = token_rows(tt)
                v = vs[:, :] if tt == 0 else VM[:, tt - 1, :]
                dve.tensor_scalar(v, v, vst[0:r, 1, tt:tt + 1], vst[0:r, 0, tt:tt + 1], ALU.add, ALU.mult).then_inc(G["v_norm"], 1)
            dve.wait_ge(G["vst_ps"], 1)
            dve.wait_ge(G["g_in3"], 32)
            n = [0]

            def step(ins):
                n[0] += 1
                ins.then_inc(vchain, 1)
                dve.wait_ge(vchain, n[0])
            step(dve.tensor_tensor(msT[:, :, :], ps[:, 6, 0:KT * NS].rearrange("p (g s) -> p g s", g=KT),
                                   gv[:, :].unsqueeze(2).to_broadcast([P, KT, NS]), ALU.mult))
            dve.tensor_tensor(vsT[:, :, :], msT[:, :, :], bv[:, :].unsqueeze(2).to_broadcast([P, KT, NS]), ALU.add).then_inc(G["vst_done"], 1)
            dve.wait_ge(G["vst_done"], 1)
            step(dve.tensor_tensor(msT[:, :, :], vsT[:, :, :], w00[:, :].unsqueeze(2).to_broadcast([P, KT, NS]), ALU.mult))
            step(dve.tensor_tensor(msT[:, :, :], msT[:, :, :], b00[:, :].unsqueeze(2).to_broadcast([P, KT, NS]), ALU.add))
            dve.wait_ge(G["vs_ps"], 1)
            for half in range(2):
                dve.tensor_copy(vs[:, half * DH:(half + 1) * DH], ps[0:NS, 6 + half, :]).then_inc(G["vs_done"], 1)
            for tile in range(SEQ // P):
                for half in range(2):
                    dve.wait_ge(G["mix_ps"], 2 * tile + half + 1)
                    for g in range(4 * half, 4 * half + 4):
                        dve.scalar_tensor_tensor(VM[:, tile, g * P:(g + 1) * P], ps[:, 6 + half, (g % 4) * P:(g % 4 + 1) * P],
                                                 gv[:, g:g + 1], RT[:, g, :], ALU.mult, ALU.add).then_inc(G["mix_done"], 1)
            dve.wait_ge(G["mix_done"], 8 * SEQ // P)
            for m in range(KT):
                for b, (c0, w) in enumerate(BLOCKS):
                    j = NB * m + b
                    t0, t1 = (0, 3, 6, 8)[b:b + 2]
                    dve.wait_ge(G["u_gelu"], j + 1)
                    off = NS if b == 0 else 0
                    if b == 0:
                        dve.tensor_tensor(msT[:, m, :], msT[:, m, :], ug[j % 2][:, 0:NS], ALU.mult)
                    y = VM[:, t0:t1, m * P:(m + 1) * P]
                    dve.tensor_tensor(y, y, ug[j % 2][:, off:w].rearrange("p (t q) -> p t q", q=P), ALU.mult).then_inc(G["y_done"], 1)
            for b, (c0, w) in enumerate(BLOCKS):
                for m in range(KT):
                    t0, t1 = (0, 3, 6, 8)[b:b + 2]
                    lo = NS + t0 * P
                    dve.wait_ge(G["yh"], KT * b + m + 1)
                    if b == 0:
                        dve.tensor_tensor(Xl[:, m, 0:NS], msT[:, m, :], Xh[:, m, 0:NS].bitcast(F32), ALU.subtract)
                    dve.tensor_tensor(Xl[:, m, lo:lo + (t1 - t0) * P].rearrange("p (t q) -> p t q", q=P),
                                      VM[:, t0:t1, m * P:(m + 1) * P],
                                      Xh[:, m, lo:lo + (t1 - t0) * P].bitcast(F32).rearrange("p (t q) -> p t q", q=P),
                                      ALU.subtract).then_inc(G["yl"], 1)

        vchain = sem("vchain")
        junk = ug[0] if False else None
        used[0] = stage_memory
        junk = nc.alloc_sbuf_tensor_at("junk", [P, DH], F32, offset=(nc.sbuf_usable_end - 4 * DH) // 32 * 32)

        used[0] = norm_end
        yt = [place(f"yt{j}", [P, D]) for j in range(2)]
        fin_lo, fin_hi, fin_act, fin_dve = (sem(n) for n in ("fin_lo", "fin_hi", "fin_act", "fin_dve"))
        y_out = sems("y_out", 2)
        n1 = NORMS

        CONSTS = 13
        block = ctx.enter_context(nc.Block())

        @block.sync
        def _(sp):
            for tt in range(NX):
                src = a["x_sample"] if tt == 0 else a["x_prompt"][(tt - 1) * P:tt * P, :]
                sp.dma_start(xs[tt][0:token_rows(tt), :], src).then_inc(x_in[tt], 16)
            with nc.allow_non_contiguous_dma("small constants, once"):
                for dst, src in ((ident[:, :], a["c_ident"]), (tri[:, :], a["c_uo"][:, 0:P]),
                                 (gains[:, 0, :], a["norm_mix"][0].rearrange("(m p) -> p m", p=P)),
                                 (gains[:, 1, :], a["norm_ffn"][0].rearrange("(m p) -> p m", p=P)),
                                 (gains[:, 2, :], a["norm_mix"][1].rearrange("(m p) -> p m", p=P)),
                                 (gains[:, 3, :], a["norm_ffn"][1].rearrange("(m p) -> p m", p=P)),
                                 (gv[:, :], a["g_v_c"][0].rearrange("(m p) -> p m", p=P)),
                                 (bv[:, :], a["b_v_c"][0].rearrange("(m p) -> p m", p=P)),
                                 (cs[:, :, :, :], a["c_rope"]),
                                 (gqk[:, 0, :], a["g_q_a"][0].partition_broadcast(P)),
                                 (gqk[:, 1, :], a["g_k_a"][0].partition_broadcast(P)),
                                 (gqk[:, 2, :], a["g_q_b"][0].partition_broadcast(P)),
                                 (gqk[:, 3, :], a["g_k_b"][0].partition_broadcast(P))):
                    sp.dma_start(dst, src).then_inc(const_in, 16)
                sp.dma_start(wf[:, :, :], a["w_in_even"][:, 3 * DH:3 * DH + HEADS].rearrange("(k p) n -> p k n", p=P)).then_inc(wf_in, 16)
                sp.dma_start(bf[:, :], a["b_forget"][0].partition_broadcast(P)).then_inc(wf_in, 16)
            for tt in range(NX, TT):
                sp.wait_ge(xt_lo, tt - NX + 1)
                sp.wait_ge(xt_hi, tt - NX + 1)
                sp.dma_start(xs[tt % NX][:, :], a["x_prompt"][(tt - 1) * P:tt * P, :]).then_inc(x_in[tt % NX], 16)

            def project(i):
                for c in range(3):
                    for j in range(IN_UNITS):
                        n = 4 * c + j
                        src = a["w_in_even"][2 * j * P:(2 * j + 2) * P, bass.ds(i * (3 * DH + HEADS) + c * DH, DH)]
                        load_unit(sp, BASE_IN + i * 12 + n, n, src.rearrange("(k p) n -> p k n", p=P), 2)
            peeled_loop(sp, 2, project)
            forget_sp(sp)
            att_sp(sp)
            sp.wait_ge(*ATT_DONE)
            load_narrow(sp, BASE_OUT, a["w_out_even"][0], 8)
            load_ffn(sp, BASE_F0, 0)
            gmlp_sp(sp, n1[2])
            for c in range(2):
                load_wide(sp, BASE_V + 4 * c, a["w_in_c"][0], D + c * DH)
            load_narrow(sp, BASE_U, a["w_in_c"][0], 8)
            sp.wait_ge(G["vs_done"], 2)
            sp.dma_start(a["cv_sample"], vs[:, :]).then_inc(G["cv_out"], 16)
            load_narrow(sp, BASE_OC, a["w_out_c"][0], 8)
            load_ffn(sp, BASE_F1, 1)
            sp.wait_ge(lf_out, 32)
            sp.wait_ge(G["cv_out"], 16)
            sp.wait_ge(y_out[0], 16 * 5)
            sp.wait_ge(y_out[1], 16 * 4)

        @block.gpsimd
        def _(pool):
            pool.memset(zeros[:, :], 0.0).then_inc(zero_set, 1)
            pool.memset(ones[:, :], 1.0).then_inc(zero_set, 1)
            pool.wait_ge(zero_set, 2)

            def project(i):
                for n in range(12):
                    split_unit(pool, i * 12 + n, n)
            peeled_loop(pool, 2, project)
            att_pool(pool)
            pool.wait_ge(*ATT_DONE)
            pool.wait_ge(dpv_ps, PAIRS)
            for n in range(BASE_OUT, BASE_F0):
                split_unit(pool, n, n)

            def ffn(base):
                def step(i):
                    for n in range(6):
                        split_unit(pool, base + i * 6 + n, base + n)
                peeled_loop(pool, STEPS, step)
            ffn(BASE_F0)
            for n in range(BASE_V, BASE_F1):
                split_unit(pool, n, n)
            ffn(BASE_F1)

        def input_ready(eng, b):
            n = (4, 7, 9)[b]
            eng.wait_ge(xt_act, n)
            eng.wait_ge(xt_dve, n)

        @block.tensor
        def _(pe):
            pe.wait_ge(const_in, 16 * CONSTS)
            pe.wait_ge(zero_set, 2)
            for tt in range(TT):
                r = token_rows(tt)
                pe.wait_ge(x_in[tt % NX], 16 * (tt // NX + 1))
                for half, (done, free) in enumerate(((xt_lo, xt_act), (xt_hi, xt_dve))):
                    positive_wait(pe, free, tt - 2)
                    for m in range(4):
                        last = nc.tensor.transpose(ps[:, 3 * half + tt % 3, m * P:m * P + r],
                                                   xs[tt % NX][0:r, (4 * half + m) * P:(4 * half + m + 1) * P], ident[0:r, 0:r])
                    last.then_inc(done, 1)
            norm_pe(pe, n1[0])
            in_pe(pe)
            forget_pe(pe)
            pe.wait_ge(lg, 14)
            att_pe(pe)
            pe.wait_ge(*ATT_DONE)
            narrow_pe(pe, BASE_OUT, op_ps, op_free)
            norm_pe(pe, n1[1])
            ffn_pe(pe, FFN[0], BASE_F0, n1[1], 0)
            norm_pe(pe, n1[2])
            gmlp_pe(pe, n1[2])
            pe.wait_ge(G["yl"], KT * NB)
            narrow_pe(pe, BASE_OC, oc_ps, oc_free)
            norm_pe(pe, n1[3])
            ffn_pe(pe, FFN[1], BASE_F1, n1[3], 1)
            FFN[1]["dn_add"].wait(pe, DN * STEPS)
            for tt in range(TT):
                t0 = token_columns(tt)
                for half, (done, free) in enumerate(((fin_lo, fin_act), (fin_hi, fin_dve))):
                    positive_wait(pe, free, tt - 2)
                    for m in range(4):
                        last = nc.tensor.transpose(ps[:, 3 * half + tt % 3, m * P:(m + 1) * P], xT[:, 4 * half + m, t0:t0 + P], ident[:, :])
                    last.then_inc(done, 1)

        def finish_half(eng, half):
            done, free = ((fin_lo, fin_act), (fin_hi, fin_dve))[half]
            for tt in range(TT):
                r = token_rows(tt)
                eng.wait_ge(done, tt + 1)
                positive_wait(eng, y_out[tt % 2], 16 * (tt // 2))
                dst, src = yt[tt % 2][0:r, half * 512:(half + 1) * 512], ps[0:r, 3 * half + tt % 3, :]
                if half == 0:
                    eng.activation(dst, src, ACT.Copy).then_inc(free, 1)
                    eng.wait_ge(fin_dve, tt + 1)
                    eng.wait_ge(fin_act, tt + 1)
                    out = a["y_sample"] if tt == 0 else a["y_prompt"][(tt - 1) * P:tt * P, :]
                    eng.dma_start(out, yt[tt % 2][0:r, :]).then_inc(y_out[tt % 2], 16)
                else:
                    eng.tensor_copy(dst, src).then_inc(free, 1)

        @block.scalar
        def _(act):
            for tt in range(TT):
                r, t0 = token_rows(tt), token_columns(tt)
                act.wait_ge(xt_lo, tt + 1)
                act.activation(xT[:, 0:4, t0:t0 + r], ps[:, tt % 3, :].rearrange("p (m t) -> p m t", m=4)[:, :, 0:r],
                               ACT.Copy).then_inc(xt_act, 1)
            act.wait_ge(eps_set, 1)
            norm_act(act, n1[0], input_ready)
            in_act(act)
            forget_act(act)
            act.wait_ge(lg, 14)
            att_act(act)
            norm_act(act, n1[1], lambda e, b: e.wait_ge(op_free, NB * KT - 2 + b))
            ffn_act(act, FFN[0])
            norm_act(act, n1[2], lambda e, b: FFN[0]["dn_add"].wait(e, DN * (STEPS - 1) + KT * (b + 1)))
            gmlp_act(act, n1[2])
            norm_act(act, n1[3], lambda e, b: e.wait_ge(oc_free, NB * KT - 2 + b))
            ffn_act(act, FFN[1])
            finish_half(act, 0)

        @block.vector
        def _(dve):
            dve.memset(eps[:, :], EPS).then_inc(eps_set, 1)
            for tt in range(TT):
                r, t0 = token_rows(tt), token_columns(tt)
                dve.wait_ge(xt_hi, tt + 1)
                dve.tensor_copy(xT[:, 4:8, t0:t0 + r], ps[:, 3 + tt % 3, :].rearrange("p (m t) -> p m t", m=4)[:, :, 0:r]).then_inc(xt_dve, 1)
            dve.wait_ge(const_in, 16 * CONSTS)
            norm_dve(dve, n1[0], 0, input_ready)
            dve.wait_ge(wf_in, 32)
            dve.tensor_copy(wfh[:, :, :], wf[:, :, :]).then_inc(wf_high, 1)
            dve.wait_ge(wf_high, 1)
            dve.tensor_tensor(wfl[:, :, :], wf[:, :, :], wfh[:, :, :].bitcast(F32), ALU.subtract).then_inc(wf_low, 1)
            in_dve(dve)
            forget_dve(dve)
            att_dve(dve)
            residual_dve(dve, op_ps, op_free)
            norm_dve(dve, n1[1], 1, lambda e, b: e.wait_ge(op_free, NB * KT - 2 + b))
            ffn_dve(dve, FFN[0])
            norm_dve(dve, n1[2], 2, lambda e, b: FFN[0]["dn_add"].wait(e, DN * STEPS))
            gmlp_dve(dve, n1[2])
            residual_dve(dve, oc_ps, oc_free)
            norm_dve(dve, n1[3], 3, lambda e, b: e.wait_ge(oc_free, NB * KT - 2 + b))
            ffn_dve(dve, FFN[1])
            finish_half(dve, 1)


def shape_constants():
    import numpy as np
    f = np.float32
    r, c = np.arange(P)[:, None], np.arange(P)[None, :]
    tri = (r <= c).astype(f)
    dist = SEQ - P + np.arange(P)[:, None] - np.arange(SEQ)[None, :]
    times = sum(((dist >= 0) & (dist % dil == 0) & (dist <= P * dil)).astype(int) for dil in (1, 4, 16))
    dist_bias = np.where(times > 0, np.log(np.maximum(times, 1)) / SCALE, NEG).astype(f)
    causal = np.where(c <= r, 0.0, NEG).astype(f)
    inv = (f(500000.0) ** (-np.arange(0, 16, 2, dtype=f) / f(16))).astype(f)
    rope = np.zeros((P, 2, TT, 32), f)
    rope[:, 0, :, 0:16] = 1.0
    for tt in range(TT):
        pos = np.full(P, PAGES * P) if tt == 0 else (tt - 1) * P + np.arange(P)
        ang = (pos.astype(f)[:, None] * inv[None, :]).astype(f).astype(np.float64)
        rope[:, 1, tt, 0:8] = rope[:, 1, tt, 8:16] = np.cos(ang)
        rope[:, 1, tt, 16:24], rope[:, 1, tt, 24:32] = -np.sin(ang), np.sin(ang)
    db = np.zeros((P, NS, 5, HEADS), f)
    mine = np.arange(P)[:, None] == np.arange(NS)[None, :]
    db[:, :, 0, :] = np.where(mine, 0.0, NEG)[:, :, None]
    db[P // 2:, :, 3, :] = NEG
    db[:, :, 4, :] = np.where(mine, np.log(3.0), NEG)[:, :, None]
    hsel = np.zeros((P, 4, HEADS), f)
    for ch in range(4):
        for half in range(2):
            hsel[half * HD:(half + 1) * HD, ch, 2 * ch + half] = 1.0
    return {"c_ident": np.eye(P, dtype=f), "c_uo": np.concatenate([tri, np.ones((P, SEQ - P), f)], 1),
            "c_ustrict": (r > c).astype(f), "c_dist": dist_bias, "c_causal": causal, "c_rope": rope,
            "c_dbias": db, "c_hsel": hsel}


def kernel(**inputs):
    import numpy as np
    import concourse.bacc as bacc
    from concourse.bass_utils import run_bass_kernel_spmd

    nc = bacc.Bacc("TRN2", target_bir_lowering=False, num_devices=1)
    arrays = {n: np.asarray(v) for n, v in inputs.items()}
    arrays["x_prompt"] = arrays["x_prompt"].reshape(SEQ, D)
    arrays["x_sample"] = arrays["x_sample"].reshape(NS, D)
    arrays["w_in_even"] = arrays["w_in_even"].reshape(D, -1)
    arrays.update(shape_constants())
    arrays = {n: np.ascontiguousarray(v) for n, v in arrays.items()}
    a = {n: nc.dram_tensor(f"in_{n}", v.shape, mybir.dt.from_np(v.dtype), kind="ExternalInput").ap() for n, v in arrays.items()}
    outs = {"y_prompt": (SEQ, D), "y_sample": (NS, D), "k_prompt": (2, SEQ, DH), "v_prompt": (2, SEQ, DH),
            "logf_prompt": (SEQ, HEADS), "k_sample": (2, NS, DH), "v_sample": (2, NS, DH), "logf_sample": (NS, HEADS),
            "cv_sample": (NS, D)}
    for n, shape in outs.items():
        a[n] = nc.dram_tensor(f"out_{n}", shape, F32, kind="ExternalOutput").ap()
    build(nc, a)
    r = run_bass_kernel_spmd(nc, [{f"in_{n}": v for n, v in arrays.items()}], core_ids=[0]).results[0]
    o = {n: r[f"out_{n}"] for n in outs}
    kvp, kvs = (1, 1, SEQ, HEADS, HD), (1, NS, 1, HEADS, HD)
    return (o["y_prompt"].reshape(1, SEQ, D), o["y_sample"].reshape(NS, 1, D),
            o["k_prompt"][0].reshape(kvp), o["v_prompt"][0].reshape(kvp), o["logf_prompt"].reshape(1, 1, SEQ, HEADS),
            o["k_prompt"][1].reshape(kvp), o["v_prompt"][1].reshape(kvp),
            o["k_sample"][0].reshape(kvs), o["v_sample"][0].reshape(kvs), o["logf_sample"].reshape(1, NS, 1, HEADS),
            o["k_sample"][1].reshape(kvs), o["v_sample"][1].reshape(kvs), o["cv_sample"].reshape(1, NS, 1, D))
```

```python
from contextlib import ExitStack

import concourse.bass as bass
from concourse import mybir

ALU = mybir.AluOpType
ACT = mybir.ActivationFunctionType
AX = mybir.AxisListType.X
F32 = mybir.dt.float32
F32R = mybir.dt.float32r
I32 = mybir.dt.int32
RMAX = bass.bass_isa.ReduceOp.max

P = 128
D = 1024
KT = D // P
SEQ = 1024
NS = 8
T = NS + SEQ
TT = 1 + SEQ // P
HEADS = 8
HD = 64
DH = HEADS * HD
FF = 2816
FT = FF // P
GF = 2
STEPS = FT // GF
PAGES = 8
N_PHYS = 80
EPS = 1e-6
SCALE = HD ** -0.5
NEG = -1e30
BLOCKS = [(0, NS + 3 * P), (NS + 3 * P, 3 * P), (NS + 6 * P, 2 * P)]
NB = len(BLOCKS)
RAW = 2
SPL = 6
IN_UNITS = 4
SLOTS = PAGES + 3
LOG = SLOTS + 2


def token_columns(tt):
    return 0 if tt == 0 else NS + (tt - 1) * P


def token_rows(tt):
    return NS if tt == 0 else P


def positive_wait(eng, sem, value):
    if not isinstance(value, int) or value > 0:
        eng.wait_ge(sem, value)


class Counted:

    def __init__(self, sem, start):
        self.sem, self.start = sem, start

    def wait(self, eng, value):
        if not isinstance(value, int) or value > 0:
            eng.wait_ge(self.sem, value + self.start)


def peeled_loop(eng, count, body):
    body(0)
    with eng.Fori(1, count) as i:
        body(i)


def build(nc, a):
    with ExitStack() as ctx:
        used = [nc.sbuf_base]
        ctx.enter_context(nc.sbuf_tensor("arena", [P, (nc.sbuf_usable_end - nc.sbuf_base) // 4 - 16], F32))

        def place(name, shape, dt=F32):
            n = 1
            for s in shape[1:]:
                n *= s
            off = (used[0] + 31) // 32 * 32
            used[0] = off + 4 * n
            assert used[0] <= nc.sbuf_usable_end, (name, used[0], nc.sbuf_usable_end)
            return nc.alloc_sbuf_tensor_at(name, shape, dt, offset=off)

        def sem(name):
            return ctx.enter_context(nc.semaphore(name))

        def sems(name, n):
            return [sem(f"{name}{j}") for j in range(n)]

        ident = place("ident", [P, P])
        ones = place("ones", [P, P])
        tri = place("tri", [P, P])
        gains = place("gains", [P, 4, KT])
        gv = place("gv", [P, KT])
        bv = place("bv", [P, KT])
        pt = place("pt", [1, NS * PAGES], I32)
        lfp_memory = used[0]
        lfp = place("lfp", [P, NS * PAGES, HEADS])
        eps = place("eps", [P, 1])
        zeros = place("zeros", [P, 1])
        xT = place("xT", [P, KT, T])
        Xh = place("Xh", [P, KT, T], F32R)
        Xl = place("Xl", [P, KT, T], F32R)
        overlay = used[0]
        raw = [place(f"raw{j}", [P, 1024]) for j in range(RAW)]
        Wh = [place(f"Wh{j}", [P, 1024], F32R) for j in range(SPL)]
        Wl = [place(f"Wl{j}", [P, 1024], F32R) for j in range(SPL)]
        stage_memory = used[0]

        BW = BLOCKS[0][1]
        sq = [place(f"sq{j}", [P, BW]) for j in range(2)]
        acc_sq = [place(f"acc_sq{j}", [P, BW]) for j in range(NB)]
        root = [place(f"root{j}", [P, BW]) for j in range(2)]
        NH = 4
        hs = [place(f"hs{j}", [P, BW]) for j in range(NH)]
        norm_end = used[0]

        NX = 4
        xs_memory = used[0]
        xs = [place(f"xs{j}", [P, D]) for j in range(NX)]
        NZ = 3
        zt = [place(f"zt{j}", [P, DH]) for j in range(NZ)]
        zsq = [place(f"zsq{j}", [P, DH]) for j in range(2)]
        ss = place("ss", [P, HEADS])
        zstd = place("zstd", [P, HEADS])
        zrs = place("zrs", [P, HEADS])
        rope_u = place("rope_u", [P, HEADS, 16])
        rope_w = place("rope_w", [P, HEADS, 16])
        gqk = place("gqk", [P, 4, HD])
        cs = place("cs", [P, 2, TT, 32])
        bf = place("bf", [P, HEADS])
        used[0] = xs_memory
        fT = place("fT", [HEADS, T])

        used[0] = norm_end
        Hh = place("Hh", [P, GF, T], F32R)
        Hl = place("Hl", [P, GF, T], F32R)
        sg = place("sg", [P, NB, BLOCKS[0][1]])
        hf = place("hf", [P, NB, BLOCKS[0][1]])

        used[0] = stage_memory
        VM = place("VM", [P, SEQ // P, D])
        vs = place("vs", [NS, D])
        ug = [place(f"ug{j}", [P, BLOCKS[0][1]]) for j in range(2)]
        wT = place("wT", [P, KT, P])
        RT = place("RT", [P, KT, P])
        vsum = place("vsum", [P, TT, 2])
        vst = place("vst", [P, 4, TT])
        w00 = place("w00", [P, KT])
        b00 = place("b00", [P, KT])
        vsT = place("vsT", [P, KT, NS])
        msT = place("msT", [P, KT, NS])
        vs2 = vs

        used[0] = overlay
        lft = place("lft", [P, TT, HEADS])
        qp = place("qp", [P, 8, P])
        kp = place("kp", [P, 8, P])
        vp = place("vp", [P, 8, P])
        QT = place("QT", [P, SEQ])
        KTr = place("KTr", [P, SEQ])
        bias = [place(f"bias{j}", [P, SEQ]) for j in range(2)]
        dist = place("dist", [P, SEQ])
        causal = place("causal", [P, P])
        score_memory = used[0]
        S2 = [place(f"S2{j}", [P, SEQ]) for j in range(2)]
        Pr = [place(f"Pr{j}", [P, SEQ]) for j in range(2)]
        PT = [place(f"PT{j}", [P, 8, P]) for j in range(2)]
        mx = place("mx", [P, 16])
        lsum = [place(f"lsum{j}", [P, 16]) for j in range(2)]
        rl = place("rl", [P, 16])
        O = [place(f"O{j}", [P, 8, P]) for j in range(2)]
        ring = place("ring", [P, SLOTS, DH])
        own = place("own", [NS, 4, DH])
        qrep = place("qrep", [P, 2, DH])
        prod = [place(f"prod{j}", [P, DH]) for j in range(2)]
        dbias = place("dbias", [P, NS, LOG, HEADS])
        L = place("L", [P, LOG, HEADS])
        hsel = place("hsel", [P, 4, HEADS])
        oS = place("oS", [P, KT, NS])
        used[0] = lfp_memory
        Lb = place("Lb", [P, LOG, HEADS])
        Lm = place("Lm", [P, 2, HEADS])
        LM = place("LM", [P, 2, HEADS])
        Lp = place("Lp", [P, LOG, HEADS])
        dl = place("dl", [P, 2, HEADS])
        drl = place("drl", [P, 2, HEADS])
        do1 = place("do1", [P, 2, 4, HEADS])
        do2 = place("do2", [P, 2, 4, HEADS])
        used[0] = score_memory
        UO = place("UO", [P, SEQ])
        cneg = place("cneg", [HEADS, SEQ])
        ustr = place("ustr", [P, P])
        lf_t = [place(f"lf_t{j}", [P, TT, HEADS]) for j in range(4)]
        lnd = place("lnd", [NS, NS, HEADS])
        acc = [place(f"acc{j}", [P, NS, HEADS]) for j in range(2)]

        ps = ctx.enter_context(nc.psum_tensor("ps", [P, 8, 512], F32))

        q_prompt = nc.dram_tensor("q_prompt", (2, SEQ, DH), F32).ap()
        q_sample = nc.dram_tensor("q_sample", (2, NS, DH), F32).ap()
        c_dram = nc.dram_tensor("c_dram", (HEADS, SEQ), F32).ap()
        qkv_prompt = [q_prompt, a["k_prompt"], a["v_prompt"]]
        qkv_sample = [q_sample, a["k_sample"], a["v_sample"]]

        const_in = sem("const_in")
        eps_set = sem("eps_set")
        x_in = sems("x_in", NX)
        xt_lo, xt_hi = sem("xt_lo"), sem("xt_hi")
        xt_act, xt_dve = sem("xt_act"), sem("xt_dve")
        raw_in = sems("raw_in", RAW)
        split_high, split_done, w_used = sem("split_high"), sem("split_done"), sem("w_used")
        zero_set = sem("zero_set")

        GU = 2 * NB * GF
        HB = NB * GF
        DN = NB * KT
        ffn_sem = {k: (sem(f"ffn_{k}"), n * STEPS) for k, n in (
            ("gu_ps", GU), ("silu", HB), ("hid", HB), ("high", HB), ("low", HB), ("dn_ps", DN), ("dn_add", DN))}
        FFN = [{k: Counted(x, n * j) for k, (x, n) in ffn_sem.items()} for j in range(2)]

        BASE_IN, BASE_FG, BASE_OUT = 0, 24, 25
        BASE_F0 = BASE_OUT + 8
        BASE_V = BASE_F0 + 6 * STEPS
        BASE_U = BASE_V + 8
        BASE_OC = BASE_U + 8
        BASE_F1 = BASE_OC + 8
        UNITS = BASE_F1 + 6 * STEPS

        def load_unit(sp, n, slot, src, shape):
            positive_wait(sp, split_done, n - RAW + 1)
            dst = raw[slot % RAW][:, :]
            if shape:
                dst = dst.rearrange("p (a b) -> p a b", a=shape)
            with nc.allow_non_contiguous_dma("512-byte and longer runs"):
                return sp.dma_start(dst, src).then_inc(raw_in[slot % RAW], 16)

        def rows(w, k0, nk, c0, nc_):
            return w[k0 * P:(k0 + nk) * P, c0:c0 + nc_].rearrange("(k p) n -> p k n", p=P)

        def load_wide(sp, base, w, col):
            for j in range(IN_UNITS):
                load_unit(sp, base + j, j + (base % SPL if isinstance(base, int) else 0), rows(w, 2 * j, 2, col, DH), 2)

        def load_narrow(sp, base, w, count):
            for m in range(count):
                load_unit(sp, base + m, base + m, rows(w, 0, KT, m * P, P), KT)

        def load_ffn(sp, base, layer):
            gu, down = a["w_gate_up"][layer], a["w_down"][layer]

            def step(i):
                for t in range(GF):
                    f = i * GF + t
                    for half in range(2):
                        n = 2 * t + half
                        src = gu[:, bass.ds(f * P + half * FF, P)].rearrange("(k p) n -> p k n", p=P)
                        load_unit(sp, base + i * 6 + n, base + n, src, KT)
                for t in range(GF):
                    n = 4 + t
                    load_unit(sp, base + i * 6 + n, base + n, down[bass.ds((i * GF + t) * P, P), :], 0)
            peeled_loop(sp, STEPS, step)

        def wait_released(eng, n):
            for f, base in ((FFN[0], BASE_F0), (FFN[1], BASE_F1)):
                if base <= n < base + 6 * STEPS:
                    ffn_released(eng, f, (n - base) // 6, (n - base) % 6)
                    return
            positive_wait(eng, w_used, n + 1 - (6 * STEPS if n >= BASE_V else 0))

        def ffn_released(eng, f, i, j):
            if j < 2 * GF:
                f["gu_ps"].wait(eng, i * GU + NB * (j + 1))
            else:
                f["dn_ps"].wait(eng, i * DN + DN)

        def split_unit(pool, n, slot, released):
            h, l, r = Wh[slot % SPL], Wl[slot % SPL], raw[slot % RAW]
            released()
            pool.wait_ge(raw_in[slot % RAW], raw_value(n, slot))
            pool.tensor_tensor(h[:, :], r[:, :], zeros[:, :].to_broadcast([P, 1024]), ALU.add).then_inc(split_high, 1)
            pool.wait_ge(split_high, n + 1)
            pool.tensor_tensor(l[:, :], r[:, :], h[:, :].bitcast(F32), ALU.subtract).then_inc(split_done, 1)

        def raw_value(n, slot):
            return (n - slot % RAW) * (16 // RAW) + 16

        def wh(n):
            return Wh[n % SPL]

        def wl(n):
            return Wl[n % SPL]

        norm_sem = {k: (sem(f"norm_{k}"), n) for k, n in (
            ("squared", NB * KT), ("summed", NB * KT), ("total", NB), ("root", NB), ("rstd", NB),
            ("scaled", NB * KT), ("high", NB * KT), ("low_dve", NB * KT // 2), ("low_pool", NB * KT // 2))}
        NORMS = [{k: Counted(x, n * j) for k, (x, n) in norm_sem.items()} for j in range(4)]

        def norm_ready(eng, s, b):
            s["low_dve"].wait(eng, KT // 2 * (b + 1))
            s["low_pool"].wait(eng, KT // 2 * (b + 1))

        def norm_square(act, s, t, b, m):
            c0, n = BLOCKS[b]
            s["summed"].wait(act, t - 1)
            act.activation(sq[t % 2][:, 0:n], xT[:, m, c0:c0 + n], ACT.Square).then_inc(s["squared"].sem, 1)

        def norm_add(pool, s, t, b, first):
            n = BLOCKS[b][1]
            s["squared"].wait(pool, t + 1)
            s["summed"].wait(pool, t)
            other = zeros[:, :].to_broadcast([P, n]) if first else acc_sq[b][:, 0:n]
            pool.tensor_tensor(acc_sq[b][:, 0:n], sq[t % 2][:, 0:n], other, ALU.add).then_inc(s["summed"].sem, 1)

        def norm_total(pe, s, b, summed):
            n = BLOCKS[b][1]
            s["summed"].wait(pe, summed)
            s["root"].wait(pe, b - 1)
            nc.tensor.matmul(ps[:, 6 + b % 2, 0:n], ones[:, :], acc_sq[b][:, 0:n], start=True,
                             stop=True).then_inc(s["total"].sem, 1)

        def norm_root(act, s, b):
            n = BLOCKS[b][1]
            s["total"].wait(act, b + 1)
            s["rstd"].wait(act, b - 1)
            act.activation(root[b % 2][:, 0:n], ps[:, 6 + b % 2, 0:n], ACT.Sqrt, bias=eps[:, 0:1],
                           scale=1.0 / D).then_inc(s["root"].sem, 1)

        def norm_rstd(dve, s, b):
            n = BLOCKS[b][1]
            s["root"].wait(dve, b + 1)
            dve.reciprocal(acc_sq[b][:, 0:n], root[b % 2][:, 0:n]).then_inc(s["rstd"].sem, 1)
            s["rstd"].wait(dve, b + 1)

        def norm_scale(dve, s, g, b, m):
            c0, n = BLOCKS[b]
            u = KT * b + m
            s["low_dve" if m % 2 == 0 else "low_pool"].wait(dve, (u - NH) // 2 + 1)
            dve.scalar_tensor_tensor(hs[u % NH][:, 0:n], xT[:, m, c0:c0 + n], gains[:, g, m:m + 1], acc_sq[b][:, 0:n],
                                     ALU.mult, ALU.mult).then_inc(s["scaled"].sem, 1)

        def norm_high(act, s, b, m):
            c0, n = BLOCKS[b]
            u = KT * b + m
            s["scaled"].wait(act, u + 1)
            act.activation(Xh[:, m, c0:c0 + n], hs[u % NH][:, 0:n], ACT.Copy).then_inc(s["high"].sem, 1)

        def norm_low(eng, s, b, m):
            c0, n = BLOCKS[b]
            u = KT * b + m
            s["high"].wait(eng, u + 1)
            eng.tensor_tensor(Xl[:, m, c0:c0 + n], hs[u % NH][:, 0:n], Xh[:, m, c0:c0 + n].bitcast(F32),
                              ALU.subtract).then_inc(s["low_dve" if m % 2 == 0 else "low_pool"].sem, 1)

        def norm_apply_dve(dve, s, g, b, between=None):
            norm_rstd(dve, s, b)
            for m in range(KT):
                if between:
                    between(m)
                norm_scale(dve, s, g, b, m)
                if m >= 2 and m % 2 == 0:
                    norm_low(dve, s, b, m - 2)
            norm_low(dve, s, b, KT - 2)

        def norm_apply_act(act, s, b, between=None):
            for m in range(KT):
                if between:
                    between(m)
                norm_high(act, s, b, m)

        def norm_apply_pool(pool, s, b):
            for m in range(1, KT, 2):
                norm_low(pool, s, b, m)

        def chain(out, pairs, last=None):
            for j, (w, x) in enumerate(pairs):
                ins = nc.tensor.matmul(out, w, x, start=(j == 0), stop=(j == len(pairs) - 1))
            return ins

        def split_products(w_high, w_low, x_high, x_low):
            return [(w_high, x_high), (w_high, x_low), (w_low, x_high)]

        def unit_products(n, c0, w):
            return [pr for k in range(KT)
                    for pr in split_products(Wh[n % SPL][:, k * P:(k + 1) * P], Wl[n % SPL][:, k * P:(k + 1) * P],
                                             Xh[:, k, c0:c0 + w], Xl[:, k, c0:c0 + w])]

        z_ps, z_free, z_squared, z_sum, z_root, z_rs, z_scaled, z_gain, z_rope1, z_done = (
            sem(n) for n in ("z_ps", "z_free", "z_squared", "z_sum", "z_root", "z_rs", "z_scaled", "z_gain", "z_rope1", "z_done"))
        z_out = sems("z_out", NZ)
        bf_in, f_ps, f_out, ft_ps = sem("bf_in"), sem("f_ps"), sem("f_out"), sem("ft_ps")
        ZB = 3
        NZT = 3 * TT

        def wide_products(pe, n0, s0, w_base, c, tt, q, x_ready):
            t0 = token_columns(tt)
            out = ps[:, q % ZB, :]
            for k in range(KT):
                if tt == 0 and k % 2 == 0:
                    pe.wait_ge(split_done, n0 + k // 2 + 1)
                h = Wh[(s0 + k // 2) % SPL][:, (k % 2) * DH:(k % 2 + 1) * DH]
                l = Wl[(s0 + k // 2) % SPL][:, (k % 2) * DH:(k % 2 + 1) * DH]
                xh, xl = Xh[:, k, t0:t0 + P], Xl[:, k, t0:t0 + P]
                nc.tensor.matmul(out, xh, h, start=(k == 0), stop=False)
                nc.tensor.matmul(out, xh, l, start=False, stop=False)
                last = nc.tensor.matmul(out, xl, h, start=False, stop=(k == KT - 1))
                if tt == TT - 1 and k % 2 == 1 and k < KT - 1:
                    last.then_inc(w_used, 1)
            return last

        wd_ps = {}

        def in_pe(pe):
            def step(i):
                for c in range(3):
                    for tt in range(TT):
                        q = c * TT + tt
                        if isinstance(i, int) and c == 0 and tt in (0, 4, 7):
                            norm_ready(pe, NORMS[0], (tt >= 4) + (tt >= 7))
                        positive_wait(pe, z_free, i * NZT + q - ZB + 1)
                        last = wide_products(pe, i * 12 + 4 * c, 4 * c, None, c, tt, q, None)
                        last.then_inc(z_ps, 1)
                    pe.wait_ge(z_ps, i * NZT + (c + 1) * TT)
                    pe.sem_inc(w_used, 1)
            peeled_loop(pe, 2, step)
            pe.wait_ge(split_done, BASE_FG + 1)
            for b, (c0, w) in enumerate(BLOCKS):
                last = chain(ps[:, 3 + b, 0:w], unit_products(BASE_FG, c0, w))
                last.then_inc(f_ps, 1)
            pe.wait_ge(f_ps, NB)
            pe.sem_inc(w_used, 1)
            pe.wait_ge(f_out, NB)
            for tt in range(TT):
                t0 = token_columns(tt)
                last = nc.tensor.transpose(ps[:, 6, tt * HEADS:(tt + 1) * HEADS], fT[:, t0:t0 + P], ident[0:HEADS, 0:HEADS])
            last.then_inc(ft_ps, 1)

        def in_store(act, i, c, tt, q):
            r = token_rows(tt)
            dst = qkv_sample[c][i] if tt == 0 else qkv_prompt[c][i, (tt - 1) * P:tt * P, :]
            act.wait_ge(z_done, i * NZT + q + 1)
            act.dma_start(dst, zt[q % NZ][0:r, :]).then_inc(z_out[q % NZ], 16)

        def in_act(act):
            def step(i):
                for c in range(3):
                    for tt in range(TT):
                        q, r = c * TT + tt, token_rows(tt)
                        if c < 2:
                            n = i * 2 * TT + q
                            act.wait_ge(z_ps, i * NZT + q + 1)
                            positive_wait(act, z_sum, n - 1)
                            act.activation(zsq[q % 2][0:r, :], ps[0:r, q % ZB, :], ACT.Square).then_inc(z_squared, 1)
                        if q > 0:
                            in_store(act, i, (q - 1) // TT, (q - 1) % TT, q - 1)
                        if c < 2:
                            act.wait_ge(z_sum, n + 1)
                            positive_wait(act, z_rs, n)
                            act.activation(zstd[0:r, :], ss[0:r, :], ACT.Sqrt, bias=eps[0:r, 0:1],
                                           scale=1.0 / HD).then_inc(z_root, 1)
                in_store(act, i, 2, TT - 1, NZT - 1)
            peeled_loop(act, 2, step)

        def in_dve(dve):
            def step(i):
                for c in range(3):
                    for tt in range(TT):
                        q, r = c * TT + tt, token_rows(tt)
                        z, n = zt[q % NZ], i * 2 * TT + q
                        z3 = z[0:r, :].rearrange("p (h e) -> p h e", h=HEADS)
                        p3 = ps[0:r, q % ZB, :].rearrange("p (h e) -> p h e", h=HEADS)
                        if c == 2:
                            positive_wait(dve, z_out[q % NZ], (i * (NZT // NZ) + q // NZ) * 16)
                            dve.wait_ge(z_ps, i * NZT + q + 1)
                            dve.tensor_scalar(z[0:r, :], ps[0:r, q % ZB, :], 1.0, None, ALU.mult).then_inc(z_free, 1)
                            dve.wait_ge(z_free, i * NZT + q + 1)
                            dve.tensor_scalar(ss[0:1, 0:1], z[0:1, 0:1], 1.0, None, ALU.mult).then_inc(z_done, 1)
                            continue
                        dve.wait_ge(z_squared, n + 1)
                        positive_wait(dve, z_root, n)
                        dve.tensor_reduce(ss[0:r, :], zsq[q % 2][0:r, :].rearrange("p (h e) -> p h e", h=HEADS), AX,
                                          ALU.add).then_inc(z_sum, 1)
                        dve.wait_ge(z_root, n + 1)
                        dve.reciprocal(zrs[0:r, :], zstd[0:r, :]).then_inc(z_rs, 1)
                        positive_wait(dve, z_out[q % NZ], (i * (NZT // NZ) + q // NZ) * 16)
                        dve.wait_ge(z_rs, n + 1)
                        dve.tensor_tensor(z3, p3, zrs[0:r, :].unsqueeze(2).to_broadcast([r, HEADS, HD]),
                                          ALU.mult).then_inc(z_free, 1)
                        dve.wait_ge(z_free, i * NZT + q + 1)
                        dve.tensor_tensor(z3, z3, gqk[0:r, bass.ds(2 * i + c, 1), :].to_broadcast([r, HEADS, HD]),
                                          ALU.mult).then_inc(z_gain, 1)
                        dve.wait_ge(z_gain, n + 1)
                        C = cs[0:r, bass.ds(i, 1), tt, 0:16].to_broadcast([r, HEADS, 16])
                        S1 = cs[0:r, bass.ds(i, 1), tt, 16:24].to_broadcast([r, HEADS, 8])
                        S2_ = cs[0:r, bass.ds(i, 1), tt, 24:32].to_broadcast([r, HEADS, 8])
                        dve.tensor_tensor(rope_u[0:r], z3[:, :, 0:16], C, ALU.mult)
                        dve.tensor_tensor(rope_w[0:r, :, 0:8], z3[:, :, 8:16], S1, ALU.mult)
                        dve.tensor_tensor(rope_w[0:r, :, 8:16], z3[:, :, 0:8], S2_, ALU.mult).then_inc(z_rope1, 1)
                        dve.wait_ge(z_rope1, n + 1)
                        dve.tensor_tensor(z3[:, :, 0:16], rope_u[0:r], rope_w[0:r], ALU.add).then_inc(z_done, 1)
            peeled_loop(dve, 2, step)

        lg, lg_a = sem("lg"), sem("lg_a")
        lf_out, c_ps, c_out, c_in = sem("lf_out"), sem("c_ps"), sem("c_out"), sem("c_in")
        att_const_in, page_in, lfp_in, db_ps, db = sem("att_const_in"), sem("page_in"), sem("lfp_in"), sem("db_ps"), sem("db")
        q_in, k_in, v_in, own_in, qrep_in = sem("q_in"), sem("k_in"), sem("v_in"), sem("own_in"), sem("qrep_in")
        bias_in = sems("bias_in", 2)
        ring_in = sems("ring_in", SLOTS)

        def forget_dve(dve):
            count = [0]

            def done(ins):
                count[0] += 1
                ins.then_inc(lg, 1)
                return count[0]
            for b, (c0, w) in enumerate(BLOCKS):
                dve.wait_ge(f_ps, b + 1)
                dve.tensor_copy(fT[:, c0:c0 + w], ps[0:HEADS, 3 + b, 0:w]).then_inc(f_out, 1)
            dve.wait_ge(bf_in, 16)
            dve.wait_ge(ft_ps, 1)
            z = ps[:, 6, 0:TT * HEADS].rearrange("p (t h) -> p t h", t=TT)
            n = done(dve.tensor_tensor(lf_t[0][:, :, :], z, bf[:, :].unsqueeze(1).to_broadcast([P, TT, HEADS]), ALU.add))
            dve.wait_ge(lg, n)
            n = done(dve.scalar_tensor_tensor(lf_t[1][:, :, :], lf_t[0][:, :, :], -1.0, lf_t[0][:, :, :], ALU.mult, ALU.max))
            dve.wait_ge(lg_a, 2)
            n = done(dve.scalar_tensor_tensor(lft[:, :, :], lf_t[0][:, :, :], 0.0, lf_t[3][:, :, :], ALU.min, ALU.subtract))
            dve.wait_ge(c_ps, 1)
            n = done(dve.tensor_scalar(cneg[:, :], ps[0:HEADS, 0:2, :].rearrange("p a b -> p (a b)"), -1.0 / SCALE, None, ALU.mult))
            dve.wait_ge(att_const_in, ATT_CONSTS * 16)
            n = done(dve.tensor_tensor(lnd[:, :, :], lft[0:NS, 0, :].unsqueeze(1).to_broadcast([NS, NS, HEADS]),
                                       ident[0:NS, 0:NS].unsqueeze(2).to_broadcast([NS, NS, HEADS]), ALU.mult))
            dve.memset(L[:, :, :], 0.0)
            dve.wait_ge(db_ps, 1)
            inner = ps[:, 2, :].rearrange("p (s g h) -> p s g h", s=NS, g=PAGES)
            total = ps[:, 3, :].rearrange("p (s g h) -> p s g h", s=NS, g=PAGES)
            n = done(dve.tensor_scalar(acc[0][:, :, :], ps[:, 4, 0:NS * HEADS].rearrange("p (s h) -> p s h", s=NS),
                                       1.0, None, ALU.mult))
            for j, g in enumerate(reversed(range(PAGES))):
                dve.wait_ge(lg, n)
                dve.tensor_tensor(dbias[:, :, g, :], inner[:, :, g, :], acc[j % 2][:, :, :], ALU.add)
                n = done(dve.tensor_tensor(acc[(j + 1) % 2][:, :, :], total[:, :, g, :], acc[j % 2][:, :, :], ALU.add))
            dve.wait_ge(lg, n)

        def forget_act(act):
            act.wait_ge(lg, 2)
            act.activation(lf_t[2][:, :, :], lf_t[1][:, :, :], ACT.Exp, scale=-1.0).then_inc(lg_a, 1)
            act.wait_ge(lg_a, 1)
            act.activation(lf_t[3][:, :, :], lf_t[2][:, :, :], ACT.Ln, bias=1.0).then_inc(lg_a, 1)

        def forget_pe(pe):
            pe.wait_ge(lg, 3)
            pe.wait_ge(att_const_in, ATT_CONSTS * 16)
            for half in range(2):
                lo, hi = half * 512, (half + 1) * 512
                tiles = [t for t in range(8) if t * P < hi]
                for t in tiles:
                    c0 = max(lo, t * P)
                    last = nc.tensor.matmul(ps[0:HEADS, half, c0 - lo:512], lft[:, t + 1, :],
                                            UO[:, c0 - t * P:hi - t * P], start=(t == 0), stop=(t == tiles[-1]))
            last.then_inc(c_ps, 1)
            pe.wait_ge(lfp_in, 16 * NS * PAGES)
            flat = lfp[:, :, :].rearrange("p g h -> p (g h)")
            nc.tensor.matmul(ps[:, 2, :], ustr[:, :], flat, start=True, stop=True)
            nc.tensor.matmul(ps[:, 3, :], ones[:, :], flat, start=True, stop=True)
            pe.wait_ge(lg, 5)
            nc.tensor.matmul(ps[:, 4, 0:NS * HEADS], ones[0:NS, :], lnd[:, :, :].rearrange("p s h -> p (s h)"),
                             start=True, stop=True).then_inc(db_ps, 1)

        ATT_CONSTS = 6

        def pages_sp(sp):
            sp.dma_start(pt[:, :], a["page_table"].rearrange("s g -> (s g)").rearrange("(o n) -> o n", o=1)).then_inc(page_in, 16)
            sp.wait_ge(page_in, 16)
            with nc.allow_non_contiguous_dma("eight values a token"):
                with sp.Fori(0, NS * PAGES) as g:
                    page = sp.value_load(pt[0:1, bass.ds(g, 1)], min_val=0, max_val=N_PHYS - 1)
                    sp.dma_start(lfp[:, bass.ds(g, 1), :], a["cache_a_logf"][0, bass.ds(page, 1)].rearrange("o t h -> t o h")).then_inc(lfp_in, 16)

        def forget_sp(sp):
            sp.wait_ge(ft_ps, 1)
            for j in range(NZ):
                sp.wait_ge(z_out[j], 16 * 2 * NZT // NZ)
            for dst, src in ((UO, "c_uo"), (ustr, "c_ustrict"), (dist, "c_dist"), (causal, "c_causal"), (hsel, "c_hsel")):
                sp.dma_start(dst[...] if False else dst[:], a[src]).then_inc(att_const_in, 16)
            sp.dma_start(dbias[:, :, SLOTS - 3:LOG, :], a["c_dbias"]).then_inc(att_const_in, 16)
            with nc.allow_non_contiguous_dma("rows of a head group"):
                for j, src in enumerate((a["k_sample"][0], a["v_sample"][0], a["k_sample"][1], a["v_sample"][1])):
                    sp.dma_start(own[:, j, :], src).then_inc(own_in, 16)
            sp.wait_ge(lg, 3)
            with nc.allow_non_contiguous_dma("eight values a token"):
                sp.dma_start(a["logf_prompt"].rearrange("(t p) h -> p t h", p=P), lft[:, 1:TT, :]).then_inc(lf_out, 16)
                sp.dma_start(a["logf_sample"], lft[0:NS, 0, :]).then_inc(lf_out, 16)
            sp.wait_ge(lg, 4)
            sp.dma_start(c_dram, cneg[:, :]).then_inc(c_out, 16)
            sp.wait_ge(c_out, 16)

        s_ps, s_biased, p_done, pt_ps, pt_out, pv_ps, o_out, o_norm, rl_done = (
            sem(n) for n in ("s_ps", "s_biased", "p_done", "pt_ps", "pt_out", "pv_ps", "o_out", "o_norm", "rl_done"))
        qk_ps, qk_act, qk_dve, masked, ot_ps, ot_high, ot_low = (
            sem(n) for n in ("qk_ps", "qk_act", "qk_dve", "masked", "ot_ps", "ot_high", "ot_low"))
        prod_done, log_done, dch, ar_done, dp_done, dsum_ps, dpv_ps, osamp = (
            sem(n) for n in ("prod_done", "log_done", "dch", "ar_done", "dp_done", "dsum_ps", "dpv_ps", "osamp"))
        v_in2 = sem("v_in2")
        PAIRS = 8
        HSTEPS = 8
        STEP = [(hh, qt) for hh in range(2) for qt in reversed(range(HSTEPS))]
        NSTEP = 16 * PAIRS
        DCH = 10
        LOG_AT = {4: (0, 1), 5: (2, 3), 6: (4, 5), 7: (6, 7), 8: (8,), 9: (9,), 10: (10,), 11: (11, 12)}
        QK_BANKS = (1, 3, 5, 7)
        halves = [0]
        for s_ in range(NSTEP):
            halves.append(halves[-1] + STEP[s_ % 16][1] // 4 + 1)

        def att_sp(sp):
            for it in range(PAIRS):
                grp, j = it // 4, it % 4
                cols = slice(j * P, (j + 1) * P)
                v_src = a["v_prompt"][grp, :, cols].rearrange("(t p) e -> p t e", p=P)
                with nc.allow_non_contiguous_dma("512-byte runs"):
                    positive_wait(sp, qk_ps, 4 * it)
                    sp.dma_start(qp[:, :, :], q_prompt[grp, :, cols].rearrange("(t p) e -> p t e", p=P)).then_inc(q_in, 16)
                    sp.dma_start(kp[:, :, :], a["k_prompt"][grp, :, cols].rearrange("(t p) e -> p t e", p=P)).then_inc(k_in, 16)
                    if grp == 0:
                        positive_wait(sp, s_biased, 16 * (it - 1) + 8)
                        sp.dma_start(bias[0][:, :], c_dram[2 * j, :].partition_broadcast(P)).then_inc(bias_in[0], 16)
                    positive_wait(sp, pv_ps, 16 * (it - 1) + 12)
                    sp.dma_start(vp[:, 4:8, :], v_src[:, 4:8, :]).then_inc(v_in2, 16)
                    positive_wait(sp, pv_ps, 16 * it)
                    sp.dma_start(vp[:, 0:4, :], v_src[:, 0:4, :]).then_inc(v_in, 16)
                    if grp == 0:
                        positive_wait(sp, s_biased, 16 * it)
                        sp.dma_start(bias[1][:, :], c_dram[2 * j + 1, :].partition_broadcast(P)).then_inc(bias_in[1], 16)
                    positive_wait(sp, prod_done, LOG * it)
                    for g in range(2):
                        sp.dma_start(qrep[:, g, :], q_sample[g, it, :].partition_broadcast(P)).then_inc(qrep_in, 16)
                    for kind in range(2):
                        cache = a["cache_a_k"] if kind == 0 else a["cache_a_v"]
                        state = a["state_b_k"] if kind == 0 else a["state_b_v"]
                        for slot in range(SLOTS):
                            if kind == 0:
                                positive_wait(sp, dpv_ps, it)
                            else:
                                sp.wait_ge(prod_done, LOG * it + slot + 1 + (slot >= PAGES))
                            if slot < PAGES:
                                page = sp.value_load(pt[0:1, it * PAGES + slot:it * PAGES + slot + 1], min_val=0, max_val=N_PHYS - 1)
                                src = cache[0, bass.ds(page, 1)].rearrange("o t h e -> t (o h e)")
                                sp.dma_start(ring[:, slot, :], src).then_inc(ring_in[slot], 16)
                            else:
                                dil = 4 ** (slot - PAGES)
                                r = min(P, PAGES * P // dil)
                                t0 = PAGES * P - r * dil
                                src = state[0, it, t0:PAGES * P, :, :].rearrange("(r d) h e -> r d (h e)", d=dil)[:, 0, :]
                                sp.dma_start(ring[0:r, slot, :], src).then_inc(ring_in[slot], 16)

        def log_slot(j):
            if j < PAGES:
                return P, 0, ring[:, j, :], j
            if j == PAGES:
                return NS, 0, own[0:NS, 0, :], None
            if j < LOG - 1:
                r = min(P, PAGES * P // 4 ** (j - PAGES - 1))
                return r, 1, ring[0:r, j - 1, :], j - 1
            return NS, 1, own[0:NS, 2, :], None

        def value_tile(j, c):
            r, g, _, slot = log_slot(j)
            if slot is None:
                return own[0:NS, 2 * g + 1, c * P:(c + 1) * P]
            return ring[0:r, slot, c * P:(c + 1) * P]

        def att_pool(pool):
            for it in range(PAIRS):
                pool.wait_ge(qrep_in, 32 * (it + 1))
                if it == 0:
                    pool.wait_ge(own_in, 64)
                for j in range(LOG):
                    r, g, keys, slot = log_slot(j)
                    n = LOG * it + j
                    if slot is not None:
                        pool.wait_ge(ring_in[slot], 32 * it + 16)
                    positive_wait(pool, log_done, n - 1)
                    pool.tensor_tensor(prod[n % 2][0:r, :], keys, qrep[0:r, g, :], ALU.mult).then_inc(prod_done, 1)
                pool.wait_ge(dch, DCH * it + 3)
                pool.partition_all_reduce(LM[:, :, :].rearrange("p g h -> p (g h)"), Lm[:, :, :].rearrange("p g h -> p (g h)"),
                                          P, RMAX).then_inc(ar_done, 1)

        def s_banks(s):
            return ps[:, 2 * (s % 2):2 * (s % 2) + 2, :].rearrange("p a b -> p (a b)")

        def att_pe(pe):
            def transpose_qk(it):
                for src, landed in ((qp, q_in), (kp, k_in)):
                    pe.wait_ge(landed, 16 * (it + 1))
                    for g in range(2):
                        n = 2 * (src is kp) + g
                        bank = QK_BANKS[n]
                        if bank < 4:
                            positive_wait(pe, s_biased, 16 * (it - 1) + 12)
                        elif bank == 5:
                            positive_wait(pe, pt_out, halves[16 * (it - 1) + 12] if it else 0)
                        else:
                            positive_wait(pe, ot_low, 2 * (it - 1))
                            positive_wait(pe, osamp, it - 1)
                        for b in range(4):
                            last = nc.tensor.transpose(ps[:, bank, b * P:(b + 1) * P], src[:, 4 * g + b, :], ident[:, :])
                        last.then_inc(qk_ps, 1)

            def scores(s):
                it, k = divmod(s, 16)
                hh, qt = STEP[k]
                n = P * (qt + 1)
                if k == 0:
                    pe.wait_ge(qk_act, 2 * (it + 1))
                    pe.wait_ge(qk_dve, 2 * (it + 1))
                positive_wait(pe, s_biased, s - 1)
                out = s_banks(s)
                hp = slice(hh * HD, (hh + 1) * HD)
                for c0 in range(0, n, 512):
                    c1 = min(n, c0 + 512)
                    last = nc.tensor.matmul(out[:, c0:c1], QT[hp, qt * P:(qt + 1) * P], KTr[hp, c0:c1], start=True, stop=True)
                last.then_inc(s_ps, 1)

            def transpose_numerators(s):
                qt = STEP[s % 16][1]
                pe.wait_ge(p_done, s + 1)
                for g in range(qt // 4 + 1):
                    positive_wait(pe, pt_out, halves[s])
                    for b in range(4 * g, min(qt + 1, 4 * g + 4)):
                        last = nc.tensor.transpose(ps[:, 4 + g, (b % 4) * P:(b % 4 + 1) * P], Pr[s % 2][:, b * P:(b + 1) * P], ident[:, :])
                    last.then_inc(pt_ps, 1)

            def weigh(s):
                it, k = divmod(s, 16)
                hh, qt = STEP[k]
                if k == 0:
                    pe.wait_ge(v_in, 16 * (it + 1))
                    pe.wait_ge(v_in2, 16 * (it + 1))
                positive_wait(pe, o_out, s)
                pe.wait_ge(pt_out, halves[s + 1])
                for b in range(qt + 1):
                    last = nc.tensor.matmul(ps[:, 6, 0:HD], PT[s % 2][:, b, :], vp[:, b, hh * HD:(hh + 1) * HD],
                                            start=(b == 0), stop=(b == qt))
                last.then_inc(pv_ps, 1)

            def transpose_out(it, g):
                pe.wait_ge(o_norm, 2 * (it + 1))
                positive_wait(pe, ot_low, 2 * it + g)
                pe.wait_ge(osamp, it + 1)
                for b in range(4):
                    last = nc.tensor.transpose(ps[:, 7, b * P:(b + 1) * P], O[it % 2][:, 4 * g + b, :], ident[:, :])
                last.then_inc(ot_ps, 1)

            def sample(it):
                pe.wait_ge(dp_done, it + 1)
                pe.wait_ge(ot_low, 2 * it) if it else None
                flat = Lp[:, :, :].rearrange("p j h -> p (j h)")
                nc.tensor.matmul(ps[:, 7, 0:LOG * HEADS], ones[:, :], flat, start=True, stop=True).then_inc(dsum_ps, 1)
                for slot in range(SLOTS):
                    pe.wait_ge(ring_in[slot], 32 * (it + 1))
                for g, tiles in ((0, range(PAGES + 1)), (1, range(PAGES + 1, LOG))):
                    for c in range(4):
                        o0 = 256 + (4 * g + c) * HEADS
                        last = chain(ps[:, 7, o0:o0 + HEADS], [(value_tile(j, c), Lp[0:log_slot(j)[0], j, :]) for j in tiles])
                last.then_inc(dpv_ps, 1)

            transpose_qk(0)
            scores(0)
            scores(1)
            transpose_numerators(0)
            for s in range(NSTEP):
                it, k = divmod(s, 16)
                new_pair = k == 14 and it < PAIRS - 1
                if new_pair:
                    transpose_qk(it + 1)
                elif s + 2 < NSTEP:
                    scores(s + 2)
                if s + 1 < NSTEP:
                    transpose_numerators(s + 1)
                weigh(s)
                if new_pair:
                    scores(s + 2)
                if it and k == 0:
                    sample(it - 1)
                if it and k in (4, 6):
                    transpose_out(it - 1, k // 2 - 2)
            sample(PAIRS - 1)
            for g in range(2):
                transpose_out(PAIRS - 1, g)

        def att_act(act):
            def numerators(s):
                it, k = divmod(s, 16)
                hh, qt = STEP[k]
                n = P * (qt + 1)
                act.wait_ge(s_biased, s + 1)
                positive_wait(act, pt_ps, halves[max(s - 1, 0)])
                if k == 0:
                    positive_wait(act, o_norm, 2 * (it - 1))
                col = hh * 8 + qt
                act.activation(Pr[s % 2][:, 0:n], S2[s % 2][:, 0:n], ACT.Exp, bias=mx[:, k:k + 1], scale=-1.0,
                               accum_out=lsum[it % 2][:, col:col + 1]).then_inc(p_done, 1)

            def copy_numerators(s):
                qt = STEP[s % 16][1]
                for g in range(qt // 4 + 1):
                    act.wait_ge(pt_ps, halves[s] + g + 1)
                    positive_wait(act, pv_ps, s - 1)
                    n = min(4, qt + 1 - 4 * g)
                    act.activation(PT[s % 2][:, 4 * g:4 * g + n, :].rearrange("p b q -> p (b q)"), ps[:, 4 + g, 0:n * P],
                                   ACT.Copy).then_inc(pt_out, 1)

            def copy_out(s):
                it, k = divmod(s, 16)
                hh, qt = STEP[k]
                act.wait_ge(pv_ps, s + 1)
                if k == 0:
                    positive_wait(act, ot_ps, 2 * (it - 1))
                act.activation(O[it % 2][:, qt, hh * HD:(hh + 1) * HD], ps[:, 6, 0:HD], ACT.Copy).then_inc(o_out, 1)

            def copy_queries(it):
                for g in range(2):
                    act.wait_ge(qk_ps, 4 * it + g + 1)
                    act.activation(QT[:, 512 * g:512 * (g + 1)], ps[:, QK_BANKS[g], :], ACT.Copy).then_inc(qk_act, 1)

            copy_queries(0)
            numerators(0)
            numerators(1)
            for s in range(NSTEP):
                it, k = divmod(s, 16)
                copy_numerators(s)
                if s > 0:
                    copy_out(s - 1)
                if k == 14 and it < PAIRS - 1:
                    copy_queries(it + 1)
                if s + 2 < NSTEP:
                    numerators(s + 2)
                if k == 13:
                    act.wait_ge(dch, DCH * it + 5)
                    positive_wait(act, dpv_ps, it)
                    act.activation(Lp[:, :, :], Lb[:, :, :], ACT.Exp).then_inc(dp_done, 1)
            copy_out(NSTEP - 1)

        def att_dve(dve):
            def step(ins):
                ins.then_inc(dch, 1)

            def log_sum(it, j):
                n = LOG * it + j
                r = log_slot(j)[0]
                dve.wait_ge(prod_done, n + 1)
                dve.tensor_reduce(L[0:r, j, :], prod[n % 2][0:r, :].rearrange("p (h e) -> p h e", h=HEADS), AX,
                                  ALU.add).then_inc(log_done, 1)

            def copy_keys(it):
                for g in range(2):
                    dve.wait_ge(qk_ps, 4 * it + 2 + g + 1)
                    dve.tensor_copy(KTr[:, 512 * g:512 * (g + 1)], ps[:, QK_BANKS[2 + g], :]).then_inc(qk_dve, 1)

            def normalise(it, hh):
                o = O[it % 2][:, :, hh * HD:(hh + 1) * HD]
                r = rl[:, 8 * hh:8 * hh + 8]
                dve.wait_ge(o_out, 16 * it + 8 * (hh + 1))
                dve.reciprocal(r, lsum[it % 2][:, 8 * hh:8 * hh + 8]).then_inc(rl_done, 1)
                dve.wait_ge(rl_done, 2 * it + hh + 1)
                dve.tensor_tensor(o, o, r.unsqueeze(2).to_broadcast([P, 8, HD]), ALU.mult).then_inc(o_norm, 1)

            def out_split(it, g):
                c0 = NS + 512 * g
                dve.wait_ge(ot_ps, 2 * it + g + 1)
                dve.tensor_copy(Xh[:, it, c0:c0 + 512], ps[:, 7, :]).then_inc(ot_high, 1)
                dve.wait_ge(ot_high, 2 * it + g + 1)
                dve.tensor_tensor(Xl[:, it, c0:c0 + 512], ps[:, 7, :], Xh[:, it, c0:c0 + 512].bitcast(F32),
                                  ALU.subtract).then_inc(ot_low, 1)

            def sample_max(it):
                n = DCH * it
                dve.wait_ge(log_done, LOG * (it + 1))
                positive_wait(dve, dp_done, it)
                step(dve.scalar_tensor_tensor(Lb[:, :, :], L[:, :, :], SCALE, dbias[:, it, :, :], ALU.mult, ALU.add))
                dve.wait_ge(dch, n + 1)
                step(dve.tensor_reduce(Lm[:, 0, :], Lb[:, 0:PAGES + 1, :].rearrange("p j h -> p h j"), AX, ALU.max))
                step(dve.tensor_reduce(Lm[:, 1, :], Lb[:, PAGES + 1:LOG, :].rearrange("p j h -> p h j"), AX, ALU.max))

            def sample_shift(it):
                dve.wait_ge(ar_done, it + 1)
                step(dve.tensor_tensor(Lb[:, 0:PAGES + 1, :], Lb[:, 0:PAGES + 1, :],
                                       LM[:, 0:1, :].to_broadcast([P, PAGES + 1, HEADS]), ALU.subtract))
                step(dve.tensor_tensor(Lb[:, PAGES + 1:LOG, :], Lb[:, PAGES + 1:LOG, :],
                                       LM[:, 1:2, :].to_broadcast([P, 4, HEADS]), ALU.subtract))

            def sample_out(it):
                n = DCH * it
                dve.wait_ge(dpv_ps, it + 1)
                sums = ps[:, 7, 0:LOG * HEADS].rearrange("p (j h) -> p h j", j=LOG)
                step(dve.tensor_reduce(dl[:, 0, :], sums[:, :, 0:PAGES + 1], AX, ALU.add))
                step(dve.tensor_reduce(dl[:, 1, :], sums[:, :, PAGES + 1:LOG], AX, ALU.add))
                dve.wait_ge(dch, n + 7)
                step(dve.reciprocal(drl[:, :, :], dl[:, :, :]))
                dve.wait_ge(dch, n + 8)
                mine = ps[:, 7, 256:256 + 8 * HEADS].rearrange("p (g c h) -> p g c h", g=2, c=4)
                step(dve.tensor_tensor(do1[:, :, :, :], mine, drl[:, :, :].unsqueeze(2).to_broadcast([P, 2, 4, HEADS]), ALU.mult))
                dve.wait_ge(dch, n + 9)
                step(dve.tensor_tensor(do2[:, :, :, :], do1[:, :, :, :], hsel[:, :, :].unsqueeze(1).to_broadcast([P, 2, 4, HEADS]), ALU.mult))
                dve.wait_ge(dch, n + 10)
                dve.tensor_reduce(oS[:, :, it], do2[:, :, :, :].rearrange("p g c h -> p (g c) h"), AX, ALU.add).then_inc(osamp, 1)

            copy_keys(0)
            for s in range(NSTEP):
                it, k = divmod(s, 16)
                hh, qt = STEP[k]
                n = P * (qt + 1)
                if it // 4 == 0:
                    b = bias[hh]
                    if k % 8 == 0:
                        dve.wait_ge(bias_in[hh], 16 * (it + 1))
                    d = b[:, qt * P:(qt + 1) * P]
                    positive_wait(dve, s_biased, s)
                    dve.tensor_tensor(d, d, causal[:, :], ALU.add).then_inc(masked, 1)
                    dve.wait_ge(masked, s + 1)
                    row = b[:, 0:n]
                else:
                    row = dist[:, SEQ - n:SEQ]
                dve.wait_ge(s_ps, s + 1)
                positive_wait(dve, p_done, s - 1)
                dve.tensor_tensor_reduce(S2[s % 2][:, 0:n], s_banks(s)[:, 0:n], row, -SCALE, -NEG, ALU.add, ALU.min,
                                         accum_out=mx[:, k:k + 1]).then_inc(s_biased, 1)
                if k == 15 and it < PAIRS - 1:
                    copy_keys(it + 1)
                for j in LOG_AT.get(k, ()):
                    log_sum(it, j)
                if it and k == 2:
                    normalise(it - 1, 1)
                if it and k == 3:
                    sample_out(it - 1)
                if it and k in (6, 8):
                    out_split(it - 1, k // 2 - 3)
                if k == 11:
                    normalise(it, 0)
                if k == 12:
                    sample_max(it)
                if k == 13:
                    sample_shift(it)
            normalise(PAIRS - 1, 1)
            sample_out(PAIRS - 1)
            for g in range(2):
                out_split(PAIRS - 1, g)
            dve.wait_ge(osamp, PAIRS)
            dve.tensor_copy(Xh[:, :, 0:NS], oS[:, :, :]).then_inc(osamp, 1)
            dve.wait_ge(osamp, PAIRS + 1)
            dve.tensor_tensor(Xl[:, :, 0:NS], oS[:, :, :], Xh[:, :, 0:NS].bitcast(F32), ALU.subtract).then_inc(osamp, 1)
        ATT_DONE = (osamp, PAIRS + 2)

        def narrow_pe(pe, base, ps_done, ps_free, norm):
            for m in range(KT):
                n = base + m
                pe.wait_ge(split_done, n + 1)
                for b, (c0, w) in enumerate(BLOCKS):
                    j = NB * m + b
                    positive_wait(pe, ps_free, j - 5)
                    last = chain(ps[:, j % 6, 0:w], unit_products(n, c0, w))
                    last.then_inc(ps_done, 1)
                    if m == KT - 1 and b > 0:
                        norm_total(pe, norm, b - 1, NB * m + b)
                pe.wait_ge(ps_done, NB * (m + 1))
                pe.sem_inc(w_used, 1)
            norm_total(pe, norm, NB - 1, NB * KT)

        ORDER_NARROW = [(b, m) for m in range(KT) for b in range(NB)]

        def residual_dve(dve, ps_done, ps_free, norm, g):
            for j, (b, m) in enumerate(ORDER_NARROW):
                c0, w = BLOCKS[b]
                dve.wait_ge(ps_done, j + 1)
                x = xT[:, m, c0:c0 + w]
                dve.tensor_tensor(x, ps[:, j % 6, 0:w], x, ALU.add).then_inc(ps_free, 1)
            for b in range(NB):
                norm_apply_dve(dve, norm, g, b)

        def residual_act(act, ps_free, norm):
            for j, (b, m) in enumerate(ORDER_NARROW):
                act.wait_ge(ps_free, j + 1)
                norm_square(act, norm, j, b, m)
            for b in range(NB):
                norm_root(act, norm, b)
                norm_apply_act(act, norm, b)

        def residual_pool(pool, base, norm, ahead):
            for j, (b, m) in enumerate(ORDER_NARROW):
                norm_add(pool, norm, j, b, m == 0)
                if b == NB - 1 and m < KT - 1:
                    ahead(base + m + SPL)
            ahead(base + KT - 1 + SPL)
            for b in range(NB):
                norm_apply_pool(pool, norm, b)

        op_ps, op_free, oc_ps, oc_free = (sem(n) for n in ("op_ps", "op_free", "oc_ps", "oc_free"))

        def ffn_loop(eng, step):
            step(0, False)
            with eng.Fori(1, STEPS - 1) as i:
                step(i, False)
            step(STEPS - 1, True)

        def ffn_pe(pe, f, base, norm, after):
            def step(i, is_last):
                for q in range(GU):
                    t, half, b = q // (2 * NB), q // NB % 2, q % NB
                    c0, w = BLOCKS[b]
                    n = 2 * t + half
                    if isinstance(i, int) and i == 0 and q < NB:
                        norm_ready(pe, norm, b)
                    if b == 0:
                        pe.wait_ge(split_done, base + i * 6 + n + 1)
                    if q < 6:
                        f["dn_add"].wait(pe, i * DN - 5 + q)
                    elif q < 6 + NB:
                        f["silu"].wait(pe, i * HB + q - 5)
                    else:
                        f["hid"].wait(pe, i * HB + q - 5 - NB)
                    last = chain(ps[:, q % 6, 0:w], unit_products(base + n, c0, w))
                    last.then_inc(f["gu_ps"].sem, 1)
                for b, (c0, w) in enumerate(BLOCKS):
                    f["low"].wait(pe, i * HB + NB + b + 1)
                    for m in range(KT):
                        q = b * KT + m
                        if q == 0:
                            pe.wait_ge(split_done, base + i * 6 + 6)
                        if q < 3:
                            f["silu"].wait(pe, i * HB + NB + q + 1)
                        elif q < 6:
                            f["hid"].wait(pe, i * HB + NB + q - 3 + 1)
                        else:
                            f["dn_add"].wait(pe, i * DN + q - 5)
                        last = chain(ps[:, q % 6, 0:w],
                                     [pr for t in range(GF)
                                      for pr in split_products(wh(base + 4 + t)[:, m * P:(m + 1) * P], wl(base + 4 + t)[:, m * P:(m + 1) * P],
                                                               Hh[:, t, c0:c0 + w], Hl[:, t, c0:c0 + w])])
                        last.then_inc(f["dn_ps"].sem, 1)
                        if after and is_last and b > 0 and m == 2:
                            norm_total(pe, after, b - 1, KT * b)
                if after and is_last:
                    norm_total(pe, after, NB - 1, NB * KT)
            ffn_loop(pe, step)

        def ffn_act(act, f, after):
            def step(i, is_last):
                for t in range(GF):
                    for b, (c0, w) in enumerate(BLOCKS):
                        f["gu_ps"].wait(act, i * GU + t * 2 * NB + b + 1)
                        f["hid"].wait(act, i * HB + (t - 1) * NB + b + 1)
                        act.activation(sg[:, b, 0:w], ps[:, b, 0:w], ACT.Silu).then_inc(f["silu"].sem, 1)
                    for b, (c0, w) in enumerate(BLOCKS):
                        f["dn_ps"].wait(act, i * DN)
                        f["hid"].wait(act, i * HB + t * NB + b + 1)
                        act.activation(Hh[:, t, c0:c0 + w], hf[:, b, 0:w], ACT.Copy).then_inc(f["high"].sem, 1)
                if after and is_last:
                    def square(b, m):
                        f["dn_add"].wait(act, i * DN + KT * b + m + 1)
                        norm_square(act, after, KT * b + m, b, m)
                    for b in range(2):
                        for m in range(KT):
                            square(b, m)
                            if b == 1 and m == 4:
                                norm_root(act, after, 0)
                    norm_apply_act(act, after, 0, lambda m: square(2, m))
                    for b in (1, 2):
                        norm_root(act, after, b)
                        norm_apply_act(act, after, b)
            ffn_loop(act, step)

        def ffn_dve(dve, f, after, g):
            def step(i, is_last):
                for t in range(GF):
                    for b, (c0, w) in enumerate(BLOCKS):
                        f["gu_ps"].wait(dve, i * GU + t * 2 * NB + NB + b + 1)
                        f["silu"].wait(dve, i * HB + t * NB + b + 1)
                        dve.tensor_tensor(hf[:, b, 0:w], ps[:, 3 + b, 0:w], sg[:, b, 0:w], ALU.mult).then_inc(f["hid"].sem, 1)
                        f["high"].wait(dve, i * HB + t * NB + b + 1)
                        dve.tensor_tensor(Hl[:, t, c0:c0 + w], hf[:, b, 0:w], Hh[:, t, c0:c0 + w].bitcast(F32),
                                          ALU.subtract).then_inc(f["low"].sem, 1)
                def add(b, m):
                    c0, w = BLOCKS[b]
                    q = b * KT + m
                    f["dn_ps"].wait(dve, i * DN + q + 1)
                    x = xT[:, m, c0:c0 + w]
                    dve.tensor_tensor(x, ps[:, q % 6, 0:w], x, ALU.add).then_inc(f["dn_add"].sem, 1)
                joined = after and is_last
                for b in range(2 if joined else NB):
                    for m in range(KT):
                        add(b, m)
                if joined:
                    norm_apply_dve(dve, after, g, 0, lambda m: add(2, m))
                    for b in (1, 2):
                        norm_apply_dve(dve, after, g, b)
            ffn_loop(dve, step)

        def ffn_pool(pool, f, base, after):
            def step(i, is_last):
                for n in range(6):
                    split_unit(pool, base + (i + 1) * 6 + n, base + n, lambda: ffn_released(pool, f, i, n))
            step(0, False)
            with pool.Fori(1, STEPS - 1) as i:
                step(i, False)
            if not after:
                return
            nxt = base + 6 * STEPS
            for n in range(2 * GF):
                split_ahead(pool, nxt + n)
            for b in range(NB):
                for m in range(KT):
                    norm_add(pool, after, KT * b + m, b, m == 0)
                    if b == 2 and m % 2 == 1:
                        norm_low(pool, after, 0, m)
            for n in range(2 * GF, 6):
                split_ahead(pool, nxt + n)
            for b in (1, 2):
                norm_apply_pool(pool, after, b)

        def split_ahead(pool, n):
            if n < UNITS:
                split_unit(pool, n, n, (lambda: wait_released(pool, n - SPL)) if n >= SPL else (lambda: None))

        names = ("g_in g_in2 g_in3 wt_ps wt_done rt_ps rt_done v_ps v_gelu v_sqsum v_stat v_norm mix_ps mix_done vst_ps vst_done "
                 "vs_ps vs_done u_ps u_gelu y_done yh yl cv_out")
        G = {n: sem(n) for n in names.split()}
        bvrep, bsrow, wsp = VM[:, 7, :], VM[0:1, 6, :], VM[:, 5, :]

        def gmlp_sp(sp):
            FFN[0]["dn_ps"].wait(sp, DN * STEPS)
            sp.dma_start(wsp.rearrange("p (g s) -> p g s", g=KT), a["w_spatial"][0].rearrange("g t s -> t g s")).then_inc(G["g_in"], 16)
            sp.dma_start(bvrep, a["b_v_c"][0, :].partition_broadcast(P)).then_inc(G["g_in2"], 16)
            sp.dma_start(bsrow, a["b_spatial"].rearrange("o g t -> o (g t)")).then_inc(G["g_in2"], 16)
            with nc.allow_non_contiguous_dma("one number a head group"):
                sp.dma_start(w00[:, :], a["w_spatial"][0, :, 0, 0].partition_broadcast(P)).then_inc(G["g_in3"], 16)
                sp.dma_start(b00[:, :], a["b_spatial"][0, :, 0].partition_broadcast(P)).then_inc(G["g_in3"], 16)

        def gmlp_pe(pe, norm):
            pe.wait_ge(G["g_in"], 16)
            for g in range(KT):
                last = nc.tensor.transpose(ps[:, 4 + g // 4, (g % 4) * P:(g % 4 + 1) * P], wsp[:, g * P:(g + 1) * P], ident[:, :])
                if g % 4 == 3:
                    last.then_inc(G["wt_ps"], 1)
            pe.wait_ge(G["wt_done"], 2)
            pe.wait_ge(G["g_in2"], 32)
            for g in range(KT):
                last = chain(ps[:, 4 + g // 4, (g % 4) * P:(g % 4 + 1) * P],
                             [(bvrep[:, g * P:(g + 1) * P], wT[:, g, :]), (ones[0:1, :], bsrow[:, g * P:(g + 1) * P])])
                if g % 4 == 3:
                    last.then_inc(G["rt_ps"], 1)
            for c in range(2):
                for tt in range(TT):
                    q = c * TT + tt
                    if c == 0 and tt in (0, 4, 7):
                        norm_ready(pe, norm, (tt >= 4) + (tt >= 7))
                    positive_wait(pe, G["v_gelu"], q - ZB + 1)
                    wide_products(pe, BASE_V + 4 * c, BASE_V + 4 * c, None, c, tt, q, None).then_inc(G["v_ps"], 1)
                pe.wait_ge(G["v_ps"], (c + 1) * TT)
                pe.sem_inc(w_used, 1)

            def u_unit(m):
                n = BASE_U + m
                pe.wait_ge(split_done, n + 1)
                for b, (c0, w) in enumerate(BLOCKS):
                    j = NB * m + b
                    if j < 6:
                        pe.wait_ge(G["v_gelu"], 2 * TT)
                        pe.wait_ge(G["rt_done"], 2)
                    positive_wait(pe, G["u_gelu"], j - 5)
                    last = chain(ps[:, j % 6, 0:w], unit_products(n, c0, w))
                    last.then_inc(G["u_ps"], 1)
                pe.wait_ge(G["u_ps"], NB * (m + 1))
                pe.sem_inc(w_used, 1)
            u_unit(0)
            u_unit(1)
            pe.wait_ge(G["v_norm"], TT)
            for g in range(KT):
                last = nc.tensor.transpose(ps[:, 6, g * NS:(g + 1) * NS], vs[:, g * P:(g + 1) * P], ident[0:NS, 0:NS])
            last.then_inc(G["vst_ps"], 1)
            pe.wait_ge(G["vst_done"], 1)
            for g in range(KT):
                last = nc.tensor.matmul(ps[0:NS, 6 + g // 4, (g % 4) * P:(g % 4 + 1) * P], vsT[:, g, :], ident[:, :], start=True, stop=True)
            last.then_inc(G["vs_ps"], 1)
            pe.wait_ge(G["vs_done"], 2)
            for tile in range(SEQ // P):
                for half in range(2):
                    j = 2 * tile + half
                    positive_wait(pe, G["mix_done"], (j - 1) * 4)
                    for g in range(4 * half, 4 * half + 4):
                        last = nc.tensor.matmul(ps[:, 6 + half, (g % 4) * P:(g % 4 + 1) * P], VM[:, tile, g * P:(g + 1) * P],
                                                wT[:, g, :], start=True, stop=True)
                    last.then_inc(G["mix_ps"], 1)
            for m in range(2, KT):
                u_unit(m)

        def gmlp_act(act, norm):
            for half in range(2):
                act.wait_ge(G["rt_ps"], half + 1)
                act.activation(RT[:, 4 * half:4 * half + 4, :].rearrange("p g t -> p (g t)"), ps[:, 4 + half, :], ACT.Copy).then_inc(G["rt_done"], 1)
            norm_ready(act, norm, NB - 1)
            act.wait_ge(G["rt_ps"], 2)
            act.wait_ge(G["v_stat"], 1)
            for c in range(2):
                for tt in range(TT):
                    q, r = c * TT + tt, token_rows(tt)
                    dst = vs[:, c * DH:(c + 1) * DH] if tt == 0 else VM[:, tt - 1, c * DH:(c + 1) * DH]
                    act.wait_ge(G["v_ps"], q + 1)
                    act.activation(dst, ps[0:r, q % ZB, :], ACT.Gelu, accum_out=vsum[0:r, tt, c:c + 1]).then_inc(G["v_gelu"], 1)
            act.wait_ge(G["v_stat"], 3)
            for tt in range(TT):
                r = token_rows(tt)
                src = vs[:, :] if tt == 0 else VM[:, tt - 1, :]
                for c in range(2):
                    positive_wait(act, G["v_sqsum"], 2 * tt + c)
                    act.activation(junk[0:r, 0:DH], src[:, c * DH:(c + 1) * DH], ACT.Square, bias=vst[0:r, 1, tt:tt + 1],
                                   accum_out=vsum[0:r, tt, c:c + 1]).then_inc(G["v_sqsum"], 1)
            act.wait_ge(G["v_stat"], 4)
            act.activation(vst[:, 3, :], vst[:, 2, :], ACT.Sqrt, bias=eps[:, 0:1], scale=1.0 / D).then_inc(G["v_sqsum"], 1)
            for m in range(KT):
                for b, (c0, w) in enumerate(BLOCKS):
                    j = NB * m + b
                    act.wait_ge(G["u_ps"], j + 1)
                    positive_wait(act, G["y_done"], j - 1)
                    act.wait_ge(G["v_norm"], TT)
                    act.activation(ug[j % 2][:, 0:w], ps[:, j % 6, 0:w], ACT.Gelu).then_inc(G["u_gelu"], 1)
            act.wait_ge(G["u_ps"], NB * KT)
            for b, (c0, w) in enumerate(BLOCKS):
                for m in range(KT):
                    if b == 0:
                        act.wait_ge(G["y_done"], NB * m + 3)
                        act.activation(Xh[:, m, 0:NS], msT[:, m, :], ACT.Copy)
                    t0, t1 = (0, 3, 6, 8)[b:b + 2]
                    lo = NS + t0 * P
                    act.activation(Xh[:, m, lo:lo + (t1 - t0) * P].rearrange("p (t q) -> p t q", q=P),
                                   VM[:, t0:t1, m * P:(m + 1) * P], ACT.Copy).then_inc(G["yh"], 1)

        junk = wT_src = None

        def gmlp_dve(dve, norm):
            for half in range(2):
                dve.wait_ge(G["wt_ps"], half + 1)
                dve.tensor_tensor(wT[:, 4 * half:4 * half + 4, :], ps[:, 4 + half, :].rearrange("p (g t) -> p g t", g=4),
                                  tri[:, :].unsqueeze(1).to_broadcast([P, 4, P]), ALU.mult).then_inc(G["wt_done"], 1)
            dve.memset(vsum[:, :, :], 0.0).then_inc(G["v_stat"], 1)
            dve.wait_ge(G["v_gelu"], 2 * TT)
            dve.tensor_tensor(vst[:, 0, :], vsum[:, :, 0], vsum[:, :, 1], ALU.add).then_inc(G["v_stat"], 1)
            dve.wait_ge(G["v_stat"], 2)
            dve.tensor_scalar(vst[:, 1, :], vst[:, 0, :], -1.0 / D, None, ALU.mult).then_inc(G["v_stat"], 1)
            dve.wait_ge(G["v_sqsum"], 2 * TT)
            dve.tensor_tensor(vst[:, 2, :], vsum[:, :, 0], vsum[:, :, 1], ALU.add).then_inc(G["v_stat"], 1)
            dve.wait_ge(G["v_sqsum"], 2 * TT + 1)
            dve.reciprocal(vst[:, 0, :], vst[:, 3, :]).then_inc(G["v_stat"], 1)
            dve.wait_ge(G["v_stat"], 5)
            for tt in range(TT):
                r = token_rows(tt)
                v = vs[:, :] if tt == 0 else VM[:, tt - 1, :]
                dve.tensor_scalar(v, v, vst[0:r, 1, tt:tt + 1], vst[0:r, 0, tt:tt + 1], ALU.add, ALU.mult).then_inc(G["v_norm"], 1)
            dve.wait_ge(G["vst_ps"], 1)
            dve.wait_ge(G["g_in3"], 32)
            n = [0]

            def step(ins):
                n[0] += 1
                ins.then_inc(vchain, 1)
                dve.wait_ge(vchain, n[0])
            step(dve.tensor_tensor(msT[:, :, :], ps[:, 6, 0:KT * NS].rearrange("p (g s) -> p g s", g=KT),
                                   gv[:, :].unsqueeze(2).to_broadcast([P, KT, NS]), ALU.mult))
            dve.tensor_tensor(vsT[:, :, :], msT[:, :, :], bv[:, :].unsqueeze(2).to_broadcast([P, KT, NS]), ALU.add).then_inc(G["vst_done"], 1)
            dve.wait_ge(G["vst_done"], 1)
            step(dve.tensor_tensor(msT[:, :, :], vsT[:, :, :], w00[:, :].unsqueeze(2).to_broadcast([P, KT, NS]), ALU.mult))
            step(dve.tensor_tensor(msT[:, :, :], msT[:, :, :], b00[:, :].unsqueeze(2).to_broadcast([P, KT, NS]), ALU.add))
            dve.wait_ge(G["vs_ps"], 1)
            for half in range(2):
                dve.tensor_copy(vs[:, half * DH:(half + 1) * DH], ps[0:NS, 6 + half, :]).then_inc(G["vs_done"], 1)
            for tile in range(SEQ // P):
                for half in range(2):
                    dve.wait_ge(G["mix_ps"], 2 * tile + half + 1)
                    for g in range(4 * half, 4 * half + 4):
                        dve.scalar_tensor_tensor(VM[:, tile, g * P:(g + 1) * P], ps[:, 6 + half, (g % 4) * P:(g % 4 + 1) * P],
                                                 gv[:, g:g + 1], RT[:, g, :], ALU.mult, ALU.add).then_inc(G["mix_done"], 1)
            dve.wait_ge(G["mix_done"], 8 * SEQ // P)
            for m in range(KT):
                for b, (c0, w) in enumerate(BLOCKS):
                    j = NB * m + b
                    t0, t1 = (0, 3, 6, 8)[b:b + 2]
                    dve.wait_ge(G["u_gelu"], j + 1)
                    off = NS if b == 0 else 0
                    if b == 0:
                        dve.tensor_tensor(msT[:, m, :], msT[:, m, :], ug[j % 2][:, 0:NS], ALU.mult)
                    y = VM[:, t0:t1, m * P:(m + 1) * P]
                    dve.tensor_tensor(y, y, ug[j % 2][:, off:w].rearrange("p (t q) -> p t q", q=P), ALU.mult).then_inc(G["y_done"], 1)
            for b, (c0, w) in enumerate(BLOCKS):
                for m in range(KT):
                    t0, t1 = (0, 3, 6, 8)[b:b + 2]
                    lo = NS + t0 * P
                    dve.wait_ge(G["yh"], KT * b + m + 1)
                    if b == 0:
                        dve.tensor_tensor(Xl[:, m, 0:NS], msT[:, m, :], Xh[:, m, 0:NS].bitcast(F32), ALU.subtract)
                    dve.tensor_tensor(Xl[:, m, lo:lo + (t1 - t0) * P].rearrange("p (t q) -> p t q", q=P),
                                      VM[:, t0:t1, m * P:(m + 1) * P],
                                      Xh[:, m, lo:lo + (t1 - t0) * P].bitcast(F32).rearrange("p (t q) -> p t q", q=P),
                                      ALU.subtract).then_inc(G["yl"], 1)

        vchain = sem("vchain")
        junk = ug[0] if False else None
        used[0] = stage_memory
        junk = nc.alloc_sbuf_tensor_at("junk", [P, DH], F32, offset=(nc.sbuf_usable_end - 4 * DH) // 32 * 32)

        used[0] = norm_end
        yt = [place(f"yt{j}", [P, D]) for j in range(2)]
        fin_lo, fin_hi, fin_act, fin_dve = (sem(n) for n in ("fin_lo", "fin_hi", "fin_act", "fin_dve"))
        y_out = sems("y_out", 2)
        n1 = NORMS

        CONSTS = 13
        block = ctx.enter_context(nc.Block())

        @block.sync
        def _(sp):
            for tt in range(NX):
                src = a["x_sample"] if tt == 0 else a["x_prompt"][(tt - 1) * P:tt * P, :]
                sp.dma_start(xs[tt][0:token_rows(tt), :], src).then_inc(x_in[tt], 16)
            with nc.allow_non_contiguous_dma("small constants, once"):
                for dst, src in ((ident[:, :], a["c_ident"]), (tri[:, :], a["c_uo"][:, 0:P]),
                                 (gains[:, 0, :], a["norm_mix"][0].rearrange("(m p) -> p m", p=P)),
                                 (gains[:, 1, :], a["norm_ffn"][0].rearrange("(m p) -> p m", p=P)),
                                 (gains[:, 2, :], a["norm_mix"][1].rearrange("(m p) -> p m", p=P)),
                                 (gains[:, 3, :], a["norm_ffn"][1].rearrange("(m p) -> p m", p=P)),
                                 (gv[:, :], a["g_v_c"][0].rearrange("(m p) -> p m", p=P)),
                                 (bv[:, :], a["b_v_c"][0].rearrange("(m p) -> p m", p=P)),
                                 (cs[:, :, :, :], a["c_rope"]),
                                 (gqk[:, 0, :], a["g_q_a"][0].partition_broadcast(P)),
                                 (gqk[:, 1, :], a["g_k_a"][0].partition_broadcast(P)),
                                 (gqk[:, 2, :], a["g_q_b"][0].partition_broadcast(P)),
                                 (gqk[:, 3, :], a["g_k_b"][0].partition_broadcast(P))):
                    sp.dma_start(dst, src).then_inc(const_in, 16)
                sp.dma_start(bf[:, :], a["b_forget"][0].partition_broadcast(P)).then_inc(bf_in, 16)
            for tt in range(NX, TT):
                sp.wait_ge(xt_lo, tt - NX + 1)
                sp.wait_ge(xt_hi, tt - NX + 1)
                sp.dma_start(xs[tt % NX][:, :], a["x_prompt"][(tt - 1) * P:tt * P, :]).then_inc(x_in[tt % NX], 16)

            def project(i):
                for c in range(3):
                    for j in range(IN_UNITS):
                        n = 4 * c + j
                        src = a["w_in_even"][2 * j * P:(2 * j + 2) * P, bass.ds(i * (3 * DH + HEADS) + c * DH, DH)]
                        load_unit(sp, BASE_IN + i * 12 + n, n, src.rearrange("(k p) n -> p k n", p=P), 2)
            peeled_loop(sp, 2, project)
            load_unit(sp, BASE_FG, BASE_FG, rows(a["w_in_even"], 0, KT, 3 * DH, P), KT)
            pages_sp(sp)
            forget_sp(sp)
            att_sp(sp)
            sp.wait_ge(*ATT_DONE)
            load_narrow(sp, BASE_OUT, a["w_out_even"][0], 8)
            load_ffn(sp, BASE_F0, 0)
            load_wide(sp, BASE_V, a["w_in_c"][0], D)
            gmlp_sp(sp)
            load_wide(sp, BASE_V + 4, a["w_in_c"][0], D + DH)
            load_narrow(sp, BASE_U, a["w_in_c"][0], 8)
            sp.wait_ge(G["vs_done"], 2)
            sp.dma_start(a["cv_sample"], vs[:, :]).then_inc(G["cv_out"], 16)
            load_narrow(sp, BASE_OC, a["w_out_c"][0], 8)
            load_ffn(sp, BASE_F1, 1)
            sp.wait_ge(lf_out, 32)
            sp.wait_ge(G["cv_out"], 16)
            sp.wait_ge(y_out[0], 16 * 5)
            sp.wait_ge(y_out[1], 16 * 4)

        @block.gpsimd
        def _(pool):
            pool.memset(zeros[:, :], 0.0).then_inc(zero_set, 1)
            pool.memset(ones[:, :], 1.0).then_inc(zero_set, 1)
            pool.wait_ge(zero_set, 2)

            for t in range(NB * KT):
                b = t // KT
                norm_add(pool, n1[0], t, b, t % KT == 0)
                if t < SPL:
                    split_ahead(pool, t)
                if b > 0 and t % 2 == 1:
                    norm_low(pool, n1[0], b - 1, t % KT)
            norm_apply_pool(pool, n1[0], NB - 1)

            def project(i):
                for n in range(12):
                    if not isinstance(i, int) or i > 0 or n >= SPL:
                        split_unit(pool, i * 12 + n, n, lambda: positive_wait(pool, w_used, i * 12 + n - SPL + 1))
            peeled_loop(pool, 2, project)
            split_ahead(pool, BASE_FG)
            att_pool(pool)
            pool.wait_ge(*ATT_DONE)
            pool.wait_ge(dpv_ps, PAIRS)
            for n in range(BASE_OUT, BASE_OUT + SPL):
                split_ahead(pool, n)
            residual_pool(pool, BASE_OUT, n1[1], lambda n: split_ahead(pool, n))
            ffn_pool(pool, FFN[0], BASE_F0, n1[2])
            for n in range(BASE_V + SPL, BASE_OC + SPL):
                split_ahead(pool, n)
            residual_pool(pool, BASE_OC, n1[3], lambda n: split_ahead(pool, n))
            ffn_pool(pool, FFN[1], BASE_F1, None)

        def input_ready(eng, b):
            n = (4, 7, 9)[b]
            eng.wait_ge(xt_act, n)
            eng.wait_ge(xt_dve, n)

        @block.tensor
        def _(pe):
            pe.wait_ge(const_in, 16 * CONSTS)
            pe.wait_ge(zero_set, 2)
            for tt in range(TT):
                r = token_rows(tt)
                pe.wait_ge(x_in[tt % NX], 16 * (tt // NX + 1))
                for half, (done, free) in enumerate(((xt_lo, xt_act), (xt_hi, xt_dve))):
                    positive_wait(pe, free, tt - 2)
                    for m in range(4):
                        last = nc.tensor.transpose(ps[:, 3 * half + tt % 3, m * P:m * P + r],
                                                   xs[tt % NX][0:r, (4 * half + m) * P:(4 * half + m + 1) * P], ident[0:r, 0:r])
                    last.then_inc(done, 1)
            for b in range(NB):
                norm_total(pe, n1[0], b, KT * (b + 1))
            in_pe(pe)
            forget_pe(pe)
            pe.wait_ge(lg, 14)
            att_pe(pe)
            pe.wait_ge(*ATT_DONE)
            narrow_pe(pe, BASE_OUT, op_ps, op_free, n1[1])
            ffn_pe(pe, FFN[0], BASE_F0, n1[1], n1[2])
            gmlp_pe(pe, n1[2])
            pe.wait_ge(G["yl"], KT * NB)
            narrow_pe(pe, BASE_OC, oc_ps, oc_free, n1[3])
            ffn_pe(pe, FFN[1], BASE_F1, n1[3], None)
            FFN[1]["dn_add"].wait(pe, DN * STEPS)
            for tt in range(TT):
                t0 = token_columns(tt)
                for half, (done, free) in enumerate(((fin_lo, fin_act), (fin_hi, fin_dve))):
                    positive_wait(pe, free, tt - 2)
                    for m in range(4):
                        last = nc.tensor.transpose(ps[:, 3 * half + tt % 3, m * P:(m + 1) * P], xT[:, 4 * half + m, t0:t0 + P], ident[:, :])
                    last.then_inc(done, 1)

        def finish_half(eng, half):
            done, free = ((fin_lo, fin_act), (fin_hi, fin_dve))[half]
            for tt in range(TT):
                r = token_rows(tt)
                eng.wait_ge(done, tt + 1)
                positive_wait(eng, y_out[tt % 2], 16 * (tt // 2))
                dst, src = yt[tt % 2][0:r, half * 512:(half + 1) * 512], ps[0:r, 3 * half + tt % 3, :]
                if half == 0:
                    eng.activation(dst, src, ACT.Copy).then_inc(free, 1)
                    eng.wait_ge(fin_dve, tt + 1)
                    eng.wait_ge(fin_act, tt + 1)
                    out = a["y_sample"] if tt == 0 else a["y_prompt"][(tt - 1) * P:tt * P, :]
                    eng.dma_start(out, yt[tt % 2][0:r, :]).then_inc(y_out[tt % 2], 16)
                else:
                    eng.tensor_copy(dst, src).then_inc(free, 1)

        @block.scalar
        def _(act):
            for tt in range(TT):
                r, t0 = token_rows(tt), token_columns(tt)
                act.wait_ge(xt_lo, tt + 1)
                act.activation(xT[:, 0:4, t0:t0 + r], ps[:, tt % 3, :].rearrange("p (m t) -> p m t", m=4)[:, :, 0:r],
                               ACT.Copy).then_inc(xt_act, 1)
            act.wait_ge(eps_set, 1)
            for t in range(NB * KT):
                b = t // KT
                if t % KT == 0:
                    input_ready(act, b)
                    if b > 0:
                        norm_root(act, n1[0], b - 1)
                norm_square(act, n1[0], t, b, t % KT)
                if b > 0:
                    norm_high(act, n1[0], b - 1, t % KT)
            norm_root(act, n1[0], NB - 1)
            norm_apply_act(act, n1[0], NB - 1)
            in_act(act)
            forget_act(act)
            act.wait_ge(lg, 14)
            att_act(act)
            residual_act(act, op_free, n1[1])
            ffn_act(act, FFN[0], n1[2])
            gmlp_act(act, n1[2])
            residual_act(act, oc_free, n1[3])
            ffn_act(act, FFN[1], None)
            finish_half(act, 0)

        @block.vector
        def _(dve):
            dve.memset(eps[:, :], EPS).then_inc(eps_set, 1)
            for tt in range(TT):
                r, t0 = token_rows(tt), token_columns(tt)
                dve.wait_ge(xt_hi, tt + 1)
                dve.tensor_copy(xT[:, 4:8, t0:t0 + r], ps[:, 3 + tt % 3, :].rearrange("p (m t) -> p m t", m=4)[:, :, 0:r]).then_inc(xt_dve, 1)
            dve.wait_ge(const_in, 16 * CONSTS)
            for b in range(NB):
                norm_apply_dve(dve, n1[0], 0, b)
            in_dve(dve)
            forget_dve(dve)
            att_dve(dve)
            residual_dve(dve, op_ps, op_free, n1[1], 1)
            ffn_dve(dve, FFN[0], n1[2], 2)
            gmlp_dve(dve, n1[2])
            residual_dve(dve, oc_ps, oc_free, n1[3], 3)
            ffn_dve(dve, FFN[1], None, 0)
            finish_half(dve, 1)


def shape_constants():
    import numpy as np
    f = np.float32
    r, c = np.arange(P)[:, None], np.arange(P)[None, :]
    tri = (r <= c).astype(f)
    dist = SEQ - P + np.arange(P)[:, None] - np.arange(SEQ)[None, :]
    times = sum(((dist >= 0) & (dist % dil == 0) & (dist <= P * dil)).astype(int) for dil in (1, 4, 16))
    dist_bias = np.where(times > 0, np.log(np.maximum(times, 1)) / SCALE, NEG).astype(f)
    causal = np.where(c <= r, 0.0, NEG).astype(f)
    inv = (f(500000.0) ** (-np.arange(0, 16, 2, dtype=f) / f(16))).astype(f)
    rope = np.zeros((P, 2, TT, 32), f)
    rope[:, 0, :, 0:16] = 1.0
    for tt in range(TT):
        pos = np.full(P, PAGES * P) if tt == 0 else (tt - 1) * P + np.arange(P)
        ang = (pos.astype(f)[:, None] * inv[None, :]).astype(f).astype(np.float64)
        rope[:, 1, tt, 0:8] = rope[:, 1, tt, 8:16] = np.cos(ang)
        rope[:, 1, tt, 16:24], rope[:, 1, tt, 24:32] = -np.sin(ang), np.sin(ang)
    db = np.zeros((P, NS, 5, HEADS), f)
    mine = np.arange(P)[:, None] == np.arange(NS)[None, :]
    db[:, :, 0, :] = np.where(mine, 0.0, NEG)[:, :, None]
    db[P // 2:, :, 3, :] = NEG
    db[:, :, 4, :] = np.where(mine, np.log(3.0), NEG)[:, :, None]
    hsel = np.zeros((P, 4, HEADS), f)
    for ch in range(4):
        for half in range(2):
            hsel[half * HD:(half + 1) * HD, ch, 2 * ch + half] = 1.0
    return {"c_ident": np.eye(P, dtype=f), "c_uo": np.concatenate([tri, np.ones((P, SEQ - P), f)], 1),
            "c_ustrict": (r > c).astype(f), "c_dist": dist_bias, "c_causal": causal, "c_rope": rope,
            "c_dbias": db, "c_hsel": hsel}


def kernel(**inputs):
    import numpy as np
    import concourse.bacc as bacc
    from concourse.bass_utils import run_bass_kernel_spmd

    nc = bacc.Bacc("TRN2", target_bir_lowering=False, num_devices=1)
    arrays = {n: np.asarray(v) for n, v in inputs.items()}
    arrays["x_prompt"] = arrays["x_prompt"].reshape(SEQ, D)
    arrays["x_sample"] = arrays["x_sample"].reshape(NS, D)
    arrays["w_in_even"] = arrays["w_in_even"].reshape(D, -1)
    arrays.update(shape_constants())
    arrays = {n: np.ascontiguousarray(v) for n, v in arrays.items()}
    a = {n: nc.dram_tensor(f"in_{n}", v.shape, mybir.dt.from_np(v.dtype), kind="ExternalInput").ap() for n, v in arrays.items()}
    outs = {"y_prompt": (SEQ, D), "y_sample": (NS, D), "k_prompt": (2, SEQ, DH), "v_prompt": (2, SEQ, DH),
            "logf_prompt": (SEQ, HEADS), "k_sample": (2, NS, DH), "v_sample": (2, NS, DH), "logf_sample": (NS, HEADS),
            "cv_sample": (NS, D)}
    for n, shape in outs.items():
        a[n] = nc.dram_tensor(f"out_{n}", shape, F32, kind="ExternalOutput").ap()
    build(nc, a)
    r = run_bass_kernel_spmd(nc, [{f"in_{n}": v for n, v in arrays.items()}], core_ids=[0]).results[0]
    o = {n: r[f"out_{n}"] for n in outs}
    kvp, kvs = (1, 1, SEQ, HEADS, HD), (1, NS, 1, HEADS, HD)
    return (o["y_prompt"].reshape(1, SEQ, D), o["y_sample"].reshape(NS, 1, D),
            o["k_prompt"][0].reshape(kvp), o["v_prompt"][0].reshape(kvp), o["logf_prompt"].reshape(1, 1, SEQ, HEADS),
            o["k_prompt"][1].reshape(kvp), o["v_prompt"][1].reshape(kvp),
            o["k_sample"][0].reshape(kvs), o["v_sample"][0].reshape(kvs), o["logf_sample"].reshape(1, NS, 1, HEADS),
            o["k_sample"][1].reshape(kvs), o["v_sample"][1].reshape(kvs), o["cv_sample"].reshape(1, NS, 1, D))
```

```python
from contextlib import ExitStack

import concourse.bass as bass
from concourse import mybir

ALU = mybir.AluOpType
ACT = mybir.ActivationFunctionType
AX = mybir.AxisListType.X
F32 = mybir.dt.float32
F32R = mybir.dt.float32r
I32 = mybir.dt.int32
RMAX = bass.bass_isa.ReduceOp.max

P = 128
D = 1024
KT = D // P
SEQ = 1024
NS = 8
T = NS + SEQ
TT = 1 + SEQ // P
HEADS = 8
HD = 64
DH = HEADS * HD
FF = 2816
FT = FF // P
GF = 2
STEPS = FT // GF
PAGES = 8
N_PHYS = 80
EPS = 1e-6
SCALE = HD ** -0.5
NEG = -1e30
BLOCKS = [(0, NS + 3 * P), (NS + 3 * P, 3 * P), (NS + 6 * P, 2 * P)]
NB = len(BLOCKS)
RAW = 2
SPL = 6
IN_UNITS = 4
SLOTS = PAGES + 3
LOG = SLOTS + 2


BASE_FG, BASE_IN, BASE_OUT = 0, 1, 25
BASE_F0 = BASE_OUT + 8
BASE_V = BASE_F0 + 6 * STEPS
BASE_U = BASE_V + 8
BASE_OC = BASE_U + 8
BASE_F1 = BASE_OC + 8
UNITS = BASE_F1 + 6 * STEPS


def token_columns(tt):
    return 0 if tt == 0 else NS + (tt - 1) * P


def token_rows(tt):
    return NS if tt == 0 else P


def positive_wait(eng, sem, value):
    if not isinstance(value, int) or value > 0:
        eng.wait_ge(sem, value)


class Counted:

    def __init__(self, sem, start):
        self.sem, self.start = sem, start

    def wait(self, eng, value):
        if not isinstance(value, int) or value > 0:
            eng.wait_ge(self.sem, value + self.start)


def is_first(i):
    return isinstance(i, int) and i == 0


def peeled_loop(eng, count, body):
    body(0)
    with eng.Fori(1, count) as i:
        body(i)


def build(nc, a):
    with ExitStack() as ctx:
        used = [nc.sbuf_base]
        ctx.enter_context(nc.sbuf_tensor("arena", [P, (nc.sbuf_usable_end - nc.sbuf_base) // 4 - 16], F32))

        def place(name, shape, dt=F32):
            n = 1
            for s in shape[1:]:
                n *= s
            off = (used[0] + 31) // 32 * 32
            used[0] = off + 4 * n
            assert used[0] <= nc.sbuf_usable_end, (name, used[0], nc.sbuf_usable_end)
            return nc.alloc_sbuf_tensor_at(name, shape, dt, offset=off)

        def sem(name):
            return ctx.enter_context(nc.semaphore(name))

        def sems(name, n):
            return [sem(f"{name}{j}") for j in range(n)]

        ident = place("ident", [P, P])
        ones = place("ones", [P, P])
        tri = place("tri", [P, P])
        gains = place("gains", [P, 4, KT])
        gv = place("gv", [P, KT])
        bv = place("bv", [P, KT])
        pt = place("pt", [1, NS * PAGES], I32)
        lfp_memory = used[0]
        lfp = place("lfp", [P, NS * PAGES, HEADS])
        lft = place("lft", [P, TT, HEADS])
        eps = place("eps", [P, 1])
        zeros = place("zeros", [P, 1])
        xT = place("xT", [P, KT, T])
        Xh = place("Xh", [P, KT, T], F32R)
        Xl = place("Xl", [P, KT, T], F32R)
        overlay = used[0]
        raw = [place(f"raw{j}", [P, 1024]) for j in range(RAW)]
        Wh = [place(f"Wh{j}", [P, 1024], F32R) for j in range(SPL)]
        Wl = [place(f"Wl{j}", [P, 1024], F32R) for j in range(SPL)]
        stage_memory = used[0]

        BW = BLOCKS[0][1]
        sq = [place(f"sq{j}", [P, BW]) for j in range(2)]
        acc_sq = [place(f"acc_sq{j}", [P, BW]) for j in range(NB)]
        root = [place(f"root{j}", [P, BW]) for j in range(2)]
        NH = 4
        hs = [place(f"hs{j}", [P, BW]) for j in range(NH)]
        norm_end = used[0]

        NX = 4
        xs_memory = used[0]
        xs = [place(f"xs{j}", [P, D]) for j in range(NX)]
        NZ = 3
        zt = [place(f"zt{j}", [P, DH]) for j in range(NZ)]
        zsq = [place(f"zsq{j}", [P, DH]) for j in range(2)]
        ss = place("ss", [P, HEADS])
        zstd = place("zstd", [P, HEADS])
        zrs = place("zrs", [P, HEADS])
        rope_u = place("rope_u", [P, HEADS, 16])
        rope_w = place("rope_w", [P, HEADS, 16])
        gqk = place("gqk", [P, 4, HD])
        cs = place("cs", [P, 2, TT, 32])
        bf = place("bf", [P, HEADS])
        used[0] = xs_memory
        fT = place("fT", [HEADS, T])
        cneg = place("cneg", [HEADS, SEQ])
        lf_t = [place(f"lf_t{j}", [P, TT, HEADS]) for j in range(4)]

        used[0] = norm_end
        Hh = place("Hh", [P, GF, T], F32R)
        Hl = place("Hl", [P, GF, T], F32R)
        sg = place("sg", [P, NB, BLOCKS[0][1]])
        hf = place("hf", [P, NB, BLOCKS[0][1]])

        used[0] = stage_memory
        VM = place("VM", [P, SEQ // P, D])
        vs = place("vs", [NS, D])
        ug = [place(f"ug{j}", [P, BLOCKS[0][1]]) for j in range(2)]
        wT = place("wT", [P, KT, P])
        RT = place("RT", [P, KT, P])
        vsum = place("vsum", [P, TT, 2])
        vst = place("vst", [P, 4, TT])
        w00 = place("w00", [P, KT])
        b00 = place("b00", [P, KT])
        vsT = place("vsT", [P, KT, NS])
        msT = place("msT", [P, KT, NS])

        used[0] = overlay
        assert BASE_OUT % RAW == 1 and BASE_OUT % SPL == 1
        qp = place("qp", [P, 8, P])
        kp = place("kp", [P, 8, P])
        vp = place("vp", [P, 8, P])
        bias = [place(f"bias{j}", [P, SEQ]) for j in range(2)]
        QT = place("QT", [P, SEQ])
        dist = place("dist", [P, SEQ])
        S2 = [place(f"S2{j}", [P, SEQ]) for j in range(2)]
        qrep = place("qrep", [P, 2, DH])
        prod = [place(f"prod{j}", [P, DH]) for j in range(2)]
        KTr = place("KTr", [P, SEQ])
        causal = place("causal", [P, P])
        score_memory = used[0]
        Pr = [place(f"Pr{j}", [P, SEQ]) for j in range(2)]
        PT = [place(f"PT{j}", [P, 8, P]) for j in range(2)]
        mx = place("mx", [P, 16])
        lsum = [place(f"lsum{j}", [P, 16]) for j in range(2)]
        rl = place("rl", [P, 16])
        O = [place(f"O{j}", [P, SEQ]) for j in range(2)]
        ring = place("ring", [P, SLOTS, DH])
        own = place("own", [NS, 4, DH])
        dbias = place("dbias", [P, NS, LOG, HEADS])
        L = place("L", [P, LOG, HEADS])
        hsel = place("hsel", [P, 4, HEADS])
        oS = place("oS", [P, KT, NS])
        used[0] = lfp_memory
        Lb = place("Lb", [P, LOG, HEADS])
        Lm = place("Lm", [P, 2, HEADS])
        LM = place("LM", [P, 2, HEADS])
        Lp = place("Lp", [P, LOG, HEADS])
        dl = place("dl", [P, 2, HEADS])
        drl = place("drl", [P, 2, HEADS])
        do1 = place("do1", [P, 2, 4, HEADS])
        do2 = place("do2", [P, 2, 4, HEADS])
        used[0] = score_memory
        ustr = place("ustr", [P, P])
        lnd = place("lnd", [NS, NS, HEADS])
        acc = [place(f"acc{j}", [P, NS, HEADS]) for j in range(2)]

        ps = ctx.enter_context(nc.psum_tensor("ps", [P, 8, 512], F32))

        q_prompt = nc.dram_tensor("q_prompt", (2, SEQ, DH), F32).ap()
        q_sample = nc.dram_tensor("q_sample", (2, NS, DH), F32).ap()
        c_dram = nc.dram_tensor("c_dram", (HEADS, SEQ), F32).ap()
        qkv_prompt = [q_prompt, a["k_prompt"], a["v_prompt"]]
        qkv_sample = [q_sample, a["k_sample"], a["v_sample"]]

        const_in = sem("const_in")
        eps_set = sem("eps_set")
        x_in = sems("x_in", NX)
        xt_lo, xt_hi = sem("xt_lo"), sem("xt_hi")
        xt_act, xt_dve = sem("xt_act"), sem("xt_dve")
        raw_in = sems("raw_in", RAW)
        split_high, split_done, w_used = sem("split_high"), sem("split_done"), sem("w_used")
        zero_set = sem("zero_set")

        GU = 2 * NB * GF
        HB = NB * GF
        DN = NB * KT
        ffn_sem = {k: (sem(f"ffn_{k}"), n * STEPS) for k, n in (
            ("gu_ps", GU), ("silu", HB), ("hid", HB), ("high", HB), ("low", HB), ("dn_ps", DN), ("dn_add", DN))}
        FFN = [{k: Counted(x, n * j) for k, (x, n) in ffn_sem.items()} for j in range(2)]


        def load_unit(sp, n, slot, src, shape):
            positive_wait(sp, split_done, n - RAW + 1)
            dst = raw[slot % RAW][:, :]
            if shape:
                dst = dst.rearrange("p (a b) -> p a b", a=shape)
            with nc.allow_non_contiguous_dma("512-byte and longer runs"):
                return sp.dma_start(dst, src).then_inc(raw_in[slot % RAW], 16)

        def rows(w, k0, nk, c0, nc_):
            return w[k0 * P:(k0 + nk) * P, c0:c0 + nc_].rearrange("(k p) n -> p k n", p=P)

        def load_wide(sp, base, w, col):
            for j in range(IN_UNITS):
                load_unit(sp, base + j, base + j, rows(w, 2 * j, 2, col, DH), 2)

        def load_narrow(sp, base, w, count):
            for m in range(count):
                load_unit(sp, base + m, base + m, rows(w, 0, KT, m * P, P), KT)

        def load_ffn(sp, base, layer):
            gu, down = a["w_gate_up"][layer], a["w_down"][layer]

            def step(i):
                for t in range(GF):
                    f = i * GF + t
                    for half in range(2):
                        n = 2 * t + half
                        src = gu[:, bass.ds(f * P + half * FF, P)].rearrange("(k p) n -> p k n", p=P)
                        load_unit(sp, base + i * 6 + n, base + n, src, KT)
                for t in range(GF):
                    n = 4 + t
                    load_unit(sp, base + i * 6 + n, base + n, down[bass.ds((i * GF + t) * P, P), :], 0)
            peeled_loop(sp, STEPS, step)

        def wait_released(eng, n):
            for f, base in ((FFN[0], BASE_F0), (FFN[1], BASE_F1)):
                if base <= n < base + 6 * STEPS:
                    ffn_released(eng, f, (n - base) // 6, (n - base) % 6)
                    return
            positive_wait(eng, w_used, n + 1 - (6 * STEPS if n >= BASE_V else 0))

        def ffn_released(eng, f, i, j):
            if j < 2 * GF:
                f["gu_ps"].wait(eng, i * GU + 2 * NB * (j // 2 + 1) - 1 + j % 2)
            else:
                f["dn_ps"].wait(eng, i * DN + DN)

        def split_unit(pool, n, slot, released):
            h, l, r = Wh[slot % SPL], Wl[slot % SPL], raw[slot % RAW]
            released()
            pool.wait_ge(raw_in[slot % RAW], raw_value(n, slot))
            pool.tensor_tensor(h[:, :], r[:, :], zeros[:, :].to_broadcast([P, 1024]), ALU.add).then_inc(split_high, 1)
            pool.wait_ge(split_high, n + 1)
            pool.tensor_tensor(l[:, :], r[:, :], h[:, :].bitcast(F32), ALU.subtract).then_inc(split_done, 1)

        def raw_value(n, slot):
            return (n - slot % RAW) * (16 // RAW) + 16

        norm_sem = {k: (sem(f"norm_{k}"), n) for k, n in (
            ("squared", NB * KT), ("summed", NB * KT), ("total", NB), ("root", NB), ("rstd", NB),
            ("scaled", NB * KT), ("high", NB * KT), ("low_dve", NB * KT // 2), ("low_pool", NB * KT // 2))}
        NORMS = [{k: Counted(x, n * (j - (k == "total"))) for k, (x, n) in norm_sem.items()} for j in range(4)]

        def norm_ready(eng, s, b):
            s["low_dve"].wait(eng, KT // 2 * (b + 1))
            s["low_pool"].wait(eng, KT // 2 * (b + 1))

        def norm_square(act, s, t, b, m):
            c0, n = BLOCKS[b]
            s["summed"].wait(act, t - 1)
            act.activation(sq[t % 2][:, 0:n], xT[:, m, c0:c0 + n], ACT.Square).then_inc(s["squared"].sem, 1)

        def norm_add(pool, s, t, b, first):
            n = BLOCKS[b][1]
            s["squared"].wait(pool, t + 1)
            s["summed"].wait(pool, t)
            other = zeros[:, :].to_broadcast([P, n]) if first else acc_sq[b][:, 0:n]
            pool.tensor_tensor(acc_sq[b][:, 0:n], sq[t % 2][:, 0:n], other, ALU.add).then_inc(s["summed"].sem, 1)

        def norm_total(pe, s, b, summed):
            n = BLOCKS[b][1]
            s["summed"].wait(pe, summed)
            s["root"].wait(pe, b - 1)
            nc.tensor.matmul(ps[:, 6 + b % 2, 0:n], ones[:, :], acc_sq[b][:, 0:n], start=True,
                             stop=True).then_inc(s["total"].sem, 1)

        def norm_root(act, s, b):
            n = BLOCKS[b][1]
            if s is NORMS[0]:
                s["summed"].wait(act, KT * (b + 1))
            else:
                s["total"].wait(act, b + 1)
            s["rstd"].wait(act, b - 1)
            act.activation(root[b % 2][:, 0:n], ps[:, 6 + b % 2, 0:n], ACT.Sqrt, bias=eps[:, 0:1],
                           scale=1.0 / D).then_inc(s["root"].sem, 1)

        def norm_rstd(dve, s, b):
            n = BLOCKS[b][1]
            s["root"].wait(dve, b + 1)
            dve.reciprocal(acc_sq[b][:, 0:n], root[b % 2][:, 0:n]).then_inc(s["rstd"].sem, 1)
            s["rstd"].wait(dve, b + 1)

        def norm_scale(dve, s, g, b, m):
            c0, n = BLOCKS[b]
            u = KT * b + m
            s["low_dve" if m % 2 == 0 else "low_pool"].wait(dve, (u - NH) // 2 + 1)
            dve.scalar_tensor_tensor(hs[u % NH][:, 0:n], xT[:, m, c0:c0 + n], gains[:, g, m:m + 1], acc_sq[b][:, 0:n],
                                     ALU.mult, ALU.mult).then_inc(s["scaled"].sem, 1)

        def norm_high(act, s, b, m):
            c0, n = BLOCKS[b]
            u = KT * b + m
            s["scaled"].wait(act, u + 1)
            act.activation(Xh[:, m, c0:c0 + n], hs[u % NH][:, 0:n], ACT.Copy).then_inc(s["high"].sem, 1)

        def norm_low(eng, s, b, m):
            c0, n = BLOCKS[b]
            u = KT * b + m
            s["high"].wait(eng, u + 1)
            eng.tensor_tensor(Xl[:, m, c0:c0 + n], hs[u % NH][:, 0:n], Xh[:, m, c0:c0 + n].bitcast(F32),
                              ALU.subtract).then_inc(s["low_dve" if m % 2 == 0 else "low_pool"].sem, 1)

        def norm_apply_dve(dve, s, g, b, between=None):
            norm_rstd(dve, s, b)
            for m in range(KT):
                if between:
                    between(m)
                norm_scale(dve, s, g, b, m)
                if m >= 2 and m % 2 == 0:
                    norm_low(dve, s, b, m - 2)
            norm_low(dve, s, b, KT - 2)

        def norm_apply_act(act, s, b, between=None):
            for m in range(KT):
                if between:
                    between(m)
                norm_high(act, s, b, m)

        def norm_apply_pool(pool, s, b):
            for m in range(1, KT, 2):
                norm_low(pool, s, b, m)

        def chain(out, pairs, last=None):
            for j, (w, x) in enumerate(pairs):
                ins = nc.tensor.matmul(out, w, x, start=(j == 0), stop=(j == len(pairs) - 1))
            return ins

        def split_products(w_high, w_low, x_high, x_low):
            return [(w_high, x_high), (w_high, x_low), (w_low, x_high)]

        def unit_products(n, c0, w):
            return [pr for k in range(KT)
                    for pr in split_products(Wh[n % SPL][:, k * P:(k + 1) * P], Wl[n % SPL][:, k * P:(k + 1) * P],
                                             Xh[:, k, c0:c0 + w], Xl[:, k, c0:c0 + w])]

        z_ps, z_free, z_squared, z_sum, z_root, z_rs, z_scaled, z_gain, z_rope1, z_done = (
            sem(n) for n in ("z_ps", "z_free", "z_squared", "z_sum", "z_root", "z_rs", "z_scaled", "z_gain", "z_rope1", "z_done"))
        z_out = sems("z_out", NZ)
        bf_in, f_ps, f_out, ft_ps = sem("bf_in"), sem("f_ps"), sem("f_out"), sem("ft_ps")
        ZB = 3
        NZT = 3 * TT

        def wide_products(pe, n0, s0, tt, q):
            t0 = token_columns(tt)
            out = ps[:, q % ZB, :]
            for k in range(KT):
                if tt == 0 and k % 2 == 0:
                    pe.wait_ge(split_done, n0 + k // 2 + 1)
                h = Wh[(s0 + k // 2) % SPL][:, (k % 2) * DH:(k % 2 + 1) * DH]
                l = Wl[(s0 + k // 2) % SPL][:, (k % 2) * DH:(k % 2 + 1) * DH]
                xh, xl = Xh[:, k, t0:t0 + P], Xl[:, k, t0:t0 + P]
                nc.tensor.matmul(out, xh, h, start=(k == 0), stop=False)
                nc.tensor.matmul(out, xh, l, start=False, stop=False)
                last = nc.tensor.matmul(out, xl, h, start=False, stop=(k == KT - 1))
                if tt == TT - 1 and k % 2 == 1 and k < KT - 1:
                    last.then_inc(w_used, 1)
            return last

        def forget_products(pe, b):
            c0, w = BLOCKS[b]
            if b == 0:
                pe.wait_ge(split_done, BASE_FG + 1)
            chain(ps[:, 3 + b, 0:w], unit_products(BASE_FG, c0, w)).then_inc(f_ps, 1)
            if b == NB - 1:
                pe.wait_ge(f_ps, NB)
                pe.sem_inc(w_used, 1)

        def in_pe(pe):
            def step(i):
                for c in range(3):
                    for tt in range(TT):
                        q = c * TT + tt
                        if is_first(i) and c == 0 and tt in (0, 4, 7):
                            b = (tt >= 4) + (tt >= 7)
                            norm_ready(pe, NORMS[0], b)
                            forget_products(pe, b)
                        positive_wait(pe, z_free, i * NZT + q - ZB + 1)
                        last = wide_products(pe, BASE_IN + i * 12 + 4 * c, BASE_IN + 4 * c, tt, q)
                        last.then_inc(z_ps, 1)
                    pe.wait_ge(z_ps, i * NZT + (c + 1) * TT)
                    pe.sem_inc(w_used, 1)
                    if is_first(i) and c == 0:
                        forget_transpose(pe)
                    if is_first(i) and c == 1:
                        forget_sums(pe)
            peeled_loop(pe, 2, step)

        def forget_transpose(pe):
            pe.wait_ge(f_out, NB)
            for tt in range(TT):
                t0 = token_columns(tt)
                last = nc.tensor.transpose(ps[:, 6, tt * HEADS:(tt + 1) * HEADS], fT[:, t0:t0 + P], ident[0:HEADS, 0:HEADS])
            last.then_inc(ft_ps, 1)

        def forget_sums(pe):
            pe.wait_ge(lg, 3)
            for u in range(SEQ // P):
                last = chain(ps[0:HEADS, 3 + u // 4, (u % 4) * P:(u % 4 + 1) * P],
                             [(lft[:, t + 1, :], tri[:, :] if t == u else ones[:, :]) for t in range(u + 1)])
            last.then_inc(c_ps, 1)

        def in_store(act, i, c, tt, q):
            r = token_rows(tt)
            dst = qkv_sample[c][i] if tt == 0 else qkv_prompt[c][i, (tt - 1) * P:tt * P, :]
            act.wait_ge(z_done, i * NZT + q + 1)
            act.dma_start(dst, zt[q % NZ][0:r, :]).then_inc(z_out[q % NZ], 16)

        def in_act(act):
            def step(i):
                for c in range(3):
                    for tt in range(TT):
                        q, r = c * TT + tt, token_rows(tt)
                        if c < 2:
                            n = i * 2 * TT + q
                            act.wait_ge(z_ps, i * NZT + q + 1)
                            positive_wait(act, z_sum, n - 1)
                            act.activation(zsq[q % 2][0:r, :], ps[0:r, q % ZB, :], ACT.Square).then_inc(z_squared, 1)
                        if q > 0:
                            in_store(act, i, (q - 1) // TT, (q - 1) % TT, q - 1)
                        if c < 2:
                            act.wait_ge(z_sum, n + 1)
                            positive_wait(act, z_rs, n)
                            act.activation(zstd[0:r, :], ss[0:r, :], ACT.Sqrt, bias=eps[0:r, 0:1],
                                           scale=1.0 / HD).then_inc(z_root, 1)
                    if is_first(i) and c == 0:
                        forget_act(act)
                in_store(act, i, 2, TT - 1, NZT - 1)
            peeled_loop(act, 2, step)

        def in_dve(dve):
            def step(i):
                for c in range(3):
                    if is_first(i) and c == 1:
                        forget_logs(dve)
                    if is_first(i) and c == 2:
                        forget_sums_out(dve)
                    for tt in range(TT):
                        if is_first(i) and c == 0 and tt in (3, 6, 8):
                            forget_copy(dve, (3, 6, 8).index(tt))
                        q, r = c * TT + tt, token_rows(tt)
                        z, n = zt[q % NZ], i * 2 * TT + q
                        z3 = z[0:r, :].rearrange("p (h e) -> p h e", h=HEADS)
                        p3 = ps[0:r, q % ZB, :].rearrange("p (h e) -> p h e", h=HEADS)
                        if c == 2:
                            positive_wait(dve, z_out[q % NZ], (i * (NZT // NZ) + q // NZ) * 16)
                            dve.wait_ge(z_ps, i * NZT + q + 1)
                            dve.tensor_scalar(z[0:r, :], ps[0:r, q % ZB, :], 1.0, None, ALU.mult).then_inc(z_free, 1)
                            dve.wait_ge(z_free, i * NZT + q + 1)
                            dve.tensor_scalar(ss[0:1, 0:1], z[0:1, 0:1], 1.0, None, ALU.mult).then_inc(z_done, 1)
                            continue
                        dve.wait_ge(z_squared, n + 1)
                        positive_wait(dve, z_root, n)
                        dve.tensor_reduce(ss[0:r, :], zsq[q % 2][0:r, :].rearrange("p (h e) -> p h e", h=HEADS), AX,
                                          ALU.add).then_inc(z_sum, 1)
                        dve.wait_ge(z_root, n + 1)
                        dve.reciprocal(zrs[0:r, :], zstd[0:r, :]).then_inc(z_rs, 1)
                        positive_wait(dve, z_out[q % NZ], (i * (NZT // NZ) + q // NZ) * 16)
                        dve.wait_ge(z_rs, n + 1)
                        dve.tensor_tensor(z3, p3, zrs[0:r, :].unsqueeze(2).to_broadcast([r, HEADS, HD]),
                                          ALU.mult).then_inc(z_free, 1)
                        dve.wait_ge(z_free, i * NZT + q + 1)
                        dve.tensor_tensor(z3, z3, gqk[0:r, bass.ds(2 * i + c, 1), :].to_broadcast([r, HEADS, HD]),
                                          ALU.mult).then_inc(z_gain, 1)
                        dve.wait_ge(z_gain, n + 1)
                        C = cs[0:r, bass.ds(i, 1), tt, 0:16].to_broadcast([r, HEADS, 16])
                        sin_minus = cs[0:r, bass.ds(i, 1), tt, 16:24].to_broadcast([r, HEADS, 8])
                        sin_plus = cs[0:r, bass.ds(i, 1), tt, 24:32].to_broadcast([r, HEADS, 8])
                        dve.tensor_tensor(rope_u[0:r], z3[:, :, 0:16], C, ALU.mult)
                        dve.tensor_tensor(rope_w[0:r, :, 0:8], z3[:, :, 8:16], sin_minus, ALU.mult)
                        dve.tensor_tensor(rope_w[0:r, :, 8:16], z3[:, :, 0:8], sin_plus, ALU.mult).then_inc(z_rope1, 1)
                        dve.wait_ge(z_rope1, n + 1)
                        dve.tensor_tensor(z3[:, :, 0:16], rope_u[0:r], rope_w[0:r], ALU.add).then_inc(z_done, 1)
            peeled_loop(dve, 2, step)

        lg, lg_a = sem("lg"), sem("lg_a")
        lf_out, c_ps, c_out, c_in = sem("lf_out"), sem("c_ps"), sem("c_out"), sem("c_in")
        att_const_in, page_in, lfp_in, db_ps, db = sem("att_const_in"), sem("page_in"), sem("lfp_in"), sem("db_ps"), sem("db")
        q_in, k_in, v_in, own_in, qrep_in = sem("q_in"), sem("k_in"), sem("v_in"), sem("own_in"), sem("qrep_in")
        bias_in = sems("bias_in", 2)
        ring_in = sems("ring_in", SLOTS)

        def forget_copy(dve, b):
            c0, w = BLOCKS[b]
            dve.wait_ge(f_ps, b + 1)
            dve.tensor_copy(fT[:, c0:c0 + w], ps[0:HEADS, 3 + b, 0:w]).then_inc(f_out, 1)

        def forget_logs(dve):
            dve.wait_ge(bf_in, 16)
            dve.wait_ge(ft_ps, 1)
            z = ps[:, 6, 0:TT * HEADS].rearrange("p (t h) -> p t h", t=TT)
            dve.tensor_tensor(lf_t[0][:, :, :], z, bf[:, :].unsqueeze(1).to_broadcast([P, TT, HEADS]), ALU.add).then_inc(lg, 1)
            dve.wait_ge(lg, 1)
            dve.scalar_tensor_tensor(lf_t[1][:, :, :], lf_t[0][:, :, :], -1.0, lf_t[0][:, :, :], ALU.mult, ALU.max).then_inc(lg, 1)
            dve.wait_ge(lg_a, 2)
            dve.scalar_tensor_tensor(lft[:, :, :], lf_t[0][:, :, :], 0.0, lf_t[3][:, :, :], ALU.min, ALU.subtract).then_inc(lg, 1)

        def forget_sums_out(dve):
            dve.wait_ge(c_ps, 1)
            dve.tensor_scalar(cneg[:, :], ps[0:HEADS, 3:5, :].rearrange("p a b -> p (a b)"), -1.0 / SCALE, None,
                              ALU.mult).then_inc(lg, 1)

        FORGET_DONE = 4 + 1 + 1 + PAGES

        def forget_dve(dve):
            count = [4]

            def done(ins):
                count[0] += 1
                ins.then_inc(lg, 1)
                return count[0]
            dve.wait_ge(z_ps, 2 * NZT)
            dve.tensor_tensor(ustr[:, :], ones[:, :], tri[:, :], ALU.subtract)
            n = done(dve.tensor_tensor(lnd[:, :, :], lft[0:NS, 0, :].unsqueeze(1).to_broadcast([NS, NS, HEADS]),
                                       ident[0:NS, 0:NS].unsqueeze(2).to_broadcast([NS, NS, HEADS]), ALU.mult))
            dve.memset(L[:, :, :], 0.0)
            dve.wait_ge(db_ps, 1)
            inner = ps[:, 2, :].rearrange("p (s g h) -> p s g h", s=NS, g=PAGES)
            total = ps[:, 3, :].rearrange("p (s g h) -> p s g h", s=NS, g=PAGES)
            n = done(dve.tensor_scalar(acc[0][:, :, :], ps[:, 4, 0:NS * HEADS].rearrange("p (s h) -> p s h", s=NS),
                                       1.0, None, ALU.mult))
            for j, g in enumerate(reversed(range(PAGES))):
                dve.wait_ge(lg, n)
                dve.tensor_tensor(dbias[:, :, g, :], inner[:, :, g, :], acc[j % 2][:, :, :], ALU.add)
                n = done(dve.tensor_tensor(acc[(j + 1) % 2][:, :, :], total[:, :, g, :], acc[j % 2][:, :, :], ALU.add))
            dve.wait_ge(lg, n)

        def forget_act(act):
            act.wait_ge(lg, 2)
            act.activation(lf_t[2][:, :, :], lf_t[1][:, :, :], ACT.Exp, scale=-1.0).then_inc(lg_a, 1)
            act.wait_ge(lg_a, 1)
            act.activation(lf_t[3][:, :, :], lf_t[2][:, :, :], ACT.Ln, bias=1.0).then_inc(lg_a, 1)

        def forget_pe(pe):
            pe.wait_ge(lfp_in, 16 * NS * PAGES)
            pe.wait_ge(lg, 5)
            pe.wait_ge(z_free, 2 * NZT)
            flat = lfp[:, :, :].rearrange("p g h -> p (g h)")
            nc.tensor.matmul(ps[:, 2, :], ustr[:, :], flat, start=True, stop=True)
            nc.tensor.matmul(ps[:, 3, :], ones[:, :], flat, start=True, stop=True)
            nc.tensor.matmul(ps[:, 4, 0:NS * HEADS], ones[0:NS, :], lnd[:, :, :].rearrange("p s h -> p (s h)"),
                             start=True, stop=True).then_inc(db_ps, 1)

        ATT_CONSTS = 3

        def pages_sp(sp, part):
            if part == 0:
                sp.dma_start(pt[:, :], a["page_table"].rearrange("s g -> (s g)").rearrange("(o n) -> o n", o=1)).then_inc(page_in, 16)
                sp.wait_ge(page_in, 16)
            n = NS * PAGES // 4
            with nc.allow_non_contiguous_dma("eight values a token"):
                with sp.Fori(part * n, (part + 1) * n) as g:
                    page = sp.value_load(pt[0:1, bass.ds(g, 1)], min_val=0, max_val=N_PHYS - 1)
                    sp.dma_start(lfp[:, bass.ds(g, 1), :], a["cache_a_logf"][0, bass.ds(page, 1)].rearrange("o t h -> t o h")).then_inc(lfp_in, 16)

        def forget_store(sp):
            sp.wait_ge(lg, 3)
            with nc.allow_non_contiguous_dma("eight values a token"):
                sp.dma_start(a["logf_prompt"].rearrange("(t p) h -> p t h", p=P), lft[:, 1:TT, :]).then_inc(lf_out, 16)
                sp.dma_start(a["logf_sample"], lft[0:NS, 0, :]).then_inc(lf_out, 16)
            sp.wait_ge(lg, 4)
            sp.dma_start(c_dram, cneg[:, :]).then_inc(c_out, 16)

        def load_qk(sp, it):
            grp, cols = it // 4, slice(it % 4 * P, (it % 4 + 1) * P)
            with nc.allow_non_contiguous_dma("512-byte runs"):
                sp.dma_start(qp[:, :, :], q_prompt[grp, :, cols].rearrange("(t p) e -> p t e", p=P)).then_inc(q_in, 16)
                sp.dma_start(kp[:, :, :], a["k_prompt"][grp, :, cols].rearrange("(t p) e -> p t e", p=P)).then_inc(k_in, 16)

        def att_begin_sp(sp):
            sp.wait_ge(z_ps, 2 * NZT)
            for j in range(NZ):
                sp.wait_ge(z_out[j], 16 * 2 * NZT // NZ)
            load_qk(sp, 0)
            for dst, src in ((causal, "c_causal"), (hsel, "c_hsel")):
                sp.dma_start(dst[:], a[src]).then_inc(att_const_in, 16)
            sp.dma_start(dbias[:, :, SLOTS - 3:LOG, :], a["c_dbias"]).then_inc(att_const_in, 16)
            sp.wait_ge(c_out, 16)

        def att_later_sp(sp):
            sp.dma_start(dist[:], a["c_dist"]).then_inc(dist_in, 16)
            with nc.allow_non_contiguous_dma("rows of a head group"):
                for j, src in enumerate((a["k_sample"][0], a["v_sample"][0], a["k_sample"][1], a["v_sample"][1])):
                    sp.dma_start(own[:, j, :], src).then_inc(own_in, 16)

        s_ps, s_biased, p_done, rl_done, p_scaled, pt_ps, pt_out, pv_ps, o_out = (
            sem(n) for n in ("s_ps", "s_biased", "p_done", "rl_done", "p_scaled", "pt_ps", "pt_out", "pv_ps", "o_out"))
        qk_ps, qk_act, qk_dve, masked, o_high, o_low = (
            sem(n) for n in ("qk_ps", "qk_act", "qk_dve", "masked", "o_high", "o_low"))
        prod_done, log_done, dch, ar_done, dp_done, dsum_ps, dpv_ps, osamp = (
            sem(n) for n in ("prod_done", "log_done", "dch", "ar_done", "dp_done", "dsum_ps", "dpv_ps", "osamp"))
        v_in2, dist_in = sem("v_in2"), sem("dist_in")
        PAIRS = 8
        HSTEPS = 8
        STEP = [(hh, qt) for hh in range(2) for qt in reversed(range(HSTEPS))]
        NSTEP = 16 * PAIRS
        DCH = 10
        LOG_AT = {4: (0, 1), 5: (2, 3), 6: (4, 5), 7: (6, 7), 8: (8,), 9: (9,), 10: (10,), 11: (11, 12)}
        QK_BANKS = (1, 3, 5, 7)
        halves = [0]
        for s_ in range(NSTEP):
            halves.append(halves[-1] + STEP[s_ % 16][1] // 4 + 1)

        def att_sp(sp):
            for it in range(PAIRS):
                grp, j = it // 4, it % 4
                cols = slice(j * P, (j + 1) * P)
                v_src = a["v_prompt"][grp, :, cols].rearrange("(t p) e -> p t e", p=P)
                with nc.allow_non_contiguous_dma("512-byte runs"):
                    if it:
                        sp.wait_ge(qk_ps, 4 * it)
                        load_qk(sp, it)
                    if grp == 0:
                        positive_wait(sp, s_biased, 16 * (it - 1) + 8)
                        sp.dma_start(bias[0][:, :], c_dram[2 * j, :].partition_broadcast(P)).then_inc(bias_in[0], 16)
                    positive_wait(sp, pv_ps, 16 * (it - 1) + 12)
                    sp.dma_start(vp[:, 4:8, :], v_src[:, 4:8, :]).then_inc(v_in2, 16)
                    positive_wait(sp, pv_ps, 16 * it)
                    sp.dma_start(vp[:, 0:4, :], v_src[:, 0:4, :]).then_inc(v_in, 16)
                    if grp == 0:
                        positive_wait(sp, s_biased, 16 * it)
                        sp.dma_start(bias[1][:, :], c_dram[2 * j + 1, :].partition_broadcast(P)).then_inc(bias_in[1], 16)
                    if it == 0:
                        att_later_sp(sp)
                    positive_wait(sp, prod_done, LOG * it)
                    for g in range(2):
                        sp.dma_start(qrep[:, g, :], q_sample[g, it, :].partition_broadcast(P)).then_inc(qrep_in, 16)
                    for kind in range(2):
                        cache = a["cache_a_k"] if kind == 0 else a["cache_a_v"]
                        state = a["state_b_k"] if kind == 0 else a["state_b_v"]
                        for slot in range(SLOTS):
                            if kind == 0:
                                positive_wait(sp, dpv_ps, it)
                            else:
                                sp.wait_ge(prod_done, LOG * it + slot + 1 + (slot >= PAGES))
                            if slot < PAGES:
                                page = sp.value_load(pt[0:1, it * PAGES + slot:it * PAGES + slot + 1], min_val=0, max_val=N_PHYS - 1)
                                src = cache[0, bass.ds(page, 1)].rearrange("o t h e -> t (o h e)")
                                sp.dma_start(ring[:, slot, :], src).then_inc(ring_in[slot], 16)
                            else:
                                dil = 4 ** (slot - PAGES)
                                r = min(P, PAGES * P // dil)
                                t0 = PAGES * P - r * dil
                                src = state[0, it, t0:PAGES * P, :, :].rearrange("(r d) h e -> r d (h e)", d=dil)[:, 0, :]
                                sp.dma_start(ring[0:r, slot, :], src).then_inc(ring_in[slot], 16)

        def log_slot(j):
            if j < PAGES:
                return P, 0, ring[:, j, :], j
            if j == PAGES:
                return NS, 0, own[0:NS, 0, :], None
            if j < LOG - 1:
                r = min(P, PAGES * P // 4 ** (j - PAGES - 1))
                return r, 1, ring[0:r, j - 1, :], j - 1
            return NS, 1, own[0:NS, 2, :], None

        def value_tile(j, c):
            r, g, _, slot = log_slot(j)
            if slot is None:
                return own[0:NS, 2 * g + 1, c * P:(c + 1) * P]
            return ring[0:r, slot, c * P:(c + 1) * P]

        SPLIT_LATE = PAIRS - 1

        def split_out_pool(pool, it):
            pool.wait_ge(o_out, 16 * (it + 1))
            pool.tensor_tensor(Xh[:, it, NS:T], O[it % 2][:, :], zeros[:, :].to_broadcast([P, SEQ]), ALU.add).then_inc(o_high, 1)
            pool.wait_ge(o_high, it + 1)
            pool.tensor_tensor(Xl[:, it, NS:T], O[it % 2][:, :], Xh[:, it, NS:T].bitcast(F32), ALU.subtract).then_inc(o_low, 1)

        def att_pool(pool):
            for it in range(PAIRS):
                if 1 <= it <= SPLIT_LATE:
                    split_out_pool(pool, it - 1)
                pool.wait_ge(qrep_in, 32 * (it + 1))
                if it == 0:
                    pool.wait_ge(own_in, 64)
                for j in range(LOG):
                    r, g, keys, slot = log_slot(j)
                    n = LOG * it + j
                    if slot is not None:
                        pool.wait_ge(ring_in[slot], 32 * it + 16)
                    positive_wait(pool, log_done, n - 1)
                    pool.tensor_tensor(prod[n % 2][0:r, :], keys, qrep[0:r, g, :], ALU.mult).then_inc(prod_done, 1)
                pool.wait_ge(dch, DCH * it + 3)
                pool.partition_all_reduce(LM[:, :, :].rearrange("p g h -> p (g h)"), Lm[:, :, :].rearrange("p g h -> p (g h)"),
                                          P, RMAX).then_inc(ar_done, 1)

        def s_banks(s):
            return ps[:, 2 * (s % 2):2 * (s % 2) + 2, :].rearrange("p a b -> p (a b)")

        def att_pe(pe):
            def transpose_qk(it):
                for src, landed in ((qp, q_in), (kp, k_in)):
                    pe.wait_ge(landed, 16 * (it + 1))
                    for g in range(2):
                        n = 2 * (src is kp) + g
                        bank = QK_BANKS[n]
                        if bank < 4:
                            positive_wait(pe, s_biased, 16 * (it - 1) + 12)
                        elif bank == 5:
                            positive_wait(pe, pt_out, halves[16 * (it - 1) + 12] if it else 0)
                        else:
                            positive_wait(pe, osamp, it - 1)
                        for b in range(4):
                            last = nc.tensor.transpose(ps[:, bank, b * P:(b + 1) * P], src[:, 4 * g + b, :], ident[:, :])
                        last.then_inc(qk_ps, 1)

            def scores(s):
                it, k = divmod(s, 16)
                hh, qt = STEP[k]
                n = P * (qt + 1)
                if k == 0:
                    pe.wait_ge(qk_act, 2 * (it + 1))
                    pe.wait_ge(qk_dve, 2 * (it + 1))
                positive_wait(pe, s_biased, s - 1)
                out = s_banks(s)
                hp = slice(hh * HD, (hh + 1) * HD)
                for c0 in range(0, n, 512):
                    c1 = min(n, c0 + 512)
                    last = nc.tensor.matmul(out[:, c0:c1], QT[hp, qt * P:(qt + 1) * P], KTr[hp, c0:c1], start=True, stop=True)
                last.then_inc(s_ps, 1)

            def transpose_weights(s):
                qt = STEP[s % 16][1]
                pe.wait_ge(p_scaled, s + 1)
                for g in range(qt // 4 + 1):
                    positive_wait(pe, pt_out, halves[s])
                    for b in range(4 * g, min(qt + 1, 4 * g + 4)):
                        last = nc.tensor.transpose(ps[:, 4 + g, (b % 4) * P:(b % 4 + 1) * P], Pr[s % 2][:, b * P:(b + 1) * P], ident[:, :])
                    last.then_inc(pt_ps, 1)

            def weigh(s):
                it, k = divmod(s, 16)
                hh, qt = STEP[k]
                if k == 0:
                    pe.wait_ge(v_in, 16 * (it + 1))
                    pe.wait_ge(v_in2, 16 * (it + 1))
                positive_wait(pe, o_out, s)
                pe.wait_ge(pt_out, halves[s + 1])
                last = chain(ps[:, 6, 0:P], [(vp[:, b, :], PT[s % 2][:, b, :]) for b in range(qt + 1)])
                last.then_inc(pv_ps, 1)

            def sample(it):
                pe.wait_ge(dp_done, it + 1)
                flat = Lp[:, :, :].rearrange("p j h -> p (j h)")
                nc.tensor.matmul(ps[:, 7, 0:LOG * HEADS], ones[:, :], flat, start=True, stop=True).then_inc(dsum_ps, 1)
                for slot in range(SLOTS):
                    pe.wait_ge(ring_in[slot], 32 * (it + 1))
                for g, tiles in ((0, range(PAGES + 1)), (1, range(PAGES + 1, LOG))):
                    for c in range(4):
                        o0 = 256 + (4 * g + c) * HEADS
                        last = chain(ps[:, 7, o0:o0 + HEADS], [(value_tile(j, c), Lp[0:log_slot(j)[0], j, :]) for j in tiles])
                last.then_inc(dpv_ps, 1)

            transpose_qk(0)
            for s in range(3):
                scores(s)
            transpose_weights(0)
            for s in range(NSTEP):
                it, k = divmod(s, 16)
                new_pair = k == 13 and it < PAIRS - 1
                if new_pair:
                    transpose_qk(it + 1)
                elif s + 3 < NSTEP:
                    scores(s + 3)
                if s + 1 < NSTEP:
                    transpose_weights(s + 1)
                weigh(s)
                if new_pair:
                    scores(s + 3)
                if it and k == 0:
                    sample(it - 1)
            sample(PAIRS - 1)

        def att_act(act):
            def numerators(s):
                it, k = divmod(s, 16)
                hh, qt = STEP[k]
                n = P * (qt + 1)
                act.wait_ge(s_biased, s + 1)
                positive_wait(act, pt_ps, halves[max(s - 1, 0)])
                act.activation(Pr[s % 2][:, 0:n], S2[s % 2][:, 0:n], ACT.Exp, bias=mx[:, k:k + 1], scale=-1.0,
                               accum_out=lsum[it % 2][:, k:k + 1]).then_inc(p_done, 1)

            def scale_numerators(s):
                k = s % 16
                n = P * (STEP[k][1] + 1)
                act.wait_ge(rl_done, s + 1)
                act.activation(Pr[s % 2][:, 0:n], Pr[s % 2][:, 0:n], ACT.Copy, scale=rl[:, k:k + 1]).then_inc(p_scaled, 1)

            def copy_weights(s):
                qt = STEP[s % 16][1]
                for g in range(qt // 4 + 1):
                    act.wait_ge(pt_ps, halves[s] + g + 1)
                    positive_wait(act, pv_ps, s - 1)
                    n = min(4, qt + 1 - 4 * g)
                    act.activation(PT[s % 2][:, 4 * g:4 * g + n, :].rearrange("p b q -> p (b q)"), ps[:, 4 + g, 0:n * P],
                                   ACT.Copy).then_inc(pt_out, 1)

            def copy_out(s):
                it, k = divmod(s, 16)
                hh, qt = STEP[k]
                act.wait_ge(pv_ps, s + 1)
                if k == 0:
                    positive_wait(act, o_low, it - 1)
                rows = slice(hh * HD, (hh + 1) * HD)
                act.activation(O[it % 2][rows, qt * P:(qt + 1) * P], ps[rows, 6, 0:P], ACT.Copy).then_inc(o_out, 1)

            def copy_queries(it):
                for g in range(2):
                    act.wait_ge(qk_ps, 4 * it + g + 1)
                    act.activation(QT[:, 512 * g:512 * (g + 1)], ps[:, QK_BANKS[g], :], ACT.Copy).then_inc(qk_act, 1)

            copy_queries(0)
            numerators(0)
            numerators(1)
            scale_numerators(0)
            for s in range(NSTEP):
                it, k = divmod(s, 16)
                copy_weights(s)
                if s + 1 < NSTEP:
                    scale_numerators(s + 1)
                if s > 0:
                    copy_out(s - 1)
                if k == 13 and it < PAIRS - 1:
                    copy_queries(it + 1)
                if s + 2 < NSTEP:
                    numerators(s + 2)
                if k == 13:
                    act.wait_ge(dch, DCH * it + 5)
                    positive_wait(act, dpv_ps, it)
                    act.activation(Lp[:, :, :], Lb[:, :, :], ACT.Exp).then_inc(dp_done, 1)
            copy_out(NSTEP - 1)
            act.wait_ge(o_out, NSTEP)
            for it in range(SPLIT_LATE, PAIRS):
                act.activation(Xh[:, it, NS:T], O[it % 2][:, :], ACT.Copy).then_inc(o_high, 1)

        def att_dve(dve):
            def step(ins):
                ins.then_inc(dch, 1)

            def log_sum(it, j):
                n = LOG * it + j
                r = log_slot(j)[0]
                dve.wait_ge(prod_done, n + 1)
                dve.tensor_reduce(L[0:r, j, :], prod[n % 2][0:r, :].rearrange("p (h e) -> p h e", h=HEADS), AX,
                                  ALU.add).then_inc(log_done, 1)

            def copy_keys(it):
                for g in range(2):
                    dve.wait_ge(qk_ps, 4 * it + 2 + g + 1)
                    dve.tensor_copy(KTr[:, 512 * g:512 * (g + 1)], ps[:, QK_BANKS[2 + g], :]).then_inc(qk_dve, 1)

            def reciprocals(s):
                k = s % 16
                dve.wait_ge(p_done, s + 1)
                positive_wait(dve, p_scaled, s - 15)
                dve.reciprocal(rl[:, k:k + 1], lsum[s // 16 % 2][:, k:k + 1]).then_inc(rl_done, 1)

            def sample_max(it):
                n = DCH * it
                dve.wait_ge(log_done, LOG * (it + 1))
                positive_wait(dve, dp_done, it)
                step(dve.scalar_tensor_tensor(Lb[:, :, :], L[:, :, :], SCALE, dbias[:, it, :, :], ALU.mult, ALU.add))
                dve.wait_ge(dch, n + 1)
                step(dve.tensor_reduce(Lm[:, 0, :], Lb[:, 0:PAGES + 1, :].rearrange("p j h -> p h j"), AX, ALU.max))
                step(dve.tensor_reduce(Lm[:, 1, :], Lb[:, PAGES + 1:LOG, :].rearrange("p j h -> p h j"), AX, ALU.max))

            def sample_shift(it):
                dve.wait_ge(ar_done, it + 1)
                step(dve.tensor_tensor(Lb[:, 0:PAGES + 1, :], Lb[:, 0:PAGES + 1, :],
                                       LM[:, 0:1, :].to_broadcast([P, PAGES + 1, HEADS]), ALU.subtract))
                step(dve.tensor_tensor(Lb[:, PAGES + 1:LOG, :], Lb[:, PAGES + 1:LOG, :],
                                       LM[:, 1:2, :].to_broadcast([P, 4, HEADS]), ALU.subtract))

            def sample_out(it):
                n = DCH * it
                dve.wait_ge(dpv_ps, it + 1)
                sums = ps[:, 7, 0:LOG * HEADS].rearrange("p (j h) -> p h j", j=LOG)
                step(dve.tensor_reduce(dl[:, 0, :], sums[:, :, 0:PAGES + 1], AX, ALU.add))
                step(dve.tensor_reduce(dl[:, 1, :], sums[:, :, PAGES + 1:LOG], AX, ALU.add))
                dve.wait_ge(dch, n + 7)
                step(dve.reciprocal(drl[:, :, :], dl[:, :, :]))
                dve.wait_ge(dch, n + 8)
                mine = ps[:, 7, 256:256 + 8 * HEADS].rearrange("p (g c h) -> p g c h", g=2, c=4)
                step(dve.tensor_tensor(do1[:, :, :, :], mine, drl[:, :, :].unsqueeze(2).to_broadcast([P, 2, 4, HEADS]), ALU.mult))
                dve.wait_ge(dch, n + 9)
                step(dve.tensor_tensor(do2[:, :, :, :], do1[:, :, :, :], hsel[:, :, :].unsqueeze(1).to_broadcast([P, 2, 4, HEADS]), ALU.mult))
                dve.wait_ge(dch, n + 10)
                dve.tensor_reduce(oS[:, :, it], do2[:, :, :, :].rearrange("p g c h -> p (g c) h"), AX, ALU.add).then_inc(osamp, 1)

            copy_keys(0)
            dve.wait_ge(att_const_in, 16 * ATT_CONSTS)
            for s in range(NSTEP):
                it, k = divmod(s, 16)
                hh, qt = STEP[k]
                n = P * (qt + 1)
                if s > 0:
                    reciprocals(s - 1)
                if it // 4 == 0:
                    b = bias[hh]
                    if k % 8 == 0:
                        dve.wait_ge(bias_in[hh], 16 * (it + 1))
                    d = b[:, qt * P:(qt + 1) * P]
                    positive_wait(dve, s_biased, s)
                    dve.tensor_tensor(d, d, causal[:, :], ALU.add).then_inc(masked, 1)
                    dve.wait_ge(masked, s + 1)
                    row = b[:, 0:n]
                else:
                    if it == PAIRS // 2 and k == 0:
                        dve.wait_ge(dist_in, 16)
                    row = dist[:, SEQ - n:SEQ]
                dve.wait_ge(s_ps, s + 1)
                positive_wait(dve, p_done, s - 1)
                dve.tensor_tensor_reduce(S2[s % 2][:, 0:n], s_banks(s)[:, 0:n], row, -SCALE, -NEG, ALU.add, ALU.min,
                                         accum_out=mx[:, k:k + 1]).then_inc(s_biased, 1)
                if k == 15 and it < PAIRS - 1:
                    copy_keys(it + 1)
                for j in LOG_AT.get(k, ()):
                    log_sum(it, j)
                if it and k == 4:
                    sample_out(it - 1)
                if k == 12:
                    sample_max(it)
                if k == 13:
                    sample_shift(it)
            reciprocals(NSTEP - 1)
            sample_out(PAIRS - 1)
            for it in range(SPLIT_LATE, PAIRS):
                dve.wait_ge(o_high, it + 1)
                dve.tensor_tensor(Xl[:, it, NS:T], O[it % 2][:, :], Xh[:, it, NS:T].bitcast(F32), ALU.subtract).then_inc(o_low, 1)
            dve.wait_ge(osamp, PAIRS)
            dve.tensor_copy(Xh[:, :, 0:NS], oS[:, :, :]).then_inc(osamp, 1)
            dve.wait_ge(osamp, PAIRS + 1)
            dve.tensor_tensor(Xl[:, :, 0:NS], oS[:, :, :], Xh[:, :, 0:NS].bitcast(F32), ALU.subtract).then_inc(osamp, 1)
        ATT_DONE = (osamp, PAIRS + 2)

        def narrow_pe(pe, base, ps_done, ps_free, norm, input_done):
            for m in range(KT):
                n = base + m
                pe.wait_ge(split_done, n + 1)
                for b, (c0, w) in enumerate(BLOCKS):
                    j = NB * m + b
                    if m == 0:
                        input_done(b)
                    positive_wait(pe, ps_free, j - 5)
                    last = chain(ps[:, j % 6, 0:w], unit_products(n, c0, w))
                    last.then_inc(ps_done, 1)
                    if m == KT - 1 and b > 0:
                        norm_total(pe, norm, b - 1, NB * m + b)
                pe.wait_ge(ps_done, NB * (m + 1))
                pe.sem_inc(w_used, 1)
            norm_total(pe, norm, NB - 1, NB * KT)

        ORDER_NARROW = [(b, m) for m in range(KT) for b in range(NB)]

        def residual_dve(dve, ps_done, ps_free, norm, g):
            for j, (b, m) in enumerate(ORDER_NARROW):
                c0, w = BLOCKS[b]
                dve.wait_ge(ps_done, j + 1)
                x = xT[:, m, c0:c0 + w]
                dve.tensor_tensor(x, ps[:, j % 6, 0:w], x, ALU.add).then_inc(ps_free, 1)
            for b in range(NB):
                norm_apply_dve(dve, norm, g, b)

        def residual_act(act, ps_free, norm):
            for j, (b, m) in enumerate(ORDER_NARROW):
                act.wait_ge(ps_free, j + 1)
                norm_square(act, norm, j, b, m)
            for b in range(NB):
                norm_root(act, norm, b)
                norm_apply_act(act, norm, b)

        def residual_pool(pool, base, norm, ahead):
            for j, (b, m) in enumerate(ORDER_NARROW):
                norm_add(pool, norm, j, b, m == 0)
                if b == NB - 1 and m < KT - 1:
                    ahead(base + m + SPL)
            ahead(base + KT - 1 + SPL)
            for b in range(NB):
                norm_apply_pool(pool, norm, b)

        op_ps, op_free, oc_ps, oc_free = (sem(n) for n in ("op_ps", "op_free", "oc_ps", "oc_free"))

        def ffn_loop(eng, step):
            step(0, False)
            with eng.Fori(1, STEPS - 1) as i:
                step(i, False)
            step(STEPS - 1, True)

        def ffn_pe(pe, f, base, norm, after):
            def step(i, is_last):
                for q in range(GU):
                    t, b, half = q // (2 * NB), q // 2 % NB, q % 2
                    c0, w = BLOCKS[b]
                    n = 2 * t + half
                    if is_first(i) and t == 0 and half == 0:
                        norm_ready(pe, norm, b)
                    if b == 0:
                        pe.wait_ge(split_done, base + i * 6 + n + 1)
                    if q < 6:
                        f["dn_add"].wait(pe, i * DN - 5 + q)
                    else:
                        f[("silu", "hid")[half]].wait(pe, i * HB + (t - 1) * NB + b + 1)
                    last = chain(ps[:, q % 6, 0:w], unit_products(base + n, c0, w))
                    last.then_inc(f["gu_ps"].sem, 1)
                for b, (c0, w) in enumerate(BLOCKS):
                    f["low"].wait(pe, i * HB + NB + b + 1)
                    for m in range(KT):
                        q = b * KT + m
                        if q == 0:
                            pe.wait_ge(split_done, base + i * 6 + 6)
                        if q < 6:
                            f[("silu", "hid")[q % 2]].wait(pe, i * HB + NB + q // 2 + 1)
                        else:
                            f["dn_add"].wait(pe, i * DN + q - 5)
                        last = chain(ps[:, q % 6, 0:w],
                                     [pr for t in range(GF)
                                      for pr in split_products(Wh[(base + 4 + t) % SPL][:, m * P:(m + 1) * P],
                                                               Wl[(base + 4 + t) % SPL][:, m * P:(m + 1) * P],
                                                               Hh[:, t, c0:c0 + w], Hl[:, t, c0:c0 + w])])
                        last.then_inc(f["dn_ps"].sem, 1)
                        if after and is_last and b > 0 and m == 2:
                            norm_total(pe, after, b - 1, KT * b)
                if after and is_last:
                    norm_total(pe, after, NB - 1, NB * KT)
            ffn_loop(pe, step)

        def ffn_act(act, f, after):
            def step(i, is_last):
                for t in range(GF):
                    for b, (c0, w) in enumerate(BLOCKS):
                        f["gu_ps"].wait(act, i * GU + t * 2 * NB + 2 * b + 1)
                        f["hid"].wait(act, i * HB + (t - 1) * NB + b + 1)
                        act.activation(sg[:, b, 0:w], ps[:, 2 * b, 0:w], ACT.Silu).then_inc(f["silu"].sem, 1)
                    for b, (c0, w) in enumerate(BLOCKS):
                        f["dn_ps"].wait(act, i * DN)
                        f["hid"].wait(act, i * HB + t * NB + b + 1)
                        act.activation(Hh[:, t, c0:c0 + w], hf[:, b, 0:w], ACT.Copy).then_inc(f["high"].sem, 1)
                if after and is_last:
                    def square(b, m):
                        f["dn_add"].wait(act, i * DN + KT * b + m + 1)
                        norm_square(act, after, KT * b + m, b, m)
                    for b in range(2):
                        for m in range(KT):
                            square(b, m)
                            if b == 1 and m == 4:
                                norm_root(act, after, 0)
                    norm_apply_act(act, after, 0, lambda m: square(2, m))
                    for b in (1, 2):
                        norm_root(act, after, b)
                        norm_apply_act(act, after, b)
            ffn_loop(act, step)

        def ffn_dve(dve, f, after, g):
            def step(i, is_last):
                for t in range(GF):
                    for b, (c0, w) in enumerate(BLOCKS):
                        f["gu_ps"].wait(dve, i * GU + t * 2 * NB + 2 * b + 2)
                        f["silu"].wait(dve, i * HB + t * NB + b + 1)
                        dve.tensor_tensor(hf[:, b, 0:w], ps[:, 2 * b + 1, 0:w], sg[:, b, 0:w], ALU.mult).then_inc(f["hid"].sem, 1)
                        f["high"].wait(dve, i * HB + t * NB + b + 1)
                        dve.tensor_tensor(Hl[:, t, c0:c0 + w], hf[:, b, 0:w], Hh[:, t, c0:c0 + w].bitcast(F32),
                                          ALU.subtract).then_inc(f["low"].sem, 1)
                def add(b, m):
                    c0, w = BLOCKS[b]
                    q = b * KT + m
                    f["dn_ps"].wait(dve, i * DN + q + 1)
                    x = xT[:, m, c0:c0 + w]
                    dve.tensor_tensor(x, ps[:, q % 6, 0:w], x, ALU.add).then_inc(f["dn_add"].sem, 1)
                joined = after and is_last
                for b in range(2 if joined else NB):
                    for m in range(KT):
                        add(b, m)
                if joined:
                    norm_apply_dve(dve, after, g, 0, lambda m: add(2, m))
                    for b in (1, 2):
                        norm_apply_dve(dve, after, g, b)
            ffn_loop(dve, step)

        def ffn_pool(pool, f, base, after):
            def step(i, is_last):
                for n in range(6):
                    split_unit(pool, base + (i + 1) * 6 + n, base + n, lambda: ffn_released(pool, f, i, n))
            step(0, False)
            with pool.Fori(1, STEPS - 1) as i:
                step(i, False)
            if not after:
                return
            nxt = base + 6 * STEPS
            for n in range(2 * GF):
                split_ahead(pool, nxt + n)
            for b in range(NB):
                for m in range(KT):
                    norm_add(pool, after, KT * b + m, b, m == 0)
                    if b == 2 and m % 2 == 1:
                        norm_low(pool, after, 0, m)
            for n in range(2 * GF, 6):
                split_ahead(pool, nxt + n)
            for b in (1, 2):
                norm_apply_pool(pool, after, b)

        def split_ahead(pool, n):
            if n < UNITS:
                split_unit(pool, n, n, (lambda: wait_released(pool, n - SPL)) if n >= SPL else (lambda: None))

        names = ("g_in g_in2 g_in3 wt_ps wt_done rt_ps rt_done v_ps v_gelu v_sqsum v_stat v_norm mix_ps mix_done vst_ps vst_done "
                 "vs_ps vs_done u_ps u_gelu y_done yh yl cv_out")
        G = {n: sem(n) for n in names.split()}
        bvrep, bsrow, wsp = VM[:, 7, :], VM[0:1, 6, :], VM[:, 5, :]

        def gmlp_sp(sp):
            FFN[0]["dn_ps"].wait(sp, DN * STEPS)
            sp.dma_start(wsp.rearrange("p (g s) -> p g s", g=KT), a["w_spatial"][0].rearrange("g t s -> t g s")).then_inc(G["g_in"], 16)
            sp.dma_start(bvrep, a["b_v_c"][0, :].partition_broadcast(P)).then_inc(G["g_in2"], 16)
            sp.dma_start(bsrow, a["b_spatial"].rearrange("o g t -> o (g t)")).then_inc(G["g_in2"], 16)
            with nc.allow_non_contiguous_dma("one number a head group"):
                sp.dma_start(w00[:, :], a["w_spatial"][0, :, 0, 0].partition_broadcast(P)).then_inc(G["g_in3"], 16)
                sp.dma_start(b00[:, :], a["b_spatial"][0, :, 0].partition_broadcast(P)).then_inc(G["g_in3"], 16)

        def mixing_pe(pe):
            pe.wait_ge(G["g_in"], 16)
            for g in range(KT):
                last = nc.tensor.transpose(ps[:, 4 + g // 4, (g % 4) * P:(g % 4 + 1) * P], wsp[:, g * P:(g + 1) * P], ident[:, :])
                if g % 4 == 3:
                    last.then_inc(G["wt_ps"], 1)
            pe.wait_ge(G["wt_done"], 2)
            pe.wait_ge(G["g_in2"], 32)
            for g in range(KT):
                last = chain(ps[:, 4 + g // 4, (g % 4) * P:(g % 4 + 1) * P],
                             [(bvrep[:, g * P:(g + 1) * P], wT[:, g, :]), (ones[0:1, :], bsrow[:, g * P:(g + 1) * P])])
                if g % 4 == 3:
                    last.then_inc(G["rt_ps"], 1)
        def gmlp_pe(pe, norm):
            for c in range(2):
                for tt in range(TT):
                    q = c * TT + tt
                    if c == 0 and tt in (0, 4, 7):
                        norm_ready(pe, norm, (tt >= 4) + (tt >= 7))
                    if q == ZB:
                        mixing_pe(pe)
                    positive_wait(pe, G["v_gelu"], q - ZB + 1)
                    wide_products(pe, BASE_V + 4 * c, BASE_V + 4 * c, tt, q).then_inc(G["v_ps"], 1)
                pe.wait_ge(G["v_ps"], (c + 1) * TT)
                pe.sem_inc(w_used, 1)

            def u_unit(m):
                n = BASE_U + m
                pe.wait_ge(split_done, n + 1)
                for b, (c0, w) in enumerate(BLOCKS):
                    j = NB * m + b
                    if j < 6:
                        pe.wait_ge(G["v_gelu"], 2 * TT)
                        pe.wait_ge(G["rt_done"], 2)
                    positive_wait(pe, G["u_gelu"], j - 5)
                    last = chain(ps[:, j % 6, 0:w], unit_products(n, c0, w))
                    last.then_inc(G["u_ps"], 1)
                pe.wait_ge(G["u_ps"], NB * (m + 1))
                pe.sem_inc(w_used, 1)
            u_unit(0)
            u_unit(1)
            pe.wait_ge(G["v_norm"], TT)
            for g in range(KT):
                last = nc.tensor.transpose(ps[:, 6, g * NS:(g + 1) * NS], vs[:, g * P:(g + 1) * P], ident[0:NS, 0:NS])
            last.then_inc(G["vst_ps"], 1)
            pe.wait_ge(G["vst_done"], 1)
            for g in range(KT):
                last = nc.tensor.matmul(ps[0:NS, 6 + g // 4, (g % 4) * P:(g % 4 + 1) * P], vsT[:, g, :], ident[:, :], start=True, stop=True)
            last.then_inc(G["vs_ps"], 1)
            pe.wait_ge(G["vs_done"], 2)
            for tile in range(SEQ // P):
                for half in range(2):
                    j = 2 * tile + half
                    positive_wait(pe, G["mix_done"], (j - 1) * 4)
                    for g in range(4 * half, 4 * half + 4):
                        last = nc.tensor.matmul(ps[:, 6 + half, (g % 4) * P:(g % 4 + 1) * P], VM[:, tile, g * P:(g + 1) * P],
                                                wT[:, g, :], start=True, stop=True)
                    last.then_inc(G["mix_ps"], 1)
            for m in range(2, KT):
                u_unit(m)

        def gmlp_act(act, norm):
            for half in range(2):
                act.wait_ge(G["rt_ps"], half + 1)
                act.activation(RT[:, 4 * half:4 * half + 4, :].rearrange("p g t -> p (g t)"), ps[:, 4 + half, :], ACT.Copy).then_inc(G["rt_done"], 1)
            norm_ready(act, norm, NB - 1)
            act.wait_ge(G["rt_ps"], 2)
            act.wait_ge(G["v_stat"], 1)
            for c in range(2):
                for tt in range(TT):
                    q, r = c * TT + tt, token_rows(tt)
                    dst = vs[:, c * DH:(c + 1) * DH] if tt == 0 else VM[:, tt - 1, c * DH:(c + 1) * DH]
                    act.wait_ge(G["v_ps"], q + 1)
                    act.activation(dst, ps[0:r, q % ZB, :], ACT.Gelu, accum_out=vsum[0:r, tt, c:c + 1]).then_inc(G["v_gelu"], 1)
            act.wait_ge(G["v_stat"], 3)
            for tt in range(TT):
                r = token_rows(tt)
                src = vs[:, :] if tt == 0 else VM[:, tt - 1, :]
                for c in range(2):
                    positive_wait(act, G["v_sqsum"], 2 * tt + c)
                    act.activation(centred_squares[0:r, 0:DH], src[:, c * DH:(c + 1) * DH], ACT.Square, bias=vst[0:r, 1, tt:tt + 1],
                                   accum_out=vsum[0:r, tt, c:c + 1]).then_inc(G["v_sqsum"], 1)
            act.wait_ge(G["v_stat"], 4)
            act.activation(vst[:, 3, :], vst[:, 2, :], ACT.Sqrt, bias=eps[:, 0:1], scale=1.0 / D).then_inc(G["v_sqsum"], 1)
            for m in range(KT):
                for b, (c0, w) in enumerate(BLOCKS):
                    j = NB * m + b
                    act.wait_ge(G["u_ps"], j + 1)
                    positive_wait(act, G["y_done"], j - 1)
                    act.wait_ge(G["v_norm"], TT)
                    act.activation(ug[j % 2][:, 0:w], ps[:, j % 6, 0:w], ACT.Gelu).then_inc(G["u_gelu"], 1)
            act.wait_ge(G["u_ps"], NB * KT)
            for b, (c0, w) in enumerate(BLOCKS):
                for m in range(KT):
                    if b == 0:
                        act.wait_ge(G["y_done"], NB * m + 3)
                        act.activation(Xh[:, m, 0:NS], msT[:, m, :], ACT.Copy)
                    t0, t1 = (0, 3, 6, 8)[b:b + 2]
                    lo = NS + t0 * P
                    act.activation(Xh[:, m, lo:lo + (t1 - t0) * P].rearrange("p (t q) -> p t q", q=P),
                                   VM[:, t0:t1, m * P:(m + 1) * P], ACT.Copy).then_inc(G["yh"], 1)

        def gmlp_dve(dve, norm):
            for half in range(2):
                dve.wait_ge(G["wt_ps"], half + 1)
                dve.tensor_tensor(wT[:, 4 * half:4 * half + 4, :], ps[:, 4 + half, :].rearrange("p (g t) -> p g t", g=4),
                                  tri[:, :].unsqueeze(1).to_broadcast([P, 4, P]), ALU.mult).then_inc(G["wt_done"], 1)
            dve.memset(vsum[:, :, :], 0.0).then_inc(G["v_stat"], 1)
            dve.wait_ge(G["v_gelu"], 2 * TT)
            dve.tensor_tensor(vst[:, 0, :], vsum[:, :, 0], vsum[:, :, 1], ALU.add).then_inc(G["v_stat"], 1)
            dve.wait_ge(G["v_stat"], 2)
            dve.tensor_scalar(vst[:, 1, :], vst[:, 0, :], -1.0 / D, None, ALU.mult).then_inc(G["v_stat"], 1)
            dve.wait_ge(G["v_sqsum"], 2 * TT)
            dve.tensor_tensor(vst[:, 2, :], vsum[:, :, 0], vsum[:, :, 1], ALU.add).then_inc(G["v_stat"], 1)
            dve.wait_ge(G["v_sqsum"], 2 * TT + 1)
            dve.reciprocal(vst[:, 0, :], vst[:, 3, :]).then_inc(G["v_stat"], 1)
            dve.wait_ge(G["v_stat"], 5)
            for tt in range(TT):
                r = token_rows(tt)
                v = vs[:, :] if tt == 0 else VM[:, tt - 1, :]
                dve.tensor_scalar(v, v, vst[0:r, 1, tt:tt + 1], vst[0:r, 0, tt:tt + 1], ALU.add, ALU.mult).then_inc(G["v_norm"], 1)
            dve.wait_ge(G["vst_ps"], 1)
            dve.wait_ge(G["g_in3"], 32)
            n = [0]

            def step(ins):
                n[0] += 1
                ins.then_inc(vchain, 1)
                dve.wait_ge(vchain, n[0])
            step(dve.tensor_tensor(msT[:, :, :], ps[:, 6, 0:KT * NS].rearrange("p (g s) -> p g s", g=KT),
                                   gv[:, :].unsqueeze(2).to_broadcast([P, KT, NS]), ALU.mult))
            dve.tensor_tensor(vsT[:, :, :], msT[:, :, :], bv[:, :].unsqueeze(2).to_broadcast([P, KT, NS]), ALU.add).then_inc(G["vst_done"], 1)
            dve.wait_ge(G["vst_done"], 1)
            step(dve.tensor_tensor(msT[:, :, :], vsT[:, :, :], w00[:, :].unsqueeze(2).to_broadcast([P, KT, NS]), ALU.mult))
            step(dve.tensor_tensor(msT[:, :, :], msT[:, :, :], b00[:, :].unsqueeze(2).to_broadcast([P, KT, NS]), ALU.add))
            dve.wait_ge(G["vs_ps"], 1)
            for half in range(2):
                dve.tensor_copy(vs[:, half * DH:(half + 1) * DH], ps[0:NS, 6 + half, :]).then_inc(G["vs_done"], 1)
            for tile in range(SEQ // P):
                for half in range(2):
                    dve.wait_ge(G["mix_ps"], 2 * tile + half + 1)
                    for g in range(4 * half, 4 * half + 4):
                        dve.scalar_tensor_tensor(VM[:, tile, g * P:(g + 1) * P], ps[:, 6 + half, (g % 4) * P:(g % 4 + 1) * P],
                                                 gv[:, g:g + 1], RT[:, g, :], ALU.mult, ALU.add).then_inc(G["mix_done"], 1)
            dve.wait_ge(G["mix_done"], 8 * SEQ // P)
            for m in range(KT):
                for b, (c0, w) in enumerate(BLOCKS):
                    j = NB * m + b
                    t0, t1 = (0, 3, 6, 8)[b:b + 2]
                    dve.wait_ge(G["u_gelu"], j + 1)
                    off = NS if b == 0 else 0
                    if b == 0:
                        dve.tensor_tensor(msT[:, m, :], msT[:, m, :], ug[j % 2][:, 0:NS], ALU.mult)
                    y = VM[:, t0:t1, m * P:(m + 1) * P]
                    dve.tensor_tensor(y, y, ug[j % 2][:, off:w].rearrange("p (t q) -> p t q", q=P), ALU.mult).then_inc(G["y_done"], 1)
            for b, (c0, w) in enumerate(BLOCKS):
                for m in range(KT):
                    t0, t1 = (0, 3, 6, 8)[b:b + 2]
                    lo = NS + t0 * P
                    dve.wait_ge(G["yh"], KT * b + m + 1)
                    if b == 0:
                        dve.tensor_tensor(Xl[:, m, 0:NS], msT[:, m, :], Xh[:, m, 0:NS].bitcast(F32), ALU.subtract)
                    dve.tensor_tensor(Xl[:, m, lo:lo + (t1 - t0) * P].rearrange("p (t q) -> p t q", q=P),
                                      VM[:, t0:t1, m * P:(m + 1) * P],
                                      Xh[:, m, lo:lo + (t1 - t0) * P].bitcast(F32).rearrange("p (t q) -> p t q", q=P),
                                      ALU.subtract).then_inc(G["yl"], 1)

        vchain = sem("vchain")
        centred_squares = nc.alloc_sbuf_tensor_at("centred_squares", [P, DH], F32, offset=(nc.sbuf_usable_end - 4 * DH) // 32 * 32)

        used[0] = norm_end
        yt = [place(f"yt{j}", [P, D]) for j in range(2)]
        fin_lo, fin_hi, fin_act, fin_dve = (sem(n) for n in ("fin_lo", "fin_hi", "fin_act", "fin_dve"))
        y_out = sems("y_out", 2)

        CONSTS = 13
        block = ctx.enter_context(nc.Block())

        @block.sync
        def _(sp):
            for tt in range(NX):
                src = a["x_sample"] if tt == 0 else a["x_prompt"][(tt - 1) * P:tt * P, :]
                sp.dma_start(xs[tt][0:token_rows(tt), :], src).then_inc(x_in[tt], 16)
            with nc.allow_non_contiguous_dma("small constants, once"):
                for dst, src in ((ident[:, :], a["c_ident"]), (tri[:, :], a["c_uo"][:, 0:P]),
                                 (gains[:, 0, :], a["norm_mix"][0].rearrange("(m p) -> p m", p=P)),
                                 (gains[:, 1, :], a["norm_ffn"][0].rearrange("(m p) -> p m", p=P)),
                                 (gains[:, 2, :], a["norm_mix"][1].rearrange("(m p) -> p m", p=P)),
                                 (gains[:, 3, :], a["norm_ffn"][1].rearrange("(m p) -> p m", p=P)),
                                 (gv[:, :], a["g_v_c"][0].rearrange("(m p) -> p m", p=P)),
                                 (bv[:, :], a["b_v_c"][0].rearrange("(m p) -> p m", p=P)),
                                 (cs[:, :, :, :], a["c_rope"]),
                                 (gqk[:, 0, :], a["g_q_a"][0].partition_broadcast(P)),
                                 (gqk[:, 1, :], a["g_k_a"][0].partition_broadcast(P)),
                                 (gqk[:, 2, :], a["g_q_b"][0].partition_broadcast(P)),
                                 (gqk[:, 3, :], a["g_k_b"][0].partition_broadcast(P))):
                    sp.dma_start(dst, src).then_inc(const_in, 16)
                sp.dma_start(bf[:, :], a["b_forget"][0].partition_broadcast(P)).then_inc(bf_in, 16)
            load_unit(sp, BASE_FG, BASE_FG, rows(a["w_in_even"], 0, KT, 3 * DH, P), KT)
            for tt in range(NX, TT):
                sp.wait_ge(xt_lo, tt - NX + 1)
                sp.wait_ge(xt_hi, tt - NX + 1)
                sp.dma_start(xs[tt % NX][:, :], a["x_prompt"][(tt - 1) * P:tt * P, :]).then_inc(x_in[tt % NX], 16)

            def project(i):
                for c in range(3):
                    for j in range(IN_UNITS):
                        n = BASE_IN + 4 * c + j
                        src = a["w_in_even"][2 * j * P:(2 * j + 2) * P, bass.ds(i * (3 * DH + HEADS) + c * DH, DH)]
                        load_unit(sp, i * 12 + n, n, src.rearrange("(k p) n -> p k n", p=P), 2)
                        if is_first(i) and n in (5, 7, 9, 11):
                            pages_sp(sp, (n - 5) // 2)
            project(0)
            forget_store(sp)
            with sp.Fori(1, 2) as i:
                project(i)
            att_begin_sp(sp)
            att_sp(sp)
            sp.wait_ge(qk_ps, 4 * PAIRS)
            load_narrow(sp, BASE_OUT, a["w_out_even"][0], 8)
            load_ffn(sp, BASE_F0, 0)
            load_wide(sp, BASE_V, a["w_in_c"][0], D)
            gmlp_sp(sp)
            load_wide(sp, BASE_V + 4, a["w_in_c"][0], D + DH)
            load_narrow(sp, BASE_U, a["w_in_c"][0], 8)
            sp.wait_ge(G["vs_done"], 2)
            sp.dma_start(a["cv_sample"], vs[:, :]).then_inc(G["cv_out"], 16)
            load_narrow(sp, BASE_OC, a["w_out_c"][0], 8)
            load_ffn(sp, BASE_F1, 1)
            sp.wait_ge(lf_out, 32)
            sp.wait_ge(G["cv_out"], 16)
            sp.wait_ge(y_out[0], 16 * 5)
            sp.wait_ge(y_out[1], 16 * 4)

        @block.gpsimd
        def _(pool):
            pool.memset(zeros[:, :], 0.0).then_inc(zero_set, 1)
            pool.memset(ones[:, :], 1.0).then_inc(zero_set, 1)
            pool.wait_ge(zero_set, 2)

            for b in range(NB):
                for n in range((0, 3, 5, 6)[b], (0, 3, 5, 6)[b + 1]):
                    split_ahead(pool, n)
                norm_apply_pool(pool, NORMS[0], b)

            def project(i):
                for j in range(12):
                    n = BASE_IN + j
                    if not is_first(i) or n >= SPL:
                        split_unit(pool, i * 12 + n, n, lambda: positive_wait(pool, w_used, i * 12 + n - SPL + 1))
            peeled_loop(pool, 2, project)
            att_pool(pool)
            pool.wait_ge(log_done, LOG * PAIRS)
            split_ahead(pool, BASE_OUT)
            split_ahead(pool, BASE_OUT + 1)
            pool.wait_ge(s_ps, NSTEP)
            split_ahead(pool, BASE_OUT + 2)
            pool.wait_ge(*ATT_DONE)
            pool.wait_ge(dpv_ps, PAIRS)
            for n in range(BASE_OUT + 3, BASE_OUT + SPL):
                split_ahead(pool, n)
            residual_pool(pool, BASE_OUT, NORMS[1], lambda n: split_ahead(pool, n))
            ffn_pool(pool, FFN[0], BASE_F0, NORMS[2])
            for n in range(BASE_V + SPL, BASE_OC + SPL):
                split_ahead(pool, n)
            residual_pool(pool, BASE_OC, NORMS[3], lambda n: split_ahead(pool, n))
            ffn_pool(pool, FFN[1], BASE_F1, None)

        def input_ready(eng, b):
            n = (4, 7, 9)[b]
            eng.wait_ge(xt_act, n)
            eng.wait_ge(xt_dve, n)

        @block.tensor
        def _(pe):
            pe.wait_ge(const_in, 16 * CONSTS)
            pe.wait_ge(zero_set, 2)
            for b in range(NB):
                for tt in range((0, 4, 7)[b], (4, 7, 9)[b]):
                    r = token_rows(tt)
                    pe.wait_ge(x_in[tt % NX], 16 * (tt // NX + 1))
                    for half, (done, free) in enumerate(((xt_lo, xt_act), (xt_hi, xt_dve))):
                        positive_wait(pe, free, tt - 2)
                        for m in range(4):
                            last = nc.tensor.transpose(ps[:, 3 * half + tt % 3, m * P:m * P + r],
                                                       xs[tt % NX][0:r, (4 * half + m) * P:(4 * half + m + 1) * P], ident[0:r, 0:r])
                        last.then_inc(done, 1)
                n = BLOCKS[b][1]
                NORMS[0]["root"].wait(pe, b - 1)
                for m in range(KT):
                    t = KT * b + m
                    NORMS[0]["squared"].wait(pe, t + 1)
                    nc.tensor.matmul(ps[:, 6 + b % 2, 0:n], ones[:, :], sq[t % 2][:, 0:n], start=(m == 0),
                                     stop=(m == KT - 1)).then_inc(NORMS[0]["summed"].sem, 1)
            pe.wait_ge(xt_act, TT)
            pe.wait_ge(xt_dve, TT)
            in_pe(pe)
            forget_pe(pe)
            pe.wait_ge(lg, FORGET_DONE)
            att_pe(pe)
            pe.wait_ge(*ATT_DONE)
            pe.wait_ge(o_low, PAIRS)
            narrow_pe(pe, BASE_OUT, op_ps, op_free, NORMS[1], lambda b: None)
            ffn_pe(pe, FFN[0], BASE_F0, NORMS[1], NORMS[2])
            gmlp_pe(pe, NORMS[2])
            narrow_pe(pe, BASE_OC, oc_ps, oc_free, NORMS[3], lambda b: pe.wait_ge(G["yl"], KT * (b + 1)))
            ffn_pe(pe, FFN[1], BASE_F1, NORMS[3], None)
            FFN[1]["dn_add"].wait(pe, DN * STEPS)
            for tt in range(TT):
                t0 = token_columns(tt)
                for half, (done, free) in enumerate(((fin_lo, fin_act), (fin_hi, fin_dve))):
                    positive_wait(pe, free, tt - 2)
                    for m in range(4):
                        last = nc.tensor.transpose(ps[:, 3 * half + tt % 3, m * P:(m + 1) * P], xT[:, 4 * half + m, t0:t0 + P], ident[:, :])
                    last.then_inc(done, 1)

        def finish_half(eng, half):
            done, free = ((fin_lo, fin_act), (fin_hi, fin_dve))[half]
            for tt in range(TT):
                r = token_rows(tt)
                eng.wait_ge(done, tt + 1)
                positive_wait(eng, y_out[tt % 2], 16 * (tt // 2))
                dst, src = yt[tt % 2][0:r, half * 512:(half + 1) * 512], ps[0:r, 3 * half + tt % 3, :]
                if half == 0:
                    eng.activation(dst, src, ACT.Copy).then_inc(free, 1)
                    eng.wait_ge(fin_dve, tt + 1)
                    eng.wait_ge(fin_act, tt + 1)
                    out = a["y_sample"] if tt == 0 else a["y_prompt"][(tt - 1) * P:tt * P, :]
                    eng.dma_start(out, yt[tt % 2][0:r, :]).then_inc(y_out[tt % 2], 16)
                else:
                    eng.tensor_copy(dst, src).then_inc(free, 1)

        @block.scalar
        def _(act):
            def copy_input(tiles):
                for tt in tiles:
                    r, t0 = token_rows(tt), token_columns(tt)
                    act.wait_ge(xt_lo, tt + 1)
                    act.activation(xT[:, 0:4, t0:t0 + r], ps[:, tt % 3, :].rearrange("p (m t) -> p m t", m=4)[:, :, 0:r],
                                   ACT.Copy).then_inc(xt_act, 1)

            def squares(b):
                input_ready(act, b)
                for m in range(KT):
                    norm_square(act, NORMS[0], KT * b + m, b, m)
            copy_input(range(0, 4))
            squares(0)
            copy_input(range(4, 7))
            act.wait_ge(eps_set, 1)
            norm_root(act, NORMS[0], 0)
            squares(1)
            copy_input(range(7, TT))
            norm_apply_act(act, NORMS[0], 0)
            norm_root(act, NORMS[0], 1)
            squares(2)
            norm_apply_act(act, NORMS[0], 1)
            norm_root(act, NORMS[0], 2)
            norm_apply_act(act, NORMS[0], 2)
            in_act(act)
            act.wait_ge(lg, FORGET_DONE)
            att_act(act)
            residual_act(act, op_free, NORMS[1])
            ffn_act(act, FFN[0], NORMS[2])
            gmlp_act(act, NORMS[2])
            residual_act(act, oc_free, NORMS[3])
            ffn_act(act, FFN[1], None)
            finish_half(act, 0)

        @block.vector
        def _(dve):
            dve.memset(eps[:, :], EPS).then_inc(eps_set, 1)
            for tt in range(TT):
                r, t0 = token_rows(tt), token_columns(tt)
                dve.wait_ge(xt_hi, tt + 1)
                dve.tensor_copy(xT[:, 4:8, t0:t0 + r], ps[:, 3 + tt % 3, :].rearrange("p (m t) -> p m t", m=4)[:, :, 0:r]).then_inc(xt_dve, 1)
            dve.wait_ge(const_in, 16 * CONSTS)
            for b in range(NB):
                norm_apply_dve(dve, NORMS[0], 0, b)
            in_dve(dve)
            forget_dve(dve)
            att_dve(dve)
            residual_dve(dve, op_ps, op_free, NORMS[1], 1)
            ffn_dve(dve, FFN[0], NORMS[2], 2)
            gmlp_dve(dve, NORMS[2])
            residual_dve(dve, oc_ps, oc_free, NORMS[3], 3)
            ffn_dve(dve, FFN[1], None, 0)
            finish_half(dve, 1)


def shape_constants():
    import numpy as np
    f = np.float32
    r, c = np.arange(P)[:, None], np.arange(P)[None, :]
    tri = (r <= c).astype(f)
    dist = SEQ - P + np.arange(P)[:, None] - np.arange(SEQ)[None, :]
    times = sum(((dist >= 0) & (dist % dil == 0) & (dist <= P * dil)).astype(int) for dil in (1, 4, 16))
    dist_bias = np.where(times > 0, np.log(np.maximum(times, 1)) / SCALE, NEG).astype(f)
    causal = np.where(c <= r, 0.0, NEG).astype(f)
    inv = (f(500000.0) ** (-np.arange(0, 16, 2, dtype=f) / f(16))).astype(f)
    rope = np.zeros((P, 2, TT, 32), f)
    rope[:, 0, :, 0:16] = 1.0
    for tt in range(TT):
        pos = np.full(P, PAGES * P) if tt == 0 else (tt - 1) * P + np.arange(P)
        ang = (pos.astype(f)[:, None] * inv[None, :]).astype(f).astype(np.float64)
        rope[:, 1, tt, 0:8] = rope[:, 1, tt, 8:16] = np.cos(ang)
        rope[:, 1, tt, 16:24], rope[:, 1, tt, 24:32] = -np.sin(ang), np.sin(ang)
    db = np.zeros((P, NS, 5, HEADS), f)
    mine = np.arange(P)[:, None] == np.arange(NS)[None, :]
    db[:, :, 0, :] = np.where(mine, 0.0, NEG)[:, :, None]
    db[P // 2:, :, 3, :] = NEG
    db[:, :, 4, :] = np.where(mine, np.log(3.0), NEG)[:, :, None]
    hsel = np.zeros((P, 4, HEADS), f)
    for ch in range(4):
        for half in range(2):
            hsel[half * HD:(half + 1) * HD, ch, 2 * ch + half] = 1.0
    return {"c_ident": np.eye(P, dtype=f), "c_uo": np.concatenate([tri, np.ones((P, SEQ - P), f)], 1),
            "c_ustrict": (r > c).astype(f), "c_dist": dist_bias, "c_causal": causal, "c_rope": rope,
            "c_dbias": db, "c_hsel": hsel}


def kernel(**inputs):
    import numpy as np
    import concourse.bacc as bacc
    from concourse.bass_utils import run_bass_kernel_spmd

    nc = bacc.Bacc("TRN2", target_bir_lowering=False, num_devices=1)
    arrays = {n: np.asarray(v) for n, v in inputs.items()}
    arrays["x_prompt"] = arrays["x_prompt"].reshape(SEQ, D)
    arrays["x_sample"] = arrays["x_sample"].reshape(NS, D)
    arrays["w_in_even"] = arrays["w_in_even"].reshape(D, -1)
    arrays.update(shape_constants())
    arrays = {n: np.ascontiguousarray(v) for n, v in arrays.items()}
    a = {n: nc.dram_tensor(f"in_{n}", v.shape, mybir.dt.from_np(v.dtype), kind="ExternalInput").ap() for n, v in arrays.items()}
    outs = {"y_prompt": (SEQ, D), "y_sample": (NS, D), "k_prompt": (2, SEQ, DH), "v_prompt": (2, SEQ, DH),
            "logf_prompt": (SEQ, HEADS), "k_sample": (2, NS, DH), "v_sample": (2, NS, DH), "logf_sample": (NS, HEADS),
            "cv_sample": (NS, D)}
    for n, shape in outs.items():
        a[n] = nc.dram_tensor(f"out_{n}", shape, F32, kind="ExternalOutput").ap()
    build(nc, a)
    r = run_bass_kernel_spmd(nc, [{f"in_{n}": v for n, v in arrays.items()}], core_ids=[0]).results[0]
    o = {n: r[f"out_{n}"] for n in outs}
    kvp, kvs = (1, 1, SEQ, HEADS, HD), (1, NS, 1, HEADS, HD)
    return (o["y_prompt"].reshape(1, SEQ, D), o["y_sample"].reshape(NS, 1, D),
            o["k_prompt"][0].reshape(kvp), o["v_prompt"][0].reshape(kvp), o["logf_prompt"].reshape(1, 1, SEQ, HEADS),
            o["k_prompt"][1].reshape(kvp), o["v_prompt"][1].reshape(kvp),
            o["k_sample"][0].reshape(kvs), o["v_sample"][0].reshape(kvs), o["logf_sample"].reshape(1, NS, 1, HEADS),
            o["k_sample"][1].reshape(kvs), o["v_sample"][1].reshape(kvs), o["cv_sample"].reshape(1, NS, 1, D))
```
